# Optimizing a Trainium2 kernel written in Bass

```python
import math
import jax, jax.numpy as jnp
from jax import lax
import numpy as np
import jax
import jax.numpy as jnp

D_MODEL = 1024
BATCH = 1
SEQ = 512
DEPTH = 2

N_MIXERS = 2
EPS = 1e-6
POOL_WINDOWS = (2, 4, 8, 16)
N_POOL_GROUPS = len(POOL_WINDOWS)
POOL_GROUP_DIM = D_MODEL // N_POOL_GROUPS
HEAD_DIM = 64
N_HEADS = D_MODEL // HEAD_DIM
D_ATTN = N_HEADS * HEAD_DIM
ATTN_PATTERNS = ((128, 1), (512, 4), (2048, 16))
N_ATTN_GROUPS = len(ATTN_PATTERNS)
HEAD_GROUPS = tuple(N_HEADS // N_ATTN_GROUPS + (1 if g < N_HEADS % N_ATTN_GROUPS else 0) for g in range(N_ATTN_GROUPS))
ROPE_THETA = 10000.0
D_FF = -(-8 * D_MODEL // (3 * 256)) * 256
N_POOL_LAYERS = (DEPTH + 1) // 2
N_ATTN_LAYERS = DEPTH // 2
NEG_INF = -1e30


def rmsnorm(x, g):
    xf = x.astype(jnp.float32)
    y = xf * lax.rsqrt(jnp.mean(xf * xf, axis=-1, keepdims=True) + EPS)
    return (y * g.astype(jnp.float32)).astype(x.dtype)

def rope(t):
    S, hd = t.shape[1], t.shape[-1]
    inv_freq = 1.0 / (ROPE_THETA ** (jnp.arange(0, hd, 2, dtype=jnp.float32) / hd))
    ang = jnp.arange(S, dtype=jnp.float32)[:, None] * inv_freq[None, :]
    ang = jnp.concatenate([ang, ang], axis=-1)[None, :, None, :]
    tf = t.astype(jnp.float32)
    t1, t2 = tf[..., : hd // 2], tf[..., hd // 2 :]
    rot = jnp.concatenate([-t2, t1], axis=-1)
    return (tf * jnp.cos(ang) + rot * jnp.sin(ang)).astype(t.dtype)

def pool_mixer(h, w_in, w_group, scale, w_out):
    B, S, _ = h.shape
    u = jnp.einsum('bsd,de->bse', h, w_in).reshape(B, S, N_POOL_GROUPS, POOL_GROUP_DIM)
    cs = jnp.cumsum(u.astype(jnp.float32), axis=1)
    pos = jnp.arange(S)
    outs = []
    for g, w in enumerate(POOL_WINDOWS):
        c = cs[:, :, g]
        lag = jnp.pad(c, ((0, 0), (w, 0), (0, 0)))[:, :S]
        cnt = jnp.minimum(pos + 1, w).astype(jnp.float32)[None, :, None]
        outs.append((c - lag) / cnt - u[:, :, g].astype(jnp.float32))
    p = jnp.stack(outs, axis=2).astype(h.dtype)
    z = jnp.einsum('bsgc,gce->bsge', p, w_group).reshape(B, S, D_MODEL) * scale
    return jnp.einsum('bsd,de->bse', z, w_out)

def dilated_window_attention(q, k, v, window, dilation):
    B, S, H, hd = q.shape
    w = window // dilation
    L = S // dilation
    nb = -(-L // w)
    Lp = nb * w

    def to_blocks(t):
        t = t.reshape(B, L, dilation, H, hd)
        t = jnp.pad(t, ((0, 0), (0, Lp - L), (0, 0), (0, 0), (0, 0)))
        return t.reshape(B, nb, w, dilation, H, hd)

    qb, kb, vb = to_blocks(q), to_blocks(k), to_blocks(v)

    def with_prev(t):
        prev = jnp.concatenate([jnp.zeros_like(t[:, :1]), t[:, :-1]], axis=1)
        return jnp.concatenate([prev, t], axis=2)

    kc, vc = with_prev(kb), with_prev(vb)
    s = jnp.einsum('bnqrhd,bnkrhd->bnrhqk', qb, kc).astype(jnp.float32)
    qi = jnp.arange(w)[:, None]
    kj = jnp.arange(2 * w)[None, :]
    dist = w + qi - kj
    key_idx = jnp.arange(nb)[:, None, None] * w - w + kj[None]
    mask = (dist >= 0)[None] & (dist <= w)[None] & (key_idx >= 0)
    s = jnp.where(mask[None, :, None, None], s, NEG_INF)
    m = jnp.max(s, axis=-1, keepdims=True)
    e = jnp.exp(s - m)
    den = jnp.sum(e, axis=-1, keepdims=True)
    p = (e / den).astype(v.dtype)
    o = jnp.einsum('bnrhqk,bnkrhd->bnqrhd', p, vc)
    lse = (m + jnp.log(den))[..., 0]
    lse = jnp.transpose(lse, (0, 1, 4, 2, 3))
    o = o.reshape(B, Lp, dilation, H, hd)[:, :L].reshape(B, S, H, hd)
    lse = lse.reshape(B, Lp, dilation, H)[:, :L].reshape(B, S, H)
    return o, lse

def attn_mixer(h, w_qkv, w_out):
    B, S, _ = h.shape
    qkv = jnp.einsum('bsd,de->bse', h, w_qkv).reshape(B, S, 3, N_HEADS, HEAD_DIM)
    q = rope(qkv[:, :, 0]) * jnp.asarray(HEAD_DIM ** -0.5, dtype=h.dtype)
    k = rope(qkv[:, :, 1])
    v = qkv[:, :, 2]
    outs, lses = [], []
    start = 0
    for (window, dilation), n_g in zip(ATTN_PATTERNS, HEAD_GROUPS):
        sl = slice(start, start + n_g)
        o_g, lse_g = dilated_window_attention(q[:, :, sl], k[:, :, sl], v[:, :, sl], window, dilation)
        outs.append(o_g)
        lses.append(jax.nn.logsumexp(lse_g, axis=-1) - math.log(n_g))
        start += n_g
    alpha = jax.nn.softmax(jnp.stack(lses, axis=-1), axis=-1)
    merged = jnp.concatenate(
        [o_g * (N_ATTN_GROUPS * alpha[:, :, g]).astype(o_g.dtype)[:, :, None, None] for g, o_g in enumerate(outs)],
        axis=2,
    ).reshape(B, S, D_ATTN)
    return jnp.einsum('bse,ed->bsd', merged, w_out)

def swiglu(h, w_gate, w_up, w_down):
    g = jnp.einsum('bsd,df->bsf', h, w_gate)
    u = jnp.einsum('bsd,df->bsf', h, w_up)
    return jnp.einsum('bsf,fd->bsd', jax.nn.silu(g) * u, w_down)

def first_inputs(seed: int = 0) -> dict:
    key = jax.random.key(seed)
    ks = jax.random.split(key, 14)
    f32 = jnp.float32
    nrm = lambda k, shape, fan_in: jax.random.normal(k, shape, f32) * (fan_in ** -0.5)
    return {
        "x": jax.random.normal(ks[0], (BATCH, SEQ, D_MODEL), f32),
        "norm_mix": 1.0 + 0.05 * jax.random.normal(ks[1], (DEPTH, D_MODEL), f32),
        "norm_ffn": 1.0 + 0.05 * jax.random.normal(ks[2], (DEPTH, D_MODEL), f32),
        "norm_final": 1.0 + 0.05 * jax.random.normal(ks[3], (D_MODEL,), f32),
        "pool_w_in": nrm(ks[4], (N_POOL_LAYERS, D_MODEL, D_MODEL), D_MODEL),
        "pool_w_group": nrm(ks[5], (N_POOL_LAYERS, N_POOL_GROUPS, POOL_GROUP_DIM, POOL_GROUP_DIM), POOL_GROUP_DIM),
        "pool_scale": 1.0 + 0.1 * jax.random.normal(ks[6], (N_POOL_LAYERS, D_MODEL), f32),
        "pool_w_out": nrm(ks[7], (N_POOL_LAYERS, D_MODEL, D_MODEL), D_MODEL),
        "attn_w_qkv": nrm(ks[8], (N_ATTN_LAYERS, D_MODEL, 3 * D_ATTN), D_MODEL),
        "attn_w_out": nrm(ks[9], (N_ATTN_LAYERS, D_ATTN, D_MODEL), D_ATTN),
        "ffn_w_gate": nrm(ks[10], (DEPTH, D_MODEL, D_FF), D_MODEL),
        "ffn_w_up": nrm(ks[11], (DEPTH, D_MODEL, D_FF), D_MODEL),
        "ffn_w_down": nrm(ks[12], (DEPTH, D_FF, D_MODEL), D_FF),
    }

def first_block(x, norm_mix, norm_ffn, norm_final, pool_w_in, pool_w_group, pool_scale, pool_w_out,
              attn_w_qkv, attn_w_out, ffn_w_gate, ffn_w_up, ffn_w_down):
    for i in range(DEPTH):
        h = rmsnorm(x, norm_mix[i])
        j = i // N_MIXERS
        if i % N_MIXERS == 0:
            y = pool_mixer(h, pool_w_in[j], pool_w_group[j], pool_scale[j], pool_w_out[j])
        else:
            y = attn_mixer(h, attn_w_qkv[j], attn_w_out[j])
        x = x + y
        h = rmsnorm(x, norm_ffn[i])
        x = x + swiglu(h, ffn_w_gate[i], ffn_w_up[i], ffn_w_down[i])
    return rmsnorm(x, norm_final)


MEM_LEN = 256
N_BRANCHES = 4
MIX_WIDTH = D_MODEL // N_BRANCHES
MIX_HEADS = MIX_WIDTH // HEAD_DIM

NSA_CMP_LEN = 32
NSA_CMP_STRIDE = 16
NSA_SLC_LEN = 64
NSA_TOP_N = 8
NSA_WINDOW = 512
Q_BLOCK = 128
FORCE_BONUS = 1e4
N_BUCKETS = 32
MAX_DISTANCE = 128

RET_CHUNK = 128
ROPE_BASE = 10000.0
RET_NORM_EPS = 1e-5

RWKV_DECAY_LORA = 32
RWKV_AAA_LORA = 32
RWKV_GATE_LORA = 64
RWKV_GN_EPS = 64e-5
RWKV_SIZES = (MIX_WIDTH, MIX_WIDTH, MIX_WIDTH, RWKV_DECAY_LORA, RWKV_AAA_LORA, RWKV_GATE_LORA)
RWKV_COLS = sum(RWKV_SIZES)

CONV_WIDTH = 3

XA_HEADS = 4
XA_HEAD_DIM = D_MODEL // XA_HEADS
D_FF_2 = 4 * D_MODEL

IN_SIZES = (MIX_WIDTH, 6 * HEAD_DIM, 3 * MIX_HEADS, 4 * MIX_WIDTH, RWKV_COLS, 3 * MIX_WIDTH, N_BRANCHES * D_MODEL)
IN_COLS = sum(IN_SIZES)

RMS_EPS = 1e-6
NEG_INF_2 = -1e30


def split_cols(z, sizes):
    return jnp.split(z, np.cumsum(sizes)[:-1].tolist(), axis=-1)

def rms_norm(x, g):
    xf = x.astype(jnp.float32)
    y = xf * lax.rsqrt(jnp.mean(xf * xf, axis=-1, keepdims=True) + RMS_EPS)
    return (y * g.astype(jnp.float32)).astype(x.dtype)

def head_norm(u, eps):
    mu = jnp.mean(u, axis=-1, keepdims=True)
    var = jnp.mean(jnp.square(u - mu), axis=-1, keepdims=True)
    return (u - mu) * lax.rsqrt(var + eps)

def t5_bucket(dist):
    n = jnp.maximum(dist, 0)
    max_exact = N_BUCKETS // 2
    nf = jnp.maximum(n, 1).astype(jnp.float32)
    large = max_exact + (jnp.log(nf / max_exact) / math.log(MAX_DISTANCE / max_exact)
                         * (N_BUCKETS - max_exact)).astype(jnp.int32)
    large = jnp.minimum(large, N_BUCKETS - 1)
    return jnp.where(n < max_exact, n, large)

def masked_softmax(s, valid):
    return jax.nn.softmax(jnp.where(valid, s, NEG_INF_2), axis=-1)

def nsa_mixer(q, kv, gate_logits, cmp_w, cmp_pe, rel_bias):
    B, S, H, Dh = q.shape
    dt = q.dtype
    f32 = jnp.float32
    scale = Dh ** -0.5
    k_c, v_c, k_s, v_s, k_w, v_w = jnp.split(kv, 6, axis=-1)

    n_cmp = (S - NSA_CMP_LEN) // NSA_CMP_STRIDE + 1
    cmp_start = jnp.arange(n_cmp) * NSA_CMP_STRIDE
    cmp_idx = cmp_start[:, None] + jnp.arange(NSA_CMP_LEN)[None, :]
    k_cmp = jnp.einsum('bnld,lde->bne', k_c[:, cmp_idx] + cmp_pe, cmp_w[0])
    v_cmp = jnp.einsum('bnld,lde->bne', v_c[:, cmp_idx] + cmp_pe, cmp_w[1])
    cmp_end = cmp_start + NSA_CMP_LEN - 1

    n_slc = S // NSA_SLC_LEN
    top_n = min(NSA_TOP_N, n_slc)
    slc_start = jnp.arange(n_slc) * NSA_SLC_LEN
    overlap = jnp.clip(jnp.minimum(cmp_start[:, None] + NSA_CMP_LEN, slc_start[None, :] + NSA_SLC_LEN)
                       - jnp.maximum(cmp_start[:, None], slc_start[None, :]), 0).astype(f32) / NSA_CMP_LEN
    k_blk = k_s.reshape(B, n_slc, NSA_SLC_LEN, Dh)
    v_blk = v_s.reshape(B, n_slc, NSA_SLC_LEN, Dh)
    b_idx = jnp.arange(B)[:, None, None]

    k_wp = jnp.pad(k_w, ((0, 0), (NSA_WINDOW, 0), (0, 0)))
    v_wp = jnp.pad(v_w, ((0, 0), (NSA_WINDOW, 0), (0, 0)))

    gates = jax.nn.sigmoid(gate_logits.astype(f32)).reshape(B, S, H, 3)
    n_qb = S // Q_BLOCK
    q_b = q.reshape(B, n_qb, Q_BLOCK, H, Dh).swapaxes(0, 1)
    g_b = gates.reshape(B, n_qb, Q_BLOCK, H, 3).swapaxes(0, 1)
    bias_f = rel_bias.astype(f32)

    def block_fn(args):
        qb, gb, bi = args
        t = bi * Q_BLOCK + jnp.arange(Q_BLOCK)

        d_c = t[:, None] - cmp_end[None, :]
        s_c = (jnp.einsum('bqhd,bnd->bhqn', qb, k_cmp).astype(f32) * scale
               + bias_f[t5_bucket(d_c)].transpose(2, 0, 1))
        p_c = masked_softmax(s_c, d_c >= 0) * (t >= NSA_CMP_LEN - 1)[:, None].astype(f32)
        o_c = jnp.einsum('bhqn,bnd->bqhd', p_c.astype(dt), v_cmp)

        imp = jnp.einsum('bhqn,nm->bqm', p_c, overlap)
        blk = jnp.arange(n_slc)
        cur = t // NSA_SLC_LEN
        forced = (blk[None, :] == 0) | (blk[None, :] == cur[:, None]) | (blk[None, :] == cur[:, None] - 1)
        imp = jnp.where(forced, imp + FORCE_BONUS, imp)
        imp = jnp.where(blk[None, :] <= cur[:, None], imp, NEG_INF_2)
        _, sel = lax.top_k(imp, top_n)

        k_g = k_blk[b_idx, sel].reshape(B, Q_BLOCK, top_n * NSA_SLC_LEN, Dh)
        v_g = v_blk[b_idx, sel].reshape(B, Q_BLOCK, top_n * NSA_SLC_LEN, Dh)
        pos_s = (sel[..., None] * NSA_SLC_LEN + jnp.arange(NSA_SLC_LEN)).reshape(B, Q_BLOCK, -1)
        d_s = t[None, :, None] - pos_s
        s_s = (jnp.einsum('bqhd,bqkd->bhqk', qb, k_g).astype(f32) * scale
               + bias_f[t5_bucket(d_s)].transpose(0, 3, 1, 2))
        p_s = masked_softmax(s_s, (d_s >= 0)[:, None])
        o_s = jnp.einsum('bhqk,bqkd->bqhd', p_s.astype(dt), v_g)

        k_wb = lax.dynamic_slice_in_dim(k_wp, bi * Q_BLOCK, NSA_WINDOW + Q_BLOCK, axis=1)
        v_wb = lax.dynamic_slice_in_dim(v_wp, bi * Q_BLOCK, NSA_WINDOW + Q_BLOCK, axis=1)
        pos_w = bi * Q_BLOCK - NSA_WINDOW + jnp.arange(NSA_WINDOW + Q_BLOCK)
        d_w = t[:, None] - pos_w[None, :]
        valid_w = (d_w >= 0) & (d_w < NSA_WINDOW) & (pos_w[None, :] >= 0)
        s_w = (jnp.einsum('bqhd,bkd->bhqk', qb, k_wb).astype(f32) * scale
               + bias_f[t5_bucket(d_w)].transpose(2, 0, 1))
        p_w = masked_softmax(s_w, valid_w)
        o_w = jnp.einsum('bhqk,bkd->bqhd', p_w.astype(dt), v_wb)

        out = gb[..., 0:1] * o_c + gb[..., 1:2] * o_s + gb[..., 2:3] * o_w
        return out.astype(dt)

    out = lax.map(block_fn, (q_b, g_b, jnp.arange(n_qb)))
    return out.swapaxes(0, 1).reshape(B, S, H * Dh)

def rotary(u, pos):
    half = u.shape[-1] // 2
    inv_freq = ROPE_BASE ** (-jnp.arange(half, dtype=jnp.float32) / half)
    ang = pos.astype(jnp.float32)[:, None] * inv_freq[None, :]
    cos = jnp.cos(ang)[None, :, None, :]
    sin = jnp.sin(ang)[None, :, None, :]
    u1, u2 = u[..., :half], u[..., half:]
    return jnp.concatenate([u1 * cos - u2 * sin, u2 * cos + u1 * sin], axis=-1)

def retention_mixer(q, k, v, g, norm_g):
    B, S, C = q.shape
    H = C // HEAD_DIM
    f32 = jnp.float32
    pos = jnp.arange(S)
    qh = rotary(q.reshape(B, S, H, HEAD_DIM).astype(f32), pos) * HEAD_DIM ** -0.5
    kh = rotary(k.reshape(B, S, H, HEAD_DIM).astype(f32), pos)
    vh = v.reshape(B, S, H, HEAD_DIM).astype(f32)
    L = min(RET_CHUNK, S)
    nc = S // L
    lg = jnp.log(1.0 - 2.0 ** (-5.0 - jnp.arange(H, dtype=f32)))
    n = jnp.arange(L, dtype=f32)
    diff = n[:, None] - n[None, :]
    inner_decay = jnp.where(diff >= 0, jnp.exp(jnp.maximum(diff, 0.0)[None] * lg[:, None, None]), 0.0)
    q_decay = jnp.exp((n + 1.0)[None, :] * lg[:, None])
    k_decay = jnp.exp((L - 1.0 - n)[None, :] * lg[:, None])
    chunk_decay = jnp.exp(L * lg)

    def to_chunks(u):
        return u.reshape(B, nc, L, H, HEAD_DIM).transpose(1, 0, 3, 2, 4)

    def step(state, inp):
        qc, kc, vc = inp
        att = jnp.einsum('bhld,bhmd->bhlm', qc, kc) * inner_decay
        o = (jnp.einsum('bhlm,bhmd->bhld', att, vc)
             + jnp.einsum('bhld,bhde->bhle', qc, state) * q_decay[None, :, :, None])
        state = (state * chunk_decay[None, :, None, None]
                 + jnp.einsum('bhmd,bhme->bhde', kc * k_decay[None, :, :, None], vc))
        return state, o

    state0 = jnp.zeros((B, H, HEAD_DIM, HEAD_DIM), f32)
    _, o = lax.scan(step, state0, (to_chunks(qh), to_chunks(kh), to_chunks(vh)))
    o = o.transpose(1, 0, 3, 2, 4).reshape(B, S, H, HEAD_DIM)
    o = head_norm(o, RET_NORM_EPS) * norm_g.astype(f32).reshape(H, HEAD_DIM)
    return (jax.nn.silu(g.astype(f32)) * o.reshape(B, S, C)).astype(q.dtype)

def rwkv7_mixer(z, mu, w0, w2, a0, a2, g2, k_k, k_a, r_k, ln_g, ln_b):
    B, S, _ = z.shape
    C = MIX_WIDTH
    H = C // HEAD_DIM
    N = HEAD_DIM
    dt = z.dtype
    f32 = jnp.float32
    zf = z.astype(f32)
    zf = zf + (jnp.pad(zf, ((0, 0), (1, 0), (0, 0)))[:, :-1] - zf) * mu
    r, k, v, wl, al, gl = split_cols(zf, RWKV_SIZES)
    w_log = -jax.nn.softplus(-(w0 + jnp.tanh(wl) @ w2)) - 0.5
    decay = jnp.exp(-jnp.exp(w_log))
    a = jax.nn.sigmoid(a0 + al @ a2)
    g = jax.nn.sigmoid(gl) @ g2
    kk = (k * k_k).reshape(B, S, H, N)
    kk = kk / jnp.maximum(jnp.sqrt(jnp.sum(kk * kk, axis=-1, keepdims=True)), 1e-12)
    k = k * (1.0 + (a - 1.0) * k_a)

    def heads(u):
        return u.reshape(B, S, H, N)

    rh, wh, kh, vh, ah = heads(r), heads(decay), heads(k), heads(v), heads(a)

    def seq_first(u):
        return u.transpose(1, 0, 2, 3)

    def step(state, inp):
        r_t, w_t, k_t, v_t, kk_t, a_t = inp
        sa = jnp.einsum('bhvk,bhk->bhv', state, -kk_t)
        state = (state * w_t[:, :, None, :]
                 + sa[..., None] * (kk_t * a_t)[:, :, None, :]
                 + v_t[..., None] * k_t[:, :, None, :])
        return state, jnp.einsum('bhvk,bhk->bhv', state, r_t)

    state0 = jnp.zeros((B, H, N, N), f32)
    xs = (seq_first(rh), seq_first(wh), seq_first(kh), seq_first(vh), seq_first(kk), seq_first(ah))
    _, y = lax.scan(step, state0, xs)
    y = y.transpose(1, 0, 2, 3)
    y = head_norm(y, RWKV_GN_EPS) * ln_g.astype(f32).reshape(H, N) + ln_b.astype(f32).reshape(H, N)
    y = y + jnp.sum(rh * kh * r_k.astype(f32).reshape(H, N), axis=-1, keepdims=True) * vh
    return (y.reshape(B, S, C) * g).astype(dt)

def short_conv_mixer(z, conv_w):
    b_g, c_g, xt = jnp.split(z, 3, axis=-1)
    u = c_g * xt
    C = u.shape[-1]
    y = lax.conv_general_dilated(u, conv_w[:, None, :].astype(u.dtype), window_strides=(1,),
                                 padding=[(CONV_WIDTH - 1, 0)],
                                 dimension_numbers=('NWC', 'WIO', 'NWC'),
                                 feature_group_count=C)
    return b_g * y

def cross_attention(h, m, wq, wkv, wo):
    B, S, D = h.shape
    M = m.shape[1]
    q = (h @ wq).reshape(B, S, XA_HEADS, XA_HEAD_DIM)
    k, v = jnp.split(m @ wkv, 2, axis=-1)
    k = k.reshape(B, M, XA_HEADS, XA_HEAD_DIM)
    v = v.reshape(B, M, XA_HEADS, XA_HEAD_DIM)
    s = jnp.einsum('bshd,bmhd->bhsm', q, k).astype(jnp.float32) * XA_HEAD_DIM ** -0.5
    p = jax.nn.softmax(s, axis=-1).astype(h.dtype)
    o = jnp.einsum('bhsm,bmhd->bshd', p, v).reshape(B, S, D)
    return o @ wo

def second_inputs(seed: int = 0) -> dict:
    key = jax.random.key(seed)
    ks = iter(jax.random.split(key, 48))
    f32 = jnp.float32

    def nrm(shape, scale):
        return scale * jax.random.normal(next(ks), shape, f32)

    def gain(shape):
        return 1.0 + 0.02 * jax.random.normal(next(ks), shape, f32)

    def unif(shape, lo, hi):
        return jax.random.uniform(next(ks), shape, f32, lo, hi)

    return {
        'x': nrm((BATCH, SEQ, D_MODEL), 1.0),
        'mem': nrm((BATCH, MEM_LEN, D_MODEL), 1.0),
        'ln_mix_pre': gain((DEPTH, D_MODEL)),
        'w_in': nrm((DEPTH, D_MODEL, IN_COLS), D_MODEL ** -0.5),
        'nsa_cmp_w': nrm((DEPTH, 2, NSA_CMP_LEN, HEAD_DIM, HEAD_DIM), (NSA_CMP_LEN * HEAD_DIM) ** -0.5),
        'nsa_cmp_pe': nrm((DEPTH, NSA_CMP_LEN, HEAD_DIM), 0.02),
        'rel_bias': nrm((N_BUCKETS, MIX_HEADS), 0.5),
        'ret_norm_g': gain((DEPTH, MIX_WIDTH)),
        'rwkv_mu': unif((DEPTH, RWKV_COLS), 0.0, 1.0),
        'rwkv_w0': unif((DEPTH, MIX_WIDTH), -6.0, 1.0),
        'rwkv_w2': nrm((DEPTH, RWKV_DECAY_LORA, MIX_WIDTH), 0.1),
        'rwkv_a0': nrm((DEPTH, MIX_WIDTH), 0.1),
        'rwkv_a2': nrm((DEPTH, RWKV_AAA_LORA, MIX_WIDTH), 0.1),
        'rwkv_g2': nrm((DEPTH, RWKV_GATE_LORA, MIX_WIDTH), RWKV_GATE_LORA ** -0.5),
        'rwkv_k_k': 0.85 + 0.02 * jax.random.normal(next(ks), (DEPTH, MIX_WIDTH), f32),
        'rwkv_k_a': gain((DEPTH, MIX_WIDTH)),
        'rwkv_r_k': nrm((DEPTH, MIX_WIDTH), 0.1),
        'rwkv_ln_g': gain((DEPTH, MIX_WIDTH)),
        'rwkv_ln_b': nrm((DEPTH, MIX_WIDTH), 0.02),
        'conv_w': nrm((DEPTH, CONV_WIDTH, MIX_WIDTH), CONV_WIDTH ** -0.5),
        'w_branch': nrm((DEPTH, N_BRANCHES, MIX_WIDTH, D_MODEL), MIX_WIDTH ** -0.5),
        'w_mix_out': nrm((DEPTH, D_MODEL, D_MODEL), D_MODEL ** -0.5),
        'ln_mix_post': gain((DEPTH, D_MODEL)),
        'ln_xa_pre': gain((DEPTH, D_MODEL)),
        'ln_mem': gain((DEPTH, D_MODEL)),
        'xa_wq': nrm((DEPTH, D_MODEL, D_MODEL), D_MODEL ** -0.5),
        'xa_wkv': nrm((DEPTH, D_MODEL, 2 * D_MODEL), D_MODEL ** -0.5),
        'xa_wo': nrm((DEPTH, D_MODEL, D_MODEL), D_MODEL ** -0.5),
        'ln_xa_post': gain((DEPTH, D_MODEL)),
        'ln_mlp_pre': gain((DEPTH, D_MODEL)),
        'mlp_w1': nrm((DEPTH, D_MODEL, D_FF_2), D_MODEL ** -0.5),
        'mlp_w2': nrm((DEPTH, D_FF_2, D_MODEL), D_FF_2 ** -0.5),
        'ln_mlp_post': gain((DEPTH, D_MODEL)),
    }

def second_block(x, mem, ln_mix_pre, w_in, nsa_cmp_w, nsa_cmp_pe, rel_bias, ret_norm_g,
              rwkv_mu, rwkv_w0, rwkv_w2, rwkv_a0, rwkv_a2, rwkv_g2, rwkv_k_k, rwkv_k_a, rwkv_r_k,
              rwkv_ln_g, rwkv_ln_b, conv_w, w_branch, w_mix_out, ln_mix_post,
              ln_xa_pre, ln_mem, xa_wq, xa_wkv, xa_wo, ln_xa_post,
              ln_mlp_pre, mlp_w1, mlp_w2, ln_mlp_post):
    B, S, _ = x.shape
    for l in range(DEPTH):
        h = rms_norm(x, ln_mix_pre[l])
        z = h @ w_in[l]
        z_q, z_kv, z_g, z_ret, z_rwkv, z_conv, z_gate = split_cols(z, IN_SIZES)
        o_nsa = nsa_mixer(z_q.reshape(B, S, MIX_HEADS, HEAD_DIM), z_kv, z_g,
                          nsa_cmp_w[l], nsa_cmp_pe[l], rel_bias)
        r_q, r_k, r_v, r_g = jnp.split(z_ret, 4, axis=-1)
        o_ret = retention_mixer(r_q, r_k, r_v, r_g, ret_norm_g[l])
        o_rwkv = rwkv7_mixer(z_rwkv, rwkv_mu[l], rwkv_w0[l], rwkv_w2[l], rwkv_a0[l], rwkv_a2[l],
                             rwkv_g2[l], rwkv_k_k[l], rwkv_k_a[l], rwkv_r_k[l],
                             rwkv_ln_g[l], rwkv_ln_b[l])
        o_conv = short_conv_mixer(z_conv, conv_w[l])
        gates = jax.nn.sigmoid(z_gate).reshape(B, S, N_BRANCHES, D_MODEL)
        branches = (o_nsa, o_ret, o_rwkv, o_conv)
        merged = gates[:, :, 0] * (branches[0] @ w_branch[l, 0])
        for m in range(1, N_BRANCHES):
            merged = merged + gates[:, :, m] * (branches[m] @ w_branch[l, m])
        x = x + rms_norm(merged @ w_mix_out[l], ln_mix_post[l])

        h = rms_norm(x, ln_xa_pre[l])
        mn = rms_norm(mem, ln_mem[l])
        x = x + rms_norm(cross_attention(h, mn, xa_wq[l], xa_wkv[l], xa_wo[l]), ln_xa_post[l])

        h = rms_norm(x, ln_mlp_pre[l])
        x = x + rms_norm(jnp.square(jax.nn.relu(h @ mlp_w1[l])) @ mlp_w2[l], ln_mlp_post[l])
    return x


def setup_inputs(seed=0):
    out = dict(first_inputs(seed))
    for name, value in second_inputs(seed + 1).items():
        if name != "x":
            out[name + "_2"] = value
    return out


def reference(
    x, norm_mix, norm_ffn, norm_final, pool_w_in, pool_w_group, pool_scale, pool_w_out,
    attn_w_qkv, attn_w_out, ffn_w_gate, ffn_w_up, ffn_w_down, mem_2, ln_mix_pre_2, w_in_2,
    nsa_cmp_w_2, nsa_cmp_pe_2, rel_bias_2, ret_norm_g_2, rwkv_mu_2, rwkv_w0_2, rwkv_w2_2,
    rwkv_a0_2, rwkv_a2_2, rwkv_g2_2, rwkv_k_k_2, rwkv_k_a_2, rwkv_r_k_2, rwkv_ln_g_2,
    rwkv_ln_b_2, conv_w_2, w_branch_2, w_mix_out_2, ln_mix_post_2, ln_xa_pre_2, ln_mem_2,
    xa_wq_2, xa_wkv_2, xa_wo_2, ln_xa_post_2, ln_mlp_pre_2, mlp_w1_2, mlp_w2_2, ln_mlp_post_2,
):
    x = first_block(
        x, norm_mix, norm_ffn, norm_final, pool_w_in, pool_w_group, pool_scale, pool_w_out,
        attn_w_qkv, attn_w_out, ffn_w_gate, ffn_w_up, ffn_w_down,
    )
    return second_block(
        x, mem_2, ln_mix_pre_2, w_in_2, nsa_cmp_w_2, nsa_cmp_pe_2, rel_bias_2, ret_norm_g_2,
        rwkv_mu_2, rwkv_w0_2, rwkv_w2_2, rwkv_a0_2, rwkv_a2_2, rwkv_g2_2, rwkv_k_k_2,
        rwkv_k_a_2, rwkv_r_k_2, rwkv_ln_g_2, rwkv_ln_b_2, conv_w_2, w_branch_2, w_mix_out_2,
        ln_mix_post_2, ln_xa_pre_2, ln_mem_2, xa_wq_2, xa_wkv_2, xa_wo_2, ln_xa_post_2,
        ln_mlp_pre_2, mlp_w1_2, mlp_w2_2, ln_mlp_post_2,
    )


_drawn_inputs = setup_inputs


def setup_inputs(seed=0):
    import zlib

    import numpy as np

    out = dict(_drawn_inputs(seed))
    spreads = {}
    factors = {'nsa_cmp_pe_2': 6.855,
     'ret_norm_g_2': 6.658,
     'rwkv_w2_2': 3.963,
     'rwkv_a0_2': 3.202,
     'rwkv_k_k_2': 5.243,
     'rwkv_k_a_2': 4.922,
     'rwkv_ln_g_2': 6.72,
     'rwkv_ln_b_2': 6.834,
     'ln_mix_post_2': 2.814,
     'ln_xa_pre_2': 3.468,
     'ln_xa_post_2': 3.169,
     'ln_mlp_pre_2': 3.308,
     'ln_mlp_post_2': 3.701}
    for name, (base, spread) in spreads.items():
        noise = np.random.default_rng([zlib.crc32(name.encode()), seed]).standard_normal(out[name].shape)
        drawn = base * np.exp(spread * noise) if base else spread * noise
        out[name] = jnp.asarray(drawn.astype(out[name].dtype))
    for name, factor in factors.items():
        out[name] = (out[name] * factor).astype(out[name].dtype)
    return out
```

```python
from contextlib import ExitStack, contextmanager

import numpy as np

import concourse.bass as bass
from concourse import mybir

F32 = mybir.dt.float32
F32R = mybir.dt.float32r
ALU = mybir.AluOpType
ACT = mybir.ActivationFunctionType
AX = mybir.AxisListType.X

P = 128
S = 512
D = 1024
DT = D // P
TT = S // P
HD = 64
EPS = 1e-6
NEG = -1e30
D_FF = 2816
FFN_HALVES = (12, 10)
POOL_WINDOWS = (2, 4, 8, 16)
PAD = 16
LAYERS = 2
MEM = 256
NSA_LEN, NSA_STRIDE, N_CMP = 32, 16, 31
IN_NSA, IN_RET = 0, 652
IN_GATE = 3340
DECAY = float(np.exp(-0.5))

CONST_COLS = {}


def _layout():
    at = 0
    for name, n in (("ident", P), ("ones", P), ("heads", P), ("flip", P), ("rot", P), ("cos", S), ("sin", S),
                    ("decay", 4 * S), ("level", 6 * P), ("strict", P), ("incl", P), ("chunk", HD), ("invcnt", 64), ("late", 1)):
        CONST_COLS[name] = (at, at + n)
        at += n
    return -(-at // 8) * 8


N_CONST = _layout()


def constant_table():
    t = np.zeros((P, N_CONST), np.float32)

    def put(name, a):
        lo, hi = CONST_COLS[name]
        t[:, lo:hi] = np.asarray(a, np.float32).reshape(P, hi - lo)

    p = np.arange(P)
    put("ident", np.eye(P))
    put("ones", np.ones((P, P)))
    put("heads", (p[:, None] // HD == p[None, :] // HD))
    put("flip", np.eye(P)[::-1])
    rot = np.zeros((P, P))
    for m in range(P):
        base, d = m // HD * HD, m % HD
        if d < HD // 2:
            rot[base + d + HD // 2, m] = -1.0
        else:
            rot[base + d - HD // 2, m] = 1.0
    put("rot", rot)
    inv = (np.float32(1.0) / (np.float32(10000.0) ** (np.arange(0, HD, 2, dtype=np.float32) / np.float32(HD)))).astype(np.float32)
    ang = (np.arange(S, dtype=np.float32)[None, :] * inv[p % (HD // 2)][:, None]).astype(np.float32)
    put("cos", np.cos(ang.astype(np.float64)))
    put("sin", np.sin(ang.astype(np.float64)))
    dist = np.arange(S)[None, :] - p[:, None]
    put("decay", np.concatenate([np.where(dist >= 0, (1.0 - 2.0 ** (-5.0 - h)) ** np.maximum(dist, 0), 0.0)
                                 for h in range(4)], 1))
    same = p[:, None] // HD == p[None, :] // HD
    strict = same & (p[:, None] < p[None, :])
    levels = []
    for b in (1, 2, 4, 8, 16, 32):
        levels.append((p[:, None] // (2 * b) == p[None, :] // (2 * b)) & (p[:, None] // b % 2 == 0) & (p[None, :] // b % 2 == 1))
    put("level", np.concatenate(levels, 1))
    put("strict", strict)
    put("incl", strict | np.eye(P, dtype=bool))
    put("chunk", np.tile((np.arange(HD) != 0)[None, :], (P, 1)))
    put("late", p >= 31)
    put("invcnt", np.tile(np.concatenate([1.0 / np.minimum(np.arange(16) + 1, w) for w in POOL_WINDOWS])[None], (P, 1)))
    return t


def pattern_masks():
    q = np.arange(P)[:, None]
    local = P + q - np.arange(2 * P)[None, :]
    far = q + 3 * P - np.arange(S)[None, :]
    allowed = [(local >= 0) & (local <= P), (far >= 0) & (far % 4 == 0), (far >= 0) & (far % 16 == 0)]
    return np.concatenate([np.where(a, 0.0, NEG) for a in allowed], 1).astype(np.float32)


N_DIST = 1152


def bucket_of_distance():
    d = 511 - np.arange(N_DIST)
    n = np.maximum(d, 0)
    nf = np.maximum(n, 1).astype(np.float32)
    large = 16 + (np.log(nf / np.float32(16)) / np.float32(np.log(128 / 16)) * np.float32(16)).astype(np.int32)
    bucket = np.where(n < 16, n, np.minimum(large, 31))
    t = np.zeros((33, N_DIST), np.float32)
    t[bucket[d >= 0], np.arange(N_DIST)[d >= 0]] = 1.0
    t[32, d < 0] = 1.0
    return t


BASE = 1152
SBUF_END = 229344


def build(nc, A, out, scratch, rises):
    order, credits, taken, terms = [], {}, {}, {}

    def signal(name, credit=0, credited=None):
        sem = nc.alloc_semaphore(name)
        order.append(sem)
        credits[name] = (credit, credited)
        names[id(sem)] = name
        return sem

    names = {}

    def start(sem, who, value=None):
        key = (names[id(sem)], who)
        if key not in taken:
            credit, credited = credits[key[0]]
            taken[key] = value if value is not None else 0 if who == credited else credit
            terms[key] = []
        return key

    def skip(sem, who, n):
        taken[start(sem, who)] += n

    def take(sem, who, n=1):
        key = start(sem, who)
        taken[key] += n
        value = taken[key]
        for register, per in terms[key]:
            if per:
                value = register * per + value
        return sem, value

    def ahead(sem, who, n):
        value = take(sem, who, n)
        skip(sem, who, -n)
        return value

    def settle(eng):
        eng.sem_inc(settled, 1)

    nloops = {}

    @contextmanager
    def loop(eng, who, n):
        which = (who, nloops.get(who, 0))
        nloops[who] = which[1] + 1
        per = rises.get(which, {})
        keys = [start(s, who) for s in order]
        before = [taken[key] for key in keys]
        settle(eng)
        with eng.Fori(0, n) as i:
            for a, key in enumerate(keys):
                terms[key].append((i, per.get(a, 0)))
            yield i
            settle(eng)
            for key in keys:
                terms[key].pop()
        took = {a: taken[key] - before[a] for a, key in enumerate(keys) if taken[key] != before[a]}
        rises[which] = took
        for a, key in enumerate(keys):
            taken[key] = before[a] + n * took.get(a, 0)

    free_from = [BASE]

    def sbuf_at(name, offset, shape, dtype=F32):
        assert offset + 4 * int(np.prod(shape)) <= SBUF_END, name
        return nc.alloc_sbuf_tensor_at(name, [P, *shape], dtype, offset=offset)

    def sbuf_next(name, shape, dtype=F32):
        offset = free_from[0]
        free_from[0] += 4 * int(np.prod(shape))
        return sbuf_at(name, offset, shape, dtype)

    x = sbuf_next("x", [DT, S])
    h_hi = sbuf_next("h_hi", [DT, S], F32R)
    h_lo = sbuf_next("h_lo", [DT, S], F32R)
    w_raw = sbuf_next("w_raw", [2, 2048])
    w_hi = sbuf_next("w_hi", [2, 2048], F32R)
    w_lo = sbuf_next("w_lo", [2, 2048], F32R)
    area = free_from[0]
    free_from[0] += 32 * 2048
    y_at = free_from[0]
    free_from[0] += 8 * 2048
    const = sbuf_next("const", [N_CONST])
    bias_at = free_from[0]
    bias_f = sbuf_next("bias", [4 * S])
    cbias_f = sbuf_next("cbias", [4 * TT * 32])
    bias = bias_f[:, :].rearrange("p (h s) -> p h s", s=S)
    cbias = cbias_f[:, :].rearrange("p (h q n) -> p h q n", q=TT, n=32)
    rows = sbuf_next("rows", [P])
    par = sbuf_next("par", [P])
    rstd = sbuf_next("rstd", [S])
    col = sbuf_next("col", [256])
    tmp = sbuf_next("tmp", [6, S])
    smx, ptx = sbuf_at("smx", free_from[0] - 6 * 2048, [2, S]), sbuf_at("ptx", free_from[0] - 4 * 2048, [2, S])
    sm2, pt2 = sbuf_at("sm2", free_from[0] - 6 * 2048, [2, S]), sbuf_at("pt2", free_from[0] - 4 * 2048, [2, S])

    def cst(name, a=0, b=None):
        lo, hi = CONST_COLS[name]
        return const[:, lo + a:(hi if b is None else lo + b)]

    ident, ones, heads1, flip, rot = (cst(n) for n in ("ident", "ones", "heads", "flip", "rot"))

    def area_tiles(name, first, n, dtype=F32, base=area):
        return sbuf_at(name, base + first * 2048, [n, S], dtype)

    x_rows = sbuf_at("x_rows", area, [TT, D])
    sq = area_tiles("sq", 0, DT)
    u_pool = sbuf_at("u_pool", area, [DT, PAD + S])
    s_pool = sbuf_at("s_pool", area + 4 * DT * (PAD + S), [2, 2, PAD + S])
    d_pool = sbuf_at("d_pool", y_at, [4, 2, S])
    z_hi = area_tiles("z_hi", 16, DT, F32R)
    z_lo = area_tiles("z_lo", 24, DT, F32R)
    hid_hi = area_tiles("hid_hi", 0, 16, F32R)
    hid_lo = area_tiles("hid_lo", 16, 16, F32R)
    ffn_tmp = area_tiles("ffn_tmp", 0, 8, F32, y_at)
    qk = area_tiles("qk", 0, 16)
    o_t = area_tiles("o_t", 16, DT)
    v_tok = sbuf_at("v_tok", y_at, [TT, D])
    masks = sbuf_at("masks", bias_at, [2 * P + 2 * S])
    alpha_bc = sbuf_at("alpha_bc", area + 24 * 2048, [3, S])
    alpha_dg = sbuf_at("alpha_dg", area + 27 * 2048, [3, TT, P])
    sm = area_tiles("sm", 28, 2)
    ptb = area_tiles("ptb", 30, 2)

    RET, RWK, CONV, NSA = 0, 8, 15, 21
    z = area_tiles("z", 0, 32)
    y_f = area_tiles("y_f", 0, DT, F32, y_at)
    PARTS = (0, 17, 4, 27)
    br_hi = [area_tiles(f"br_hi{a}", t, 2, F32R) for a, t in enumerate(PARTS)]
    br_lo = [area_tiles(f"br_lo{a}", t + 2, 2, F32R) for a, t in enumerate(PARTS)]
    merged = area_tiles("merged", 8, DT)
    tmp_at = free_from[0] - 6 * 2048
    mem_rows = sbuf_at("mem_rows", area, [2, D])
    mem_t = sbuf_at("mem_t", area + 4 * 2048, [DT, MEM])
    mem_sq = sbuf_at("mem_sq", area + 8 * 2048, [DT, MEM])
    onehot = sbuf_at("onehot", area + 12 * 2048, [N_DIST])
    vec = sbuf_at("vec", area + 16 * 2048, [N_DIST])
    rel = sbuf_at("rel", area + 20 * 2048, [4])
    hankel = sbuf_at("hankel", area + 21 * 2048, [4, 2 * S])
    cmp_w = sbuf_at("cmp_w", y_at, [NSA_LEN, HD])
    cmp_in_t = sbuf_at("cmp_in_t", y_at + 4 * 2048, [NSA_LEN, N_CMP])
    k_dup = area_tiles("k_dup", 6, 2, F32, y_at)
    nsa_small = sbuf_at("nsa_small", tmp_at + 4 * 2048, [2 * S])
    v_nsa = sbuf_at("v_nsa", tmp_at + 4 * 2048, [2, TT, HD])
    kc_dup = sbuf_at("kc_dup", tmp_at + 5 * 2048, [32])
    kc_raw = sbuf_at("kc_raw", tmp_at + 5 * 2048 + 128, [32])
    vc_tok = sbuf_at("vc_tok", tmp_at + 5 * 2048 + 256, [P])
    gate_tok = sbuf_at("gate_tok", tmp_at + 5 * 2048 + 768, [TT * 12])
    q_nsa = area_tiles("q_nsa", 31, 1)
    v_ret = sbuf_at("v_ret", y_at + 6 * 2048, [TT, 2 * P])
    u_conv = sbuf_at("u_conv", tmp_at, [2, S + 2])
    y_conv = sbuf_at("y_conv", tmp_at + 3 * 2048, [2, S])
    lora = sbuf_at("lora", area + 16 * 2048, [2 * P])
    sw, cw, aa = (area_tiles(n, t, 2, F32, y_at)[:, :, :] for n, t in (("sw", 0), ("cw", 2), ("aa", 4)))
    y_rw = area_tiles("y_rw", 4, 2, F32, y_at)[:, :, :]
    tok = sbuf_at("tok", y_at + 6 * 2048, [4, 2 * P])
    kk, bb, g_rw = (area_tiles(n, t, 2)[:, :, :] for n, t in (("kk", 25), ("bb", 23), ("g_rw", 14)))
    pb = sbuf_at("pb", tmp_at, [7, 2, P])
    e_in = sbuf_at("e_in", tmp_at + 7 * 1024, [2, P])
    state = sbuf_next("state", [2, P])
    e_any = sbuf_at("e_any", tmp_at + 8 * 1024, [2, P])
    w_t = sbuf_at("w_t", tmp_at + 9 * 1024, [2, P])
    g1 = sbuf_at("g1", tmp_at + 10 * 1024, [2 * P])
    u_rw = sbuf_at("u_rw", tmp_at + 11 * 1024, [2 * P])
    m_q, m_qm, m_r, m_t, m_y, m_ak, m_rk, m_rb = (sbuf_at(f"m{a}", area + t * 2048, [4, P])
                                                  for a, t in enumerate((4, 5, 6, 7, 21, 22, 16, 31)))
    mem_n = sbuf_at("mem_n", area, [DT, MEM])
    mn_hi = sbuf_at("mn_hi", area + 4 * 2048, [DT, MEM], F32R)
    mn_lo = sbuf_at("mn_lo", area + 8 * 2048, [DT, MEM], F32R)
    k_xa = sbuf_at("k_xa", area + 12 * 2048, [DT, MEM])
    v_xa = sbuf_at("v_xa", area + 16 * 2048, [2, D])
    q_xa = area_tiles("q_xa", 20, DT)
    sq2 = area_tiles("sq2", 12, DT)
    sq_h = sbuf_at("sq_h", BASE + 2 * 4 * DT * S, [DT, S])
    out_rows = sbuf_at("out_rows", area, [TT, D])

    ps = nc.alloc_psum_tensor("ps", [P, 8, S], F32)

    const_in = signal("const_in")
    rows_in = signal("rows_in")
    rows_zero = signal("rows_zero")
    raw_landed = [signal(f"raw_landed{i}") for i in range(2)]
    hi_done = signal("hi_done")
    w_split = signal("w_split")
    chunk_begun = signal("chunk_begun")
    tile_done = signal("tile_done")
    bank_free = signal("bank_free", 4, "pe")
    sq_ready = signal("sq_ready")
    ss_ready = signal("ss_ready")
    xhi_ready = signal("xhi_ready")
    xlo_ready = signal("xlo_ready")
    mv_ready = signal("mv_ready")
    rstd_ready = signal("rstd_ready")
    gate_scaled = signal("gate_scaled", 2, "pe")
    up_scaled = signal("up_scaled", 2, "pe")
    act_ready = signal("act_ready")
    prod_ready = signal("prod_ready")
    hid_hi_ready = signal("hid_hi_ready")
    hid_ready = signal("hid_ready")
    turned = signal("turned")
    x_turned = signal("x_turned")
    rot_ready = signal("rot_ready")
    rot_taken = signal("rot_taken", 4, "pe")
    staged = signal("staged")
    v_taken = signal("v_taken")
    alpha_ready = signal("alpha_ready")
    alpha_sum = signal("alpha_sum")
    par_done = signal("par_done")
    cmp_landed, lora_landed = signal("cmp_landed"), signal("lora_landed")
    mem_landed, mem_stored = signal("mem_landed"), signal("mem_stored")
    vec_ready, vec_stored, hankel_in = signal("vec_ready"), signal("vec_stored"), signal("hankel_in")
    pe_dve, pe_act = signal("pe_dve"), signal("pe_act")
    dve_pe, act_pe = signal("dve_pe"), signal("act_pe")
    copied = signal("copied", 4, "pe")
    p2_used = signal("p2_used", 8, "act")
    gate_out = signal("gate_out", 4, "pe")
    y_ready = signal("y_ready", 4, "pe")
    mn_ready = signal("mn_ready")
    v_out = signal("v_out", 4, "pe")
    settled = signal("settled")
    relu_out = signal("relu_out", 4, "pe")
    v_turned = signal("v_turned")
    out_ready = signal("out_ready")
    rel_marked = signal("rel_marked")
    a_to_d, d_to_a = signal("a_to_d"), signal("d_to_a")
    act_step = signal("act_step")
    dve_step = signal("dve_step")
    s_ready = signal("s_ready")
    s_taken = signal("s_taken", 2, "pe")
    e_ready = signal("e_ready")
    p_ready = signal("p_ready")
    pt_ready = signal("pt_ready")
    pt_copied = signal("pt_copied")
    pv_done = signal("pv_done")
    o_taken = signal("o_taken")
    stage_pe, stage_act, stage_dve = (signal(n) for n in ("stage_pe", "stage_act", "stage_dve"))
    stored = signal("stored")
    ends = {"pe": stage_pe, "act": stage_act, "dve": stage_dve}
    for who, value in (("sp", -2), ("act", -1), ("pool", -1)):
        start(chunk_begun, who, value)

    pe, act, dve, sp, pool = nc.tensor, nc.scalar, nc.vector, nc.sync, nc.gpsimd

    def wait(eng, sem_value):
        sem, value = sem_value
        if not isinstance(value, int) or value > 0:
            eng.wait_ge(sem, value)

    def end_stage(who):
        settle({"pe": pe, "act": act, "dve": dve}[who])
        {"pe": pe, "act": act, "dve": dve}[who].drain().then_inc(ends[who], 1)
        for other in ends:
            if other != who:
                {"pe": pe, "act": act, "dve": dve}[who].wait_ge(*take(ends[other], who))

    def link(ins):
        ins.then_inc(dve_step, 1)
        dve.wait_ge(*take(dve_step, "dve"))

    def alink(ins):
        ins.then_inc(act_step, 1)
        act.wait_ge(*take(act_step, "act"))

    def load(slot, *parts):
        wait(sp, take(chunk_begun, "sp"))
        settle(sp)
        for dst, src in parts:
            sp.dma_start(dst, src).then_inc(raw_landed[slot], 16)

    def raw(slot, kt, c, at=0):
        return w_raw[:, slot, at:at + kt * c].rearrange("p (k c) -> p k c", c=c)

    def split_hi(slot, size=2048):
        act.wait_ge(*take(raw_landed[slot], "act", 32))
        wait(act, take(chunk_begun, "act"))
        act.activation(w_hi[:, slot, 0:size], w_raw[:, slot, 0:size], ACT.Copy).then_inc(hi_done, 1)

    def split_lo(slot):
        pool.wait_ge(*take(hi_done, "pool"))
        wait(pool, take(chunk_begun, "pool"))
        pool.tensor_tensor(w_lo[:, slot], w_raw[:, slot], w_hi[:, slot].bitcast(F32), ALU.subtract)\
            .then_inc(w_split, 1)

    def parts_of(slot, kt, c, at=0):
        return [w[:, slot, at:at + kt * c].rearrange("p (k c) -> p k c", c=c) for w in (w_hi, w_lo)]

    def product(o, w, cols, rhs, kts, begin=False, first=True, last=True):
        (whi, wlo), (rhi, rlo) = w, rhs
        n = len(kts)
        for a, (kw, kr) in enumerate(kts):
            ins = pe.matmul(o, whi[:, kw, cols], rhi(kr), start=first and a == 0, stop=False)
            if begin and a == 0:
                ins.then_inc(chunk_begun, 1)
            pe.matmul(o, whi[:, kw, cols], rlo(kr), start=False, stop=False)
            ins = pe.matmul(o, wlo[:, kw, cols], rhi(kr), start=False, stop=last and a == n - 1)
        return ins

    def moving(hi, lo):
        return (lambda t: hi[:, t, :]), (lambda t: lo[:, t, :])

    def pe_tiles(rhs, kt, c, slot, banks, free=bank_free, n=S):
        pe.wait_ge(*take(w_split, "pe"))
        w = parts_of(slot, kt, c)
        for t in range(-(-c // P)):
            pe.wait_ge(*take(free, "pe"))
            width = min(P, c - P * t)
            product(ps[0:width, banks[t], 0:n], w, slice(P * t, P * t + width), rhs, [(a, a) for a in range(kt)], begin=t == 0)\
                .then_inc(tile_done, 1)

    def norm_act(gain, n=DT):
        for t in range(DT):
            act.activation(sq[:, t, :], x[:, t, :], ACT.Square).then_inc(sq_ready, 1)
            act.activation(h_hi[:, t, :], x[:, t, :], ACT.Identity, scale=par[:, gain + t:gain + t + 1])\
                .then_inc(xhi_ready, 1)
        factor_act()

    def factor_act(n=S):
        act.wait_ge(*take(mv_ready, "act"))
        act.activation(rstd[:, 0:n], rstd[:, 0:n], ACT.Sqrt).then_inc(rstd_ready, 1)

    def norm_dve(gain):
        for t in range(DT):
            dve.wait_ge(*take(xhi_ready, "dve"))
            dve.scalar_tensor_tensor(h_lo[:, t, :], x[:, t, :], par[:, gain + t:gain + t + 1],
                                     h_hi[:, t, :].bitcast(F32), ALU.mult, ALU.subtract).then_inc(xlo_ready, 1)
        factor_dve()

    def factor_dve(n=S):
        dve.wait_ge(*take(ss_ready, "dve"))
        link(dve.tensor_scalar(rstd[:, 0:n], ps[:, 7, 0:n], 1.0 / D, EPS, ALU.mult, ALU.add))
        dve.reciprocal(rstd[:, 0:n], rstd[:, 0:n]).then_inc(mv_ready, 1)
        dve.wait_ge(*take(rstd_ready, "dve"))

    def sums_pe(sq=sq):
        for t in range(DT):
            pe.wait_ge(*take(sq_ready, "pe"))
            ins = pe.matmul(ps[:, 7, :], ones, sq[:, t, :], start=t == 0, stop=t == DT - 1)
        ins.then_inc(ss_ready, 1)

    def norm_pe():
        sums_pe()
        pe.wait_ge(*take(xlo_ready, "pe", DT))

    def to_parts_act(src, n):
        for t in range(n):
            act.wait_ge(*take(prod_ready, "act"))
            act.activation(h_hi[:, t, :], src[:, t, :], ACT.Copy).then_inc(xhi_ready, 1)

    B1 = dict(norm_mix=0, norm_ffn=16, norm_final=32, pool_scale=40)

    def start_sp():
        sp.dma_start(const[:, :], A["const"]).then_inc(const_in, 16)
        sp.dma_start(masks[:, :], A["masks"]).then_inc(const_in, 16)
        sp.dma_start(x_rows[:, :, :], A["x"][0].rearrange("(t p) d -> p t d", p=P)).then_inc(const_in, 16)
        sp.wait_ge(*take(rows_zero, "sp"))
        for at, src, n in ((0, A["norm_mix"].rearrange("l (t c) -> (l t) c", c=P), 16),
                           (16, A["norm_ffn"].rearrange("l (t c) -> (l t) c", c=P), 16),
                           (32, A["norm_final"].rearrange("(t c) -> t c", c=P), 8),
                           (40, A["pool_scale"].rearrange("l (t c) -> (l t) c", c=P), 8)):
            sp.dma_start(rows[at:at + n, :], src).then_inc(rows_in, 16)

    def start_pe():
        pe.wait_ge(*take(const_in, "pe", 48))
        for t in range(DT):
            for q in range(TT):
                ins = pe.transpose(ps[:, t, P * q:P * q + P], x_rows[:, q, P * t:P * t + P], ident)
            ins.then_inc(turned, 1)
        pe.wait_ge(*take(rows_in, "pe", 64))
        pe.wait_ge(*take(x_turned, "pe"))
        pe.transpose(ps[:, 0, 0:P], rows[:, :], ident).then_inc(turned, 1)
        end_stage("pe")

    def start_act():
        split_hi(0)
        end_stage("act")

    def start_dve():
        for t in range(DT):
            dve.wait_ge(*take(turned, "dve"))
            dve.tensor_copy(x[:, t, :], ps[:, t, :]).then_inc(x_turned, 1)
        dve.wait_ge(*take(turned, "dve"))
        dve.tensor_copy(par[:, :], ps[:, 0, 0:P]).then_inc(par_done, 1)
        end_stage("dve")

    pool_in = A["pool_w_in"][0]
    pool_out = A["pool_w_out"][0]

    def load_cols(w, c0, slot, c=256):
        load_rows(w[:, bass.ds(c0, c)], slot, DT, c)

    def load_rows(w, slot, kt, c):
        src, dst, half = w.rearrange("(k p) c -> p k c", p=P), raw(slot, kt, c), kt // 2
        load(slot, (dst[:, 0:half, :], src[:, 0:half, :]), (dst[:, half:, :], src[:, half:, :]))

    def pool_sp():
        for c in range(4):
            load_cols(pool_in, 256 * c, c % 2)
        for c in range(2):
            load_rows(A["pool_w_group"][0].rearrange("g d c -> (g d) c")[512 * c:512 * c + 512, :], c, 4, 256)
        for c in range(4):
            load_cols(pool_out, 256 * c, c % 2)

    def pool_pe():
        norm_pe()
        hm = moving(h_hi, h_lo)
        for c in range(4):
            pe_tiles(hm, DT, 256, c % 2, (2 * c % 4, 2 * c % 4 + 1))
        end_stage("pe")
        pe.wait_ge(*take(xlo_ready, "pe", DT))
        for g in range(4):
            if g % 2 == 0:
                pe.wait_ge(*take(w_split, "pe"))
            for t in range(2):
                pe.wait_ge(*take(bank_free, "pe"))
                product(ps[:, (2 * g + t) % 4, :], parts_of(g // 2, 4, 256), slice(P * t, P * t + P), hm,
                        [(2 * (g % 2) + a, 2 * g + a) for a in range(2)], begin=g % 2 == 0 and t == 0)\
                    .then_inc(tile_done, 1)
        zm = moving(z_hi, z_lo)
        pe.wait_ge(*ahead(bank_free, "pe", 4))
        for c in range(4):
            pe_tiles(zm, DT, 256, c % 2, (2 * c % 4, 2 * c % 4 + 1))
        end_stage("pe")

    def pool_act():
        norm_act(B1["norm_mix"])
        for c in range(4):
            split_hi((c + 1) % 2)
        skip(tile_done, "act", DT)
        end_stage("act")
        for g in range(4):
            act.wait_ge(*take(prod_ready, "act"))
            act.activation(h_hi[:, 2 * g:2 * g + 2, :], d_pool[:, g], ACT.Copy).then_inc(xhi_ready, 1)
        split_hi(1)
        for t in range(DT):
            if t == 4:
                split_hi(0)
            act.wait_ge(*take(tile_done, "act"))
            act.activation(z_hi[:, t, :], ps[:, t % 4, :], ACT.Identity,
                           scale=par[:, B1["pool_scale"] + t:B1["pool_scale"] + t + 1]).then_inc(hid_hi_ready, 1)
        for c in range(4):
            split_hi((c + 1) % 2)
        skip(tile_done, "act", DT)
        end_stage("act")

    def pool_dve():
        norm_dve(B1["norm_mix"])
        for t in range(DT):
            dve.wait_ge(*take(tile_done, "dve"))
            dve.tensor_tensor(u_pool[:, t, PAD:], ps[:, t % 4, :], rstd[:, :], ALU.mult).then_inc(bank_free, 1)
        end_stage("dve")
        for t in (u_pool, s_pool[:, 0], s_pool[:, 1]):
            link(dve.memset(t[:, :, 0:PAD], 0.0))
        for g, w in enumerate(POOL_WINDOWS):
            u = u_pool[:, 2 * g:2 * g + 2, :]
            cur = u
            for s in range(g + 1):
                nxt = s_pool[:, s % 2]
                link(dve.tensor_tensor(nxt[:, :, PAD:], cur[:, :, PAD:], cur[:, :, PAD - 2 ** s:PAD + S - 2 ** s], ALU.add))
                cur = nxt
            d = d_pool[:, g]
            link(dve.scalar_tensor_tensor(d, cur[:, :, PAD:], 1.0 / w, u[:, :, PAD:], ALU.mult, ALU.subtract))
            inv = cst("invcnt", 16 * g, 16 * g + 16).unsqueeze(1).to_broadcast([P, 2, 16])
            link(dve.tensor_tensor(d[:, :, 0:16], cur[:, :, PAD:PAD + 16], inv, ALU.mult))
            dve.tensor_tensor(d[:, :, 0:16], d[:, :, 0:16], u[:, :, PAD:PAD + 16], ALU.subtract).then_inc(prod_ready, 1)
            dve.wait_ge(*take(xhi_ready, "dve"))
            dve.tensor_tensor(h_lo[:, 2 * g:2 * g + 2, :], d, h_hi[:, 2 * g:2 * g + 2, :].bitcast(F32), ALU.subtract)\
                .then_inc(xlo_ready, 2)
        for t in range(DT):
            dve.wait_ge(*take(hid_hi_ready, "dve"))
            dve.scalar_tensor_tensor(z_lo[:, t, :], ps[:, t % 4, :],
                                     par[:, B1["pool_scale"] + t:B1["pool_scale"] + t + 1],
                                     z_hi[:, t, :].bitcast(F32), ALU.mult, ALU.subtract).then_inc(bank_free, 1)
        skip(tile_done, "dve", DT)
        add_to_x_dve(DT, 0)
        end_stage("dve")

    def add_to_x_dve(n, bank):
        for t in range(n):
            dve.wait_ge(*take(tile_done, "dve"))
            dve.tensor_tensor(x[:, t, :], x[:, t, :], ps[:, bank + t % 4, :], ALU.add).then_inc(bank_free, 1)

    def ffn_sp(l):
        f0 = 0
        wg, wu, wd = A["ffn_w_gate"][l], A["ffn_w_up"][l], A["ffn_w_down"][l]
        for n in FFN_HALVES:
            with loop(sp, "sp", n // 2) as i:
                for c in range(2):
                    cols = bass.ds(i * 256 + (f0 + c) * P, P)
                    load(c, (raw(c, DT, P), wg[:, cols].rearrange("(k p) c -> p k c", p=P)),
                         (raw(c, DT, P, 1024), wu[:, cols].rearrange("(k p) c -> p k c", p=P)))
            with loop(sp, "sp", 4) as i:
                for c in range(2):
                    load_rows(wd[f0 * P:(f0 + n) * P, bass.ds(i * 256 + c * P, P)], c, n, P)
            f0 += n

    def ffn_pe():
        norm_pe()
        hm, dm = moving(h_hi, h_lo), moving(hid_hi, hid_lo)
        whole, kts = slice(0, P), [(a, a) for a in range(DT)]
        for n in FFN_HALVES:
            with loop(pe, "pe", n // 2):
                for c in range(2):
                    pe.wait_ge(*take(w_split, "pe"))
                    pe.wait_ge(*take(gate_scaled, "pe"))
                    product(ps[:, 2 * c, :], parts_of(c, DT, P), whole, hm, kts, begin=True).then_inc(tile_done, 1)
                    pe.wait_ge(*take(up_scaled, "pe"))
                    product(ps[:, 2 * c + 1, :], parts_of(c, DT, P, 1024), whole, hm, kts).then_inc(tile_done, 1)
            pe.wait_ge(*take(hid_ready, "pe", n))
            with loop(pe, "pe", 2):
                for c in range(4):
                    pe.wait_ge(*take(w_split, "pe"))
                    pe.wait_ge(*take(bank_free, "pe"))
                    product(ps[:, 4 + c, :], parts_of(c % 2, n, P), whole, dm, [(a, a) for a in range(n)], begin=True)\
                        .then_inc(tile_done, 1)
        end_stage("pe")

    def ffn_act(gain, last):
        tg, sg, _, tt = (ffn_tmp[:, 2 * a:2 * a + 2, :] for a in range(4))
        norm_act(gain)
        for half, n in enumerate(FFN_HALVES):
            with loop(act, "act", n // 2) as i:
                for c in range(2):
                    split_hi(1 - c)
                    act.wait_ge(*take(gate_scaled, "act"))
                    act.activation(sg[:, c, :], tg[:, c, :], ACT.Silu).then_inc(act_ready, 1)
                    act.wait_ge(*take(prod_ready, "act"))
                    act.activation(hid_hi[:, bass.ds(i * 2 + c, 1), :], tt[:, c:c + 1, :], ACT.Copy)\
                        .then_inc(hid_hi_ready, 1)
            for c in range(DT - (last and half == 1)):
                split_hi(1 - c % 2)
            skip(tile_done, "act", 2 * n)
            act.wait_ge(*take(tile_done, "act", DT))
        end_stage("act")

    def ffn_dve(gain):
        tg, sg, tu, tt = (ffn_tmp[:, 2 * a:2 * a + 2, :] for a in range(4))
        norm_dve(gain)
        for n in FFN_HALVES:
            with loop(dve, "dve", n // 2) as i:
                for c in range(2):
                    dve.wait_ge(*take(tile_done, "dve"))
                    dve.tensor_tensor(tg[:, c, :], ps[:, 2 * c, :], rstd[:, :], ALU.mult).then_inc(gate_scaled, 1)
                    dve.wait_ge(*take(tile_done, "dve"))
                    dve.tensor_tensor(tu[:, c, :], ps[:, 2 * c + 1, :], rstd[:, :], ALU.mult).then_inc(up_scaled, 1)
                    dve.wait_ge(*take(up_scaled, "dve"))
                    dve.wait_ge(*take(act_ready, "dve"))
                    dve.tensor_tensor(tt[:, c, :], sg[:, c, :], tu[:, c, :], ALU.mult).then_inc(prod_ready, 1)
                    dve.wait_ge(*take(hid_hi_ready, "dve"))
                    dve.tensor_tensor(hid_lo[:, bass.ds(i * 2 + c, 1), :], tt[:, c:c + 1, :],
                                      hid_hi[:, bass.ds(i * 2 + c, 1), :].bitcast(F32), ALU.subtract)\
                        .then_inc(hid_ready, 1)
                    dve.wait_ge(*take(hid_ready, "dve"))
            with loop(dve, "dve", 2) as i:
                for c in range(4):
                    xt = x[:, bass.ds(i * 4 + c, 1), :]
                    dve.wait_ge(*take(tile_done, "dve"))
                    dve.tensor_tensor(xt, xt, ps[:, 4 + c:5 + c, :], ALU.add).then_inc(bank_free, 1)
        end_stage("dve")

    w_qkv = A["attn_w_qkv"][0]

    def qkv_sp():
        with loop(sp, "sp", 6) as i:
            for c in range(2):
                load_cols(w_qkv, i * 512 + 256 * c, c)

    def value_product(o, w, rhs, tok, begin):
        (whi, wlo), (rhi, rlo) = w, rhs
        for a in range(DT):
            ins = pe.matmul(o, rhi(a)[:, tok], whi[:, a, :], start=a == 0, stop=False)
            if begin and a == 0:
                ins.then_inc(chunk_begun, 1)
            pe.matmul(o, rhi(a)[:, tok], wlo[:, a, :], start=False, stop=False)
            ins = pe.matmul(o, rlo(a)[:, tok], whi[:, a, :], start=False, stop=a == DT - 1)
        return ins

    def qkv_pe():
        norm_pe()
        hm = moving(h_hi, h_lo)
        with loop(pe, "pe", 4):
            for c in range(2):
                pe_tiles(hm, DT, 256, c, (2 * c, 2 * c + 1))
        pe.wait_ge(*ahead(bank_free, "pe", 4))
        for q in range(TT):
            ins = pe.matmul(ps[:, 6, q:q + 1], rstd[:, P * q:P * q + P], ident[:, 0:1], start=True, stop=True)
        ins.then_inc(turned, 1)
        for c in range(4):
            pe.wait_ge(*take(w_split, "pe"))
            for q in range(TT):
                pe.wait_ge(*take(bank_free, "pe"))
                value_product(ps[:, q, 0:256], parts_of(c % 2, DT, 256), hm, slice(P * q, P * q + P), begin=q == 0)\
                    .then_inc(tile_done, 1)
        pe.wait_ge(*ahead(bank_free, "pe", 4))
        with loop(pe, "pe", 4) as i:
            for c in range(4):
                pe.wait_ge(*take(rot_taken, "pe"))
                pe.matmul(ps[:, c:c + 1, :], rot, qk[:, bass.ds(i * 4 + c, 1), :], start=True, stop=True)\
                    .then_inc(rot_ready, 1)
        end_stage("pe")

    def qkv_act():
        norm_act(B1["norm_mix"] + DT)
        for c in range(8):
            split_hi(1 - c % 2)
        skip(tile_done, "act", 16)
        act.wait_ge(*take(v_taken, "act"))
        for c in range(4):
            split_hi(1 - c % 2)
            for q in range(TT):
                act.wait_ge(*take(tile_done, "act"))
                act.activation(v_tok[:, q, 256 * c:256 * c + 256], ps[:, q, 0:256], ACT.Identity, scale=col[:, q:q + 1])\
                    .then_inc(bank_free, 1)
        end_stage("act")

    def qkv_dve():
        norm_dve(B1["norm_mix"] + DT)
        with loop(dve, "dve", 4) as i:
            for c in range(4):
                dve.wait_ge(*take(tile_done, "dve"))
                dve.tensor_tensor(qk[:, bass.ds(i * 4 + c, 1), :], ps[:, c:c + 1, :], rstd[:, :].unsqueeze(1), ALU.mult)\
                    .then_inc(bank_free, 1)
        dve.wait_ge(*take(turned, "dve"))
        dve.tensor_copy(col[:, 0:TT], ps[:, 6, 0:TT]).then_inc(v_taken, 1)
        skip(tile_done, "dve", 16)
        with loop(dve, "dve", 4) as i:
            for c in range(4):
                t = qk[:, bass.ds(i * 4 + c, 1), :]
                dve.wait_ge(*take(rot_ready, "dve"))
                dve.tensor_tensor(tmp[:, c:c + 1, :], ps[:, c:c + 1, :], cst("sin").unsqueeze(1), ALU.mult)\
                    .then_inc(rot_taken, 1)
                link(dve.tensor_tensor(t, t, cst("cos").unsqueeze(1), ALU.mult))
                dve.wait_ge(*take(rot_taken, "dve"))
                link(dve.tensor_tensor(t, t, tmp[:, c:c + 1, :], ALU.add))
        end_stage("dve")

    def units_pe(units, sm, ptb):
        n = len(units)
        for step in range(n + 2):
            if step < n:
                u = units[step]
                pe.wait_ge(*take(s_taken, "pe"))
                for a, (q, key) in enumerate(zip(u["q"], u["k"])):
                    ins = pe.matmul(ps[:, step % 2, 0:u["n"]], q, key, start=a == 0, stop=a == len(u["q"]) - 1)
                ins.then_inc(s_ready, 1)
            if 0 <= step - 1 < n:
                u, b = units[step - 1], (step - 1) % 2
                pe.wait_ge(*take(p_ready, "pe"))
                for j in range(0, u["n"], P):
                    w = min(P, u["n"] - j)
                    ins = pe.transpose(ps[0:w, 2 + b, j:j + P], sm[:, b, j:j + w], ident)
                ins.then_inc(pt_ready, 1)
            if 0 <= step - 2 < n:
                u, b = units[step - 2], step % 2
                pe.wait_ge(*take(pt_copied, "pe"))
                js = range(0, u["n"], P)
                for v, o in zip(u["v"], u["o"]):
                    for j in js:
                        w = min(P, u["n"] - j)
                        pe.matmul(o, v(j // P), ptb[0:w, b, j:j + P], start=u["first"] and j == 0,
                                  stop=u["last"] and j == js[-1])

    def units_act(units, sm, ptb):
        n = len(units)
        for step in range(n + 1):
            if step < n:
                u, b = units[step], step % 2
                act.wait_ge(*take(s_taken, "act"))
                act.activation(sm[:, b, 0:u["n"]], sm[:, b, 0:u["n"]], ACT.Exp, bias=u["max"], accum_out=u["sum"])\
                    .then_inc(e_ready, 1)
            if step >= 1:
                u, b = units[step - 1], (step - 1) % 2
                w, n2 = min(P, u["n"]), -(-u["n"] // P) * P
                act.wait_ge(*take(pt_ready, "act"))
                act.activation(ptb[0:w, b, 0:n2], ps[0:w, 2 + b, 0:n2], ACT.Copy).then_inc(pt_copied, 1)

    def units_dve(units, sm, ptb):
        n = len(units)
        for step in range(n + 1):
            if step < n:
                u, b = units[step], step % 2
                dve.wait_ge(*take(s_ready, "dve"))
                s_sb, s_ps = sm[:, b, 0:u["n"]], ps[:, b, 0:u["n"]]
                if u["bias"] is None:
                    link(dve.tensor_scalar(s_sb, s_ps, u["scale"], None, ALU.mult))
                else:
                    link(dve.scalar_tensor_tensor(s_sb, s_ps, u["scale"], u["bias"], ALU.mult, ALU.add))
                dve.tensor_reduce(u["max"], s_sb, AX, ALU.max, negate=True).then_inc(s_taken, 1)
            if step >= 1:
                u, b = units[step - 1], (step - 1) % 2
                dve.wait_ge(*take(e_ready, "dve"))
                link(dve.reciprocal(u["inv"], u["sum"]))
                if u["gate"] is not None:
                    link(dve.tensor_tensor(u["inv"], u["inv"], u["gate"], ALU.mult))
                dve.tensor_scalar(sm[:, b, 0:u["n"]], sm[:, b, 0:u["n"]], u["inv"], None, ALU.mult).then_inc(p_ready, 1)

    PAIRS = ((0, 3, (0, 0)), (3, 2, (1, 1)), (5, 1, (1, 2)), (6, 2, (2, 2)))
    maxes, sums, invs = col[:, 0:64], col[:, 64:128], col[:, 128:130]

    def mask_of(g, a, n):
        return masks[:, (0, 2 * P, 2 * P + S)[g] + a:(0, 2 * P, 2 * P + S)[g] + a + n]

    def pattern_units(i, t0, groups):
        units = []
        for e in range(2):
            f = slice(HD * e, HD * e + HD)
            for q in range(TT):
                g = groups[e]
                k0 = max(q - 1, 0) if g == 0 else 0
                n = (q + 1 - k0) * P
                bias_ = mask_of(0, 2 * P - n, n) if g == 0 else mask_of(g, S - n, n)
                c = (2 * t0 + e) * TT + q
                units.append(dict(
                    q=[tmp[f, 0, P * q:P * q + P]], k=[tmp[f, 2, P * k0:P * k0 + n]], gate=None,
                    n=n, bias=bias_, scale=HD ** -0.5, max=maxes[:, bass.ds(i * 8 + c, 1)],
                    sum=sums[:, bass.ds(i * 8 + c, 1)], inv=invs[:, q % 2:q % 2 + 1],
                    v=[lambda j, k0=k0, e=e: tmp[:, 1, (k0 + j) * P + HD * e:(k0 + j) * P + HD * e + HD]],
                    o=[ps[f, 4, P * q:P * q + P]], first=True, last=True))
        return units

    def pattern_pe():
        for t0, n, groups in PAIRS:
            with loop(pe, "pe", n) as i:
                pe.wait_ge(*take(staged, "pe"))
                units_pe(pattern_units(i, t0, groups), sm, ptb)
                pe.drain().then_inc(pv_done, 1)
                pe.wait_ge(*take(o_taken, "pe"))
        for g in range(3):
            for q in range(TT):
                pe.wait_ge(*take(alpha_ready, "pe"))
                ins = pe.matmul(ps[:, g, P * q:P * q + P], ones, alpha_dg[:, g, q, :], start=True, stop=True)
        ins.then_inc(alpha_sum, 1)
        pe.wait_ge(*take(xlo_ready, "pe", DT))
        hm = moving(h_hi, h_lo)
        for c in range(4):
            pe_tiles(hm, DT, 256, c % 2, (4 + 2 * c % 4, 5 + 2 * c % 4))
        end_stage("pe")

    lse, top, total, best, scale3 = (col[:, a:b] for a, b in ((130, 194), (194, 206), (206, 218), (218, 222), (222, 226)))
    HEADS = ((0, 6), (6, 11), (11, 16))

    def by_group(a, g):
        lo, hi = HEADS[g]
        return a[:, lo * TT:hi * TT].rearrange("p (h q) -> p q h", q=TT)

    def pattern_act():
        for t0, n, groups in PAIRS:
            with loop(act, "act", n) as i:
                units_act(pattern_units(i, t0, groups), sm, ptb)
                act.wait_ge(*take(pv_done, "act"))
                act.activation(o_t[:, bass.ds(i + t0, 1), :], ps[:, 4:5, :], ACT.Copy).then_inc(o_taken, 1)
        act.activation(lse, sums, ACT.Ln).then_inc(a_to_d, 1)
        act.wait_ge(*take(d_to_a, "act"))
        act.activation(lse, lse, ACT.Exp).then_inc(a_to_d, 1)
        act.wait_ge(*take(d_to_a, "act"))
        for g, (lo, hi) in enumerate(HEADS):
            t = total[:, TT * g:TT * g + TT]
            act.activation(t, t, ACT.Ln, scale=1.0 / (hi - lo)).then_inc(a_to_d, 1)
        act.wait_ge(*take(d_to_a, "act"))
        act.activation(total, total, ACT.Exp).then_inc(a_to_d, 1)
        to_parts_act(o_t, DT)
        for c in range(4):
            split_hi(1 - c % 2)
        skip(tile_done, "act", DT)
        end_stage("act")

    def pattern_dve():
        for t0, n, groups in PAIRS:
            with loop(dve, "dve", n) as i:
                link(dve.tensor_copy(tmp[:, 2:3, :], qk[:, bass.ds(i + t0 + DT, 1), :]))
                link(dve.tensor_copy(tmp[:, 0:1, :], qk[:, bass.ds(i + t0, 1), :]))
                dve.tensor_copy(tmp[:, 1, :].rearrange("p (t c) -> p t c", c=P), v_tok[:, :, bass.ds((i + t0) * P, P)])\
                    .then_inc(staged, 1)
                units_dve(pattern_units(i, t0, groups), sm, ptb)
                dve.wait_ge(*take(pv_done, "dve"))
        dve.wait_ge(*take(a_to_d, "dve"))
        link(dve.tensor_tensor(lse, lse, maxes, ALU.subtract))
        for g, (lo, hi) in enumerate(HEADS):
            t = top[:, TT * g:TT * g + TT]
            link(dve.tensor_reduce(t, by_group(lse, g), AX, ALU.max))
            ins = dve.tensor_tensor(by_group(lse, g), by_group(lse, g),
                                    t.unsqueeze(2).to_broadcast([P, TT, hi - lo]), ALU.subtract)
            if g < 2:
                link(ins)
        ins.then_inc(d_to_a, 1)
        dve.wait_ge(*take(a_to_d, "dve"))
        for g in range(3):
            ins = dve.tensor_reduce(total[:, TT * g:TT * g + TT], by_group(lse, g), AX, ALU.add)
        ins.then_inc(d_to_a, 1)
        dve.wait_ge(*take(a_to_d, "dve", 3))
        link(dve.tensor_tensor(total, total, top, ALU.add))
        over = total.rearrange("p (g q) -> p q g", q=TT)
        link(dve.tensor_reduce(best, over, AX, ALU.max))
        dve.tensor_tensor(over, over, best.unsqueeze(2).to_broadcast([P, TT, 3]), ALU.subtract).then_inc(d_to_a, 1)
        dve.wait_ge(*take(a_to_d, "dve"))
        link(dve.tensor_reduce(best, over, AX, ALU.add))
        link(dve.reciprocal(scale3, best))
        link(dve.tensor_scalar(scale3, scale3, 3.0, None, ALU.mult))
        link(dve.tensor_tensor(over, over, scale3.unsqueeze(2).to_broadcast([P, TT, 3]), ALU.mult))
        for g in range(3):
            for q in range(TT):
                dve.tensor_scalar(alpha_dg[:, g, q, :], ident, total[:, TT * g + q:TT * g + q + 1], None, ALU.mult)\
                    .then_inc(alpha_ready, 1)
        dve.wait_ge(*take(alpha_sum, "dve"))
        for t in range(DT):
            for f, g in (((slice(0, P), 0),) if t < 3 else ((slice(0, P), 1),) if t < 5 else
                         ((slice(0, HD), 1), (slice(HD, P), 2)) if t == 5 else ((slice(0, P), 2),)):
                ins = dve.tensor_tensor(o_t[f, t, :], o_t[f, t, :], ps[f, g, :], ALU.mult)
            ins.then_inc(prod_ready, 1)
            dve.wait_ge(*take(xhi_ready, "dve"))
            dve.tensor_tensor(h_lo[:, t, :], o_t[:, t, :], h_hi[:, t, :].bitcast(F32), ALU.subtract).then_inc(xlo_ready, 1)
        add_to_x_dve(DT, 4)
        end_stage("dve")

    def pattern_sp():
        for c in range(4):
            load_cols(A["attn_w_out"][0], 256 * c, c % 2)

    def final_act():
        for t in range(DT):
            act.activation(sq[:, t, :], x[:, t, :], ACT.Square).then_inc(sq_ready, 1)
        factor_act()
        end_stage("act")

    def final_pe():
        sums_pe()
        end_stage("pe")

    def final_dve():
        factor_dve()
        for t in range(DT):
            g = B1["norm_final"] + t
            link(dve.scalar_tensor_tensor(x[:, t, :], x[:, t, :], par[:, g:g + 1], rstd[:, :], ALU.mult, ALU.mult))
        end_stage("dve")


    MIX_PRE, MIX_POST, XA_PRE, LN_MEM, XA_POST, MLP_PRE, MLP_POST = range(0, 56, 8)
    RET_G, MU, W0, A0, K_K, K_A, R_K, LN_G, LN_B, CONV_W, CMP_PE = 56, 58, 65, 67, 69, 71, 73, 75, 77, 79, 96

    def par_of(col0, t=0):
        return par[:, col0 + t:col0 + t + 1]

    def layer_of(name, l, *at):
        return A[name][(bass.ds(l, 1), *at)].rearrange("o r c -> (o r) c")

    def setup_sp():
        sp.wait_ge(*take(rel_marked, "sp"))
        sp.dma_start(mem_rows[:, :, :], A["mem_2"][0].rearrange("(t p) d -> p t d", p=P)).then_inc(mem_landed, 16)
        sp.dma_start(onehot[0:33, :], A["onehot"]).then_inc(mem_landed, 16)
        sp.dma_start(rel[0:32, :], A["rel_bias_2"]).then_inc(mem_landed, 16)
        sp.wait_ge(*take(vec_ready, "sp"))
        sp.dma_start(scratch["vec"], vec[0:4, :]).then_inc(vec_stored, 16)
        sp.wait_ge(*take(vec_stored, "sp", 16))
        shifted = bass.AP(scratch["vec"].tensor, 0, [[1, P], [N_DIST, 4], [1, 2 * S]])
        sp.dma_start(hankel[:, :, :], shifted).then_inc(hankel_in, 16)
        sp.wait_ge(*take(mn_ready, "sp"))
        sp.dma_start(scratch["mem"], mem_t[:, :, :]).then_inc(mem_stored, 16)

    def setup_pe():
        pe.wait_ge(*take(mem_landed, "pe", 48))
        for f in range(DT):
            for q in range(2):
                at = MEM * (f % 2) + P * q
                ins = pe.transpose(ps[:, f // 2, at:at + P], mem_rows[:, q, P * f:P * f + P], ident)
        ins.then_inc(turned, 1)
        for a in range(3):
            ins = pe.matmul(ps[0:4, 4 + a, 0:384], rel[0:33, :], onehot[0:33, 384 * a:384 * a + 384], start=True, stop=True)
        ins.then_inc(pe_dve, 1)
        pe.wait_ge(*take(act_pe, "pe"))
        for f in range(DT):
            ins = pe.matmul(ps[:, 7, 0:MEM], ones, mem_sq[:, f, :], start=f == 0, stop=f == DT - 1)
        ins.then_inc(ss_ready, 1)
        pe.wait_ge(*take(hankel_in, "pe", 16))
        pe.wait_ge(*take(mn_ready, "pe"))
        for h in range(4):
            for a in range(2):
                ins = pe.matmul(ps[:, 2 * h + a, :], flip, hankel[:, h, S * a:S * a + S], start=True, stop=True)
        ins.then_inc(pe_dve, 1)
        end_stage("pe")

    def setup_act():
        act.wait_ge(*take(d_to_a, "act"))
        act.activation(mem_sq[:, :, :], mem_t[:, :, :], ACT.Square).then_inc(act_pe, 1)
        factor_act(MEM)
        skip(mem_landed, "act", 48)
        act.wait_ge(*take(mem_stored, "act", 16))
        end_stage("act")

    def setup_dve():
        dve.memset(rel[0:33, :], NEG).then_inc(rel_marked, 1)
        dve.wait_ge(*take(turned, "dve"))
        dve.tensor_copy(mem_t[:, :, :].rearrange("p (b f) m -> p b (f m)", f=2), ps[:, 0:4, :]).then_inc(d_to_a, 1)
        dve.wait_ge(*take(pe_dve, "dve"))
        dve.tensor_copy(vec[0:4, :].rearrange("p (a c) -> p a c", c=384), ps[0:4, 4:7, 0:384]).then_inc(vec_ready, 1)
        factor_dve(MEM)
        dve.tensor_tensor(mem_t[:, :, :], mem_t[:, :, :], rstd[:, 0:MEM].unsqueeze(1).to_broadcast([P, DT, MEM]), ALU.mult)\
            .then_inc(mn_ready, 1)
        dve.wait_ge(*take(pe_dve, "dve"))
        dve.tensor_copy(bias[:, :, :], ps[:, 0:8:2, :])
        for h in range(4):
            wide = ps[:, 2 * h:2 * h + 2, :].rearrange("p a s -> p (a s)")
            for q in range(TT):
                at = 3 * P + NSA_LEN - 1 - P * q
                dve.tensor_copy(cbias[:, h, q, 0:N_CMP], wide[:, at:at + NSA_STRIDE * (N_CMP - 1) + 1:NSA_STRIDE])
        end_stage("dve")

    def params_sp(l):
        wait(sp, take(par_done, "sp"))
        at = 0
        for name, n in (("ln_mix_pre_2", 8), ("ln_mix_post_2", 8), ("ln_xa_pre_2", 8), ("ln_mem_2", 8), ("ln_xa_post_2", 8),
                        ("ln_mlp_pre_2", 8), ("ln_mlp_post_2", 8), ("ret_norm_g_2", 2), ("rwkv_mu_2", 7), ("rwkv_w0_2", 2),
                        ("rwkv_a0_2", 2), ("rwkv_k_k_2", 2), ("rwkv_k_a_2", 2), ("rwkv_r_k_2", 2), ("rwkv_ln_g_2", 2),
                        ("rwkv_ln_b_2", 2)):
            sp.dma_start(rows[at:at + n, :], A[name][bass.ds(l, 1)].rearrange("o (t c) -> (o t) c", c=P))\
                .then_inc(rows_in, 16)
            at += n
        sp.dma_start(rows[CONV_W:CONV_W + 6, :], A["conv_w_2"][bass.ds(l, 1)].rearrange("o j (t c) -> (o j t) c", c=P))\
            .then_inc(rows_in, 16)
        for a in range(2):
            sp.dma_start(rows[CMP_PE:P, HD * a:HD * a + HD], layer_of("nsa_cmp_pe_2", l)).then_inc(rows_in, 16)

    def params_pe():
        pe.wait_ge(*take(rows_in, "pe", 19 * 16))
        pe.transpose(ps[:, 0, 0:P], rows[:, :], ident).then_inc(turned, 1)
        end_stage("pe")

    def params_act(l):
        for a in range(2):
            act.dma_start(cmp_w[HD * a:HD * a + HD, :, :], A["nsa_cmp_w_2"][bass.ds(l, 1), a].rearrange("o l d e -> d (o l) e"))\
                .then_inc(cmp_landed, 16)
        split_hi(0)
        end_stage("act")

    def params_dve():
        dve.wait_ge(*take(turned, "dve"))
        dve.tensor_copy(par[:, :], ps[:, 0, 0:P]).then_inc(par_done, 1)
        end_stage("dve")

    def mixer_in_sp(l):
        w = layer_of("w_in_2", l)
        with loop(sp, "sp", 5) as i:
            for c in range(2):
                load_cols(w, i * 512 + (IN_RET + 256 * c), c)
        load_cols(w, IN_RET + 2560, 0, P)
        load_cols(w, IN_NSA, 1)
        load_cols(w, IN_NSA + 256, 0)
        load_cols(w, IN_NSA + 512, 1, IN_RET - 512)

    def mixer_in_pe():
        norm_pe()
        hm = moving(h_hi, h_lo)
        with loop(pe, "pe", 5):
            for c in range(2):
                pe_tiles(hm, DT, 256, c, (2 * c, 2 * c + 1))
        pe_tiles(hm, DT, P, 0, (0,))
        pe_tiles(hm, DT, 256, 1, (1, 2))
        pe_tiles(hm, DT, 256, 0, (3, 0))
        pe_tiles(hm, DT, IN_RET - 512, 1, (1, 2))
        end_stage("pe")

    def mixer_in_act():
        norm_act(MIX_PRE)
        with loop(act, "act", 7):
            for c in range(2):
                split_hi(1 - c)
        skip(tile_done, "act", 27)
        end_stage("act")

    def mixer_in_dve():
        norm_dve(MIX_PRE)
        with loop(dve, "dve", 5) as i:
            for c in range(4):
                dve.wait_ge(*take(tile_done, "dve"))
                dve.tensor_tensor(z[:, bass.ds(i * 4 + c, 1), :], ps[:, c:c + 1, :], rstd[:, :].unsqueeze(1), ALU.mult)\
                    .then_inc(bank_free, 1)
        for t in range(20, 27):
            r = slice(0, P if t < 26 else 12)
            dve.wait_ge(*take(tile_done, "dve"))
            dve.tensor_tensor(z[r, t, :], ps[r, t % 4, :], rstd[r, :], ALU.mult).then_inc(bank_free, 1)
        end_stage("dve")

    def branch_act(m, src):
        for t in range(2):
            act.wait_ge(*take(prod_ready, "act"))
            act.activation(br_hi[m][:, t, :], src[:, t, :], ACT.Copy).then_inc(xhi_ready, 1)

    def branch_dve(m, src):
        for t in range(2):
            dve.wait_ge(*take(xhi_ready, "dve"))
            dve.tensor_tensor(br_lo[m][:, t, :], src[:, t, :], br_hi[m][:, t, :].bitcast(F32), ALU.subtract)\
                .then_inc(xlo_ready, 1)

    def conv_act():
        branch_act(3, y_conv)
        end_stage("act")

    def conv_dve():
        link(dve.memset(u_conv[:, :, 0:2], 0.0))
        link(dve.tensor_tensor(u_conv[:, :, 2:], z[:, CONV + 2:CONV + 4, :], z[:, CONV + 4:CONV + 6, :], ALU.mult))
        for t in range(2):
            y = y_conv[:, t, :]
            link(dve.tensor_scalar(y, u_conv[:, t, 0:S], par_of(CONV_W, t), None, ALU.mult))
            for j in (1, 2):
                link(dve.scalar_tensor_tensor(y, u_conv[:, t, j:j + S], par_of(CONV_W + 2 * j, t), y, ALU.mult, ALU.add))
            dve.tensor_tensor(y, y, z[:, CONV + t, :], ALU.mult).then_inc(prod_ready, 1)
        branch_dve(3, y_conv)
        end_stage("dve")

    def head_norm_pe(o, v):
        for src, bank in ((o, 0), (v, 2)):
            pe.wait_ge(*take(act_pe, "pe"))
            for t in range(2):
                ins = pe.matmul(ps[:, bank + t, :], heads1, src[:, t, :], start=True, stop=True)
            ins.then_inc(pe_dve, 1)

    def head_norm_act(c, v):
        act.wait_ge(*take(d_to_a, "act"))
        act.activation(v, c, ACT.Square).then_inc(act_pe, 1)
        act.wait_ge(*take(d_to_a, "act"))
        act.activation(v, v, ACT.Sqrt).then_inc(a_to_d, 1)

    def head_norm_dve(o, c, v, eps):
        dve.wait_ge(*take(pe_dve, "dve"))
        dve.scalar_tensor_tensor(c, ps[:, 0:2, :], -1.0 / HD, o, ALU.mult, ALU.add).then_inc(d_to_a, 1)
        dve.wait_ge(*take(pe_dve, "dve"))
        link(dve.tensor_scalar(v, ps[:, 2:4, :], 1.0 / HD, eps, ALU.mult, ALU.add))
        dve.reciprocal(v, v).then_inc(d_to_a, 1)
        dve.wait_ge(*take(a_to_d, "dve"))
        link(dve.tensor_tensor(c, c, v, ALU.mult))

    rq, rk, rv, rg = (z[:, RET + 2 * a:RET + 2 * a + 2, :] for a in range(4))
    RET_UNITS = [(h, j) for h in range(4) for j in range(TT)]

    def retention_pe():
        for t in range(4):
            pe.matmul(ps[:, t, :], rot, z[:, RET + t, :], start=True, stop=True).then_inc(rot_ready, 1)
        for t in range(2):
            for q in range(TT):
                ins = pe.transpose(ps[:, 4 + t, P * q:P * q + P], rv[:, t, P * q:P * q + P], ident)
            ins.then_inc(v_turned, 1)
        pe.wait_ge(*take(staged, "pe"))
        pe.wait_ge(*take(act_pe, "pe", 2))

        def outputs(u, more):
            h, j = RET_UNITS[u]
            f = slice(HD * (h % 2), HD * (h % 2) + HD)
            pe.wait_ge(*ahead(s_taken, "pe", more))
            return pe.matmul(ps[f, 6 + h // 2, P * j:S], v_ret[:, j, HD * h:HD * h + HD], tmp[:, u % 2, 0:S - P * j],
                             start=j == 0, stop=j == TT - 1)

        for u, (h, j) in enumerate(RET_UNITS):
            f = slice(HD * (h % 2), HD * (h % 2) + HD)
            pe.wait_ge(*take(s_taken, "pe"))
            pe.matmul(ps[:, u % 2, 0:S - P * j], rk[f, h // 2, P * j:P * j + P], rq[f, h // 2, P * j:S], start=True, stop=True)\
                .then_inc(s_ready, 1)
            if u:
                outputs(u - 1, 1)
        outputs(len(RET_UNITS) - 1, 2).then_inc(pe_act, 1)
        head_norm_pe(rq, rv)
        end_stage("pe")

    def retention_act(l):
        for at, name in ((0, "rwkv_w2_2"), (32, "rwkv_a2_2"), (64, "rwkv_g2_2")):
            n = 32 if at < 64 else 64
            act.dma_start(lora[at:at + n, :], layer_of(name, l)).then_inc(lora_landed, 16)
        act.activation(rg, rg, ACT.Silu)
        skip(s_taken, "act", len(RET_UNITS))
        for t in range(2):
            act.wait_ge(*take(v_turned, "act"))
            act.activation(v_ret[:, :, P * t:P * t + P], ps[:, 4 + t, :].rearrange("p (q c) -> p q c", c=P), ACT.Copy)\
                .then_inc(act_pe, 1)
        act.wait_ge(*take(pe_act, "act"))
        act.activation(rq, ps[:, 6:8, :], ACT.Copy).then_inc(act_pe, 1)
        head_norm_act(rk, rv)
        branch_act(1, rk)
        end_stage("act")

    def retention_dve():
        dve.wait_ge(*take(rot_ready, "dve", 4))
        qk4, t4 = z[:, RET:RET + 4, :], tmp[:, 0:4, :]
        link(dve.tensor_tensor(t4, ps[:, 0:4, :], cst("sin").unsqueeze(1).to_broadcast([P, 4, S]), ALU.mult))
        link(dve.tensor_tensor(qk4, qk4, cst("cos").unsqueeze(1).to_broadcast([P, 4, S]), ALU.mult))
        link(dve.tensor_tensor(qk4, qk4, t4, ALU.add))
        dve.sem_inc(staged, 1)
        for u, (h, j) in enumerate(RET_UNITS):
            n = S - P * j
            dve.wait_ge(*take(s_ready, "dve"))
            dve.scalar_tensor_tensor(tmp[:, u % 2, 0:n], ps[:, u % 2, 0:n], HD ** -0.5, cst("decay", S * h, S * h + n),
                                     ALU.mult, ALU.mult).then_inc(s_taken, 1)
        head_norm_dve(rq, rk, rv, 1e-5)
        for t in range(2):
            dve.scalar_tensor_tensor(rk[:, t, :], rk[:, t, :], par_of(RET_G, t), rg[:, t, :], ALU.mult, ALU.mult)\
                .then_inc(prod_ready, 1)
        branch_dve(1, rk)
        end_stage("dve")

    def nsa_units(i):
        units = []
        for e in range(2):
            f = slice(HD * e, HD * e + HD)
            for q in range(TT):
                for b in range(3):
                    n = N_CMP if b == 0 else P * (q + 1)
                    if b == 0:
                        key, bias_ = kc_dup[f, 0:n], cbias_f[:, bass.ds(i * (2 * TT * 32) + (TT * e + q) * 32, n)]
                        v = lambda j: vc_tok[0:N_CMP, HD:P]
                    else:
                        key, bias_ = k_dup[f, b - 1, 0:n], bias_f[:, bass.ds(i * (2 * S) + (S * e + S - n), n)]
                        v = lambda j, b=b: v_nsa[:, b - 1, j, :]
                    u = len(units)
                    units.append(dict(q=[q_nsa[f, 0, P * q:P * q + P]], k=[key], n=n, bias=bias_, scale=HD ** -0.5,
                                      max=col[:, u:u + 1], sum=col[:, 32 + u:33 + u], inv=col[:, 64 + u % 2:65 + u % 2],
                                      gate=gate_tok[:, bass.ds(i * 6 + (12 * q + 3 * e + b), 1)], v=[v],
                                      o=[ps[f, 4, P * q:P * q + P]], first=b == 0, last=b == 2))
        return units

    def nsa_pe():
        pe.wait_ge(*take(act_pe, "pe"))
        for b in range(2):
            for q in range(TT):
                pe.transpose(ps[:, 2 + b, P * q:P * q + P], z[:, NSA + 3 + b, P * q:P * q + P], ident)
        for q in range(TT):
            ins = pe.transpose(ps[:, 1, 12 * q:12 * q + 12], z[0:12, NSA + 5, P * q:P * q + P], ident[0:12, 0:12])
        ins.then_inc(pe_dve, 1)
        pe.wait_ge(*take(cmp_landed, "pe", 32))
        pe.wait_ge(*take(dve_pe, "pe"))
        settle(pe)
        for a in range(2):
            f = slice(HD * a, HD * a + HD)
            for j in range(NSA_LEN):
                ins = pe.matmul(ps[f, 0, 0:N_CMP], cmp_w[f, j, :], cmp_in_t[f, j, :], start=j == 0, stop=j == NSA_LEN - 1)
        ins.then_inc(pe_dve, 1)
        pe.wait_ge(*take(dve_pe, "pe"))
        pe.transpose(ps[0:N_CMP, 4, 0:P], kc_raw[:, 0:N_CMP], ident).then_inc(pe_dve, 1)
        with loop(pe, "pe", 2) as i:
            pe.wait_ge(*take(staged, "pe"))
            units_pe(nsa_units(i), sm2, pt2)
            pe.drain().then_inc(pv_done, 1)
            pe.wait_ge(*take(o_taken, "pe"))
        end_stage("pe")

    def nsa_act():
        g = z[0:12, NSA + 5, :]
        act.activation(g, g, ACT.Sigmoid).then_inc(act_pe, 1)
        with loop(act, "act", 2) as i:
            units_act(nsa_units(i), sm2, pt2)
            act.wait_ge(*take(pv_done, "act"))
            act.activation(br_hi[0][:, bass.ds(i, 1), :], ps[:, 4:5, :], ACT.Copy).then_inc(xhi_ready, 1)
        end_stage("act")

    def nsa_dve():
        strided = z[:, NSA + 2, :].rearrange("p (n b) -> p b n", b=NSA_STRIDE)
        for a in range(2):
            pe_cols = par[:, CMP_PE + NSA_STRIDE * a:CMP_PE + NSA_STRIDE * a + NSA_STRIDE]
            ins = dve.tensor_tensor(cmp_in_t[:, NSA_STRIDE * a:NSA_STRIDE * a + NSA_STRIDE, :], strided[:, :, a:a + N_CMP],
                                    pe_cols.unsqueeze(2).to_broadcast([P, NSA_STRIDE, N_CMP]), ALU.add)
        ins.then_inc(dve_pe, 1)
        for b in range(2):
            for e in range(2):
                dve.tensor_copy(k_dup[HD * e:HD * e + HD, b, :], z[0:HD, NSA + 3 + b, :])
        dve.wait_ge(*take(pe_dve, "dve"))
        link(dve.tensor_copy(gate_tok[:, :], ps[:, 1, 0:12 * TT]))
        link(dve.tensor_scalar(gate_tok[:, 0:12:3], gate_tok[:, 0:12:3], cst("late"), None, ALU.mult))
        dve.tensor_copy(v_nsa[:, :, :, :], ps[:, 2:4, :].rearrange("p b (q c) -> p b q c", c=P)[:, :, :, HD:P])
        dve.wait_ge(*take(pe_dve, "dve"))
        for e in range(2):
            dve.tensor_copy(kc_dup[HD * e:HD * e + HD, 0:N_CMP], ps[0:HD, 0, 0:N_CMP])
        dve.tensor_copy(kc_raw[:, 0:N_CMP], ps[:, 0, 0:N_CMP]).then_inc(dve_pe, 1)
        dve.wait_ge(*take(pe_dve, "dve"))
        dve.tensor_copy(vc_tok[0:N_CMP, :], ps[0:N_CMP, 4, 0:P])
        with loop(dve, "dve", 2) as i:
            dve.tensor_copy(q_nsa[:, :, :], z[:, bass.ds(i + NSA, 1), :]).then_inc(staged, 1)
            units_dve(nsa_units(i), sm2, pt2)
            dve.wait_ge(*take(pv_done, "dve"))
            dve.wait_ge(*take(xhi_ready, "dve"))
            dve.tensor_tensor(br_lo[0][:, bass.ds(i, 1), :], ps[:, 4:5, :], br_hi[0][:, bass.ds(i, 1), :].bitcast(F32),
                              ALU.subtract).then_inc(o_taken, 1)
        end_stage("dve")

    wr, wk, wv = (z[:, RWK + 2 * a:RWK + 2 * a + 2, :] for a in range(3))
    misc = z[:, RWK + 6, :]
    RT, AT, KH, BH, KBAR, BBAR, VV = range(7)
    ROW = [slice(HD * e, HD * e + HD) for e in range(2)]

    def wide(a):
        return a.unsqueeze(1).to_broadcast([P, 4, P])

    def rwkv_pe():
        pe.wait_ge(*take(act_pe, "pe", 2))
        pe.wait_ge(*take(lora_landed, "pe", 48))
        for r, bank in ((slice(0, 32), 0), (slice(32, 64), 2), (slice(64, P), 4)):
            for t in range(2):
                pe.matmul(ps[:, bank + t, :], lora[r, P * t:P * t + P], misc[r, :], start=True, stop=True)
        for t in range(2):
            ins = pe.matmul(ps[:, 6 + t, :], heads1, bb[:, t, :], start=True, stop=True)
        ins.then_inc(pe_act, 1)
        with loop(pe, "pe", TT):
            pair_pe()
        pe.wait_ge(*take(dve_pe, "pe"))
        for t in range(2):
            ins = pe.matmul(ps[:, 4 + t, :], heads1, wr[:, t, :], start=True, stop=True)
        ins.then_inc(pe_dve, 1)
        head_norm_pe(y_rw, cw)
        end_stage("pe")

    HEADS_RW = [(2 * t + e, t, ROW[e], 2 * e + t, slice(HD * (2 * t + e), HD * (2 * t + e) + HD)) for e in range(2) for t in range(2)]

    def pair_pe():
        def inner(bank, a, b):
            for h, t, f, c, _ in HEADS_RW:
                ins = pe.matmul(ps[:, bank + c // 2, P * t:P * t + P], pb[f, a, t, :], pb[f, b, t, :], start=True, stop=True)
            return ins

        def place(bank, c):
            return ps[:, bank, P * c:P * c + P]

        pe.wait_ge(*take(dve_pe, "pe"))
        inner(0, BH, AT).then_inc(pe_dve, 1)
        pe.wait_ge(*take(dve_pe, "pe"))
        inner(2, KH, AT)
        inner(4, BH, RT)
        inner(6, KH, RT).then_inc(pe_dve, 1)
        pe.wait_ge(*take(dve_pe, "pe"))
        for h, t, f, c, d in HEADS_RW:
            ins = pe.matmul(place(0, c), m_qm[:, c, :], ident, start=True, stop=True)
        ins.then_inc(pe_dve, 1)
        pe.wait_ge(*take(dve_pe, "pe"))
        pe.wait_ge(*take(act_pe, "pe"))
        for o, src in enumerate((AT, KBAR, BBAR, VV)):
            for t in range(2):
                at = 2 * P * (o % 2) + P * t
                ins = pe.transpose(ps[:, 4 + o // 2, at:at + P], pb[:, src, t, :], ident)
        ins.then_inc(pe_act, 1)
        for level in range(1, 6):
            pe.wait_ge(*take(dve_pe, "pe"))
            for h, t, f, c, d in HEADS_RW:
                ins = pe.matmul(place(0, c), m_qm[:, c, :], m_t[:, c, :], start=True, stop=True)
            ins.then_inc(pe_dve, 1)
            pe.wait_ge(*take(dve_pe, "pe"))
            if level < 5:
                for h, t, f, c, d in HEADS_RW:
                    pe.matmul(place(2, c), m_r[:, c, :], m_y[:, c, :], start=True, stop=True)
            for h, t, f, c, d in HEADS_RW:
                ins = pe.matmul(place(3, c), m_y[:, c, :], m_r[:, c, :], start=True, stop=True)
            ins.then_inc(pe_dve, 1)
            if level == 1:
                pe.wait_ge(*take(act_pe, "pe"))
                for h, t, f, c, d in HEADS_RW:
                    ins = pe.matmul(ps[:, 6, d], m_ak[:, c, :], tok[:, 3, d], start=True, stop=True)
                ins.then_inc(pe_act, 1)
                for h, t, f, c, d in HEADS_RW:
                    pe.matmul(ps[f, 4 + t, 0:P], tok[:, 3, d], m_rk[:, c, :], start=True, stop=False)
        pe.wait_ge(*take(dve_pe, "pe"))
        for h, t, f, c, d in HEADS_RW:
            pe.matmul(ps[f, 7, P * t:P * t + P], tok[:, 0, d], m_r[:, c, :], start=True, stop=True)
        pe.wait_ge(*take(act_pe, "pe"))
        for h, t, f, c, d in HEADS_RW:
            ins = pe.matmul(ps[:, 6, d], m_r[:, c, :], g1[:, d], start=True, stop=True)
        ins.then_inc(pe_act, 1)
        pe.wait_ge(*take(act_pe, "pe"))
        for n in range(2):
            r = ROW[n]
            for t in range(2):
                ins = pe.matmul(ps[:, 0, P * t:P * t + P], w_t[:, t, :], state[:, t, :], start=True, stop=True)
            ins.then_inc(pe_dve, 1)
            for t in range(2):
                pe.matmul(ps[:, 4 + t, r], state[:, t, :], pb[:, RT, t, r], start=False, stop=False)
            pe.wait_ge(*take(dve_pe, "pe"))
            for t in range(2):
                o, both = ps[:, 1, P * t:P * t + P], slice(P * t, P * t + P)
                pe.matmul(o, tok[r, 1, both], tok[r, 3, both], start=True, stop=False)
                ins = pe.matmul(o, tok[r, 2, both], u_rw[r, both], start=False, stop=True)
            ins.then_inc(pe_dve, 1)
            if n == 1:
                for h, t, f, c, d in HEADS_RW:
                    ins = pe.matmul(ps[f, 4 + t, 0:P], u_rw[:, d], m_rb[:, c, :], start=False, stop=True)
                ins.then_inc(pe_act, 1)
            pe.wait_ge(*take(dve_pe, "pe"))
        pe.wait_ge(*take(act_pe, "pe"))

    def rwkv_act():
        act.wait_ge(*take(d_to_a, "act"))
        act.activation(misc[0:32, :], misc[0:32, :], ACT.Tanh)
        act.activation(misc[HD:P, :], misc[HD:P, :], ACT.Sigmoid).then_inc(act_pe, 1)
        act.wait_ge(*take(d_to_a, "act"))
        act.activation(bb, kk, ACT.Square).then_inc(act_pe, 1)
        act.wait_ge(*take(pe_act, "act"))
        act.activation(bb, ps[:, 6:8, :], ACT.Sqrt).then_inc(a_to_d, 1)
        for t in range(2):
            act.activation(sw[:, t, :], ps[:, t, :], ACT.Sigmoid, bias=par_of(W0, t))
            act.activation(aa[:, t, :], ps[:, 2 + t, :], ACT.Sigmoid, bias=par_of(A0, t))
        act.activation(g_rw[:, :, :], ps[:, 4:6, :], ACT.Copy).then_inc(a_to_d, 1)
        with loop(act, "act", TT) as j:
            J = bass.ds(j * P, P)
            act.wait_ge(*take(d_to_a, "act"))
            act.activation(e_any[:, :, :], e_any[:, :, :], ACT.Exp, scale=-DECAY)
            act.activation(pb[:, BBAR], cw[:, :, J], ACT.Exp, scale=DECAY).then_inc(a_to_d, 1)
            act.activation(e_in[:, :, :], cw[:, :, J], ACT.Exp, scale=-DECAY).then_inc(a_to_d, 1)
            act.activation(pb[:, VV], wv[:, :, J], ACT.Copy).then_inc(act_pe, 1)
            act.wait_ge(*take(pe_act, "act"))
            act.activation(tok[:, :, :].rearrange("p (b o) c -> p b (o c)", o=2), ps[:, 4:6, :], ACT.Copy).then_inc(act_pe, 1)
            act.wait_ge(*take(pe_act, "act"))
            act.activation(g1[:, :], ps[:, 6, 0:2 * P], ACT.Copy).then_inc(act_pe, 1)
            act.wait_ge(*take(pe_act, "act"))
            act.activation(w_t[:, :, :].rearrange("p t c -> p (t c)"), ps[:, 7, 0:2 * P], ACT.Copy)
            act.activation(u_rw[:, :], ps[:, 6, 0:2 * P], ACT.Copy).then_inc(act_pe, 1)
            act.wait_ge(*take(pe_act, "act"))
            act.activation(y_rw[:, :, J], ps[:, 4:6, 0:P], ACT.Copy).then_inc(act_pe, 1)
        act.drain().then_inc(act_pe, 1)
        head_norm_act(sw[:, :, :], cw[:, :, :])
        branch_act(2, sw)
        end_stage("act")

    def rwkv_dve():
        for at, n in ((0, 4), (4, 3)):
            zt, d = z[:, RWK + at:RWK + at + n, :], tmp[:, 0:n, :]
            dve.tensor_tensor(d[:, :, 1:], zt[:, :, 0:S - 1], zt[:, :, 1:], ALU.subtract)
            link(dve.tensor_scalar(d[:, :, 0:1], zt[:, :, 0:1], -1.0, None, ALU.mult))
            for t in range(n):
                ins = dve.scalar_tensor_tensor(zt[:, t, :], d[:, t, :], par_of(MU, at + t), zt[:, t, :], ALU.mult, ALU.add)
            if at == 0:
                link(ins)
        ins.then_inc(d_to_a, 1)
        for t in range(2):
            ins = dve.tensor_scalar(kk[:, t, :], wk[:, t, :], par_of(K_K, t), None, ALU.mult)
        ins.then_inc(d_to_a, 1)
        dve.memset(state[:, :, :], 0.0)
        dve.wait_ge(*take(a_to_d, "dve"))
        link(dve.tensor_scalar(bb, bb, 1e-12, None, ALU.max))
        link(dve.reciprocal(bb, bb))
        link(dve.tensor_tensor(kk, kk, bb, ALU.mult))
        dve.wait_ge(*take(a_to_d, "dve"))
        link(dve.tensor_copy(tmp[:, 2, :].rearrange("p (n s) -> p n s", s=HD),
                             cst("chunk").unsqueeze(1).to_broadcast([P, S // HD, HD])))
        for t in range(2):
            link(dve.tensor_tensor_scan(cw[:, t, :], tmp[:, 2, :], sw[:, t, :], 0.0, ALU.mult, ALU.add))
        link(dve.tensor_tensor(bb, kk, aa, ALU.mult))
        for t in range(2):
            link(dve.tensor_scalar(tmp[:, t, :], aa[:, t, :], -1.0, par_of(K_A, t), ALU.add, ALU.mult))
            link(dve.scalar_tensor_tensor(wk[:, t, :], tmp[:, t, :], 1.0, wk[:, t, :], ALU.add, ALU.mult))
        with loop(dve, "dve", TT) as j:
            pair_dve(bass.ds(j * P, P))
        for t in range(2):
            ins = dve.scalar_tensor_tensor(wr[:, t, :], wr[:, t, :], par_of(R_K, t), wk[:, t, :], ALU.mult, ALU.mult)
        ins.then_inc(dve_pe, 1)
        dve.wait_ge(*take(pe_dve, "dve"))
        link(dve.tensor_tensor(wv, wv, ps[:, 4:6, :], ALU.mult))
        head_norm_dve(y_rw, sw[:, :, :], cw[:, :, :], 64e-5)
        for t in range(2):
            s = sw[:, t, :]
            link(dve.tensor_scalar(s, s, par_of(LN_G, t), par_of(LN_B, t), ALU.mult, ALU.add))
            link(dve.tensor_tensor(s, s, wv[:, t, :], ALU.add))
            dve.tensor_tensor(s, s, g_rw[:, t, :], ALU.mult).then_inc(prod_ready, 1)
        branch_dve(2, sw)
        end_stage("dve")

    def pair_dve(J):
        dve.tensor_tensor(e_any[:, :, :], cw[:, :, J], sw[:, :, J], ALU.subtract).then_inc(d_to_a, 1)
        dve.wait_ge(*take(a_to_d, "dve"))
        dve.scalar_tensor_tensor(pb[:, AT], kk[:, :, J], -1.0, e_any[:, :, :], ALU.mult, ALU.mult)
        dve.tensor_tensor(pb[:, BH], bb[:, :, J], pb[:, BBAR], ALU.mult).then_inc(dve_pe, 1)
        link(dve.tensor_tensor(pb[:, KH], wk[:, :, J], pb[:, BBAR], ALU.mult))
        dve.wait_ge(*take(a_to_d, "dve"))
        end = e_in[:, :, HD - 1::HD].unsqueeze(3).to_broadcast([P, 2, 2, HD])
        for dst, src in ((KBAR, KH), (BBAR, BH)):
            dve.tensor_tensor(pb[:, dst].rearrange("p t (c s) -> p t c s", s=HD), pb[:, src].rearrange("p t (c s) -> p t c s", s=HD),
                              end, ALU.mult)
        dve.tensor_tensor(pb[:, RT], wr[:, :, J], e_in[:, :, :], ALU.mult).then_inc(dve_pe, 1)

        def bank(b):
            return ps[:, b, :].rearrange("p (h c) -> p h c", c=P)

        def masked(dst, b, mask):
            return dve.tensor_tensor(dst[:, :, :].rearrange("p (e t) c -> p e t c", e=2),
                                     ps[:, b:b + 2, 0:2 * P].rearrange("p e (t c) -> p e t c", c=P),
                                     cst(mask).unsqueeze(1).unsqueeze(1).to_broadcast([P, 2, 2, P]), ALU.mult)

        def level_of(n):
            return wide(cst("level", P * n, P * n + P))

        dve.wait_ge(*take(pe_dve, "dve"))
        link(masked(m_q, 0, "strict"))
        link(dve.tensor_tensor(m_qm[:, :, :], m_q[:, :, :], level_of(0), ALU.mult))
        dve.tensor_tensor(m_r[:, :, :], m_qm[:, :, :], wide(ident), ALU.add).then_inc(dve_pe, 1)
        dve.wait_ge(*take(pe_dve, "dve"))
        masked(m_ak, 2, "strict")
        masked(m_rb, 4, "incl")
        masked(m_rk, 6, "incl").then_inc(dve_pe, 1)
        dve.wait_ge(*take(pe_dve, "dve"))
        dve.tensor_tensor(m_t[:, :, :], bank(0), wide(ident), ALU.add)
        dve.tensor_tensor(m_qm[:, :, :], m_q[:, :, :], level_of(1), ALU.mult).then_inc(dve_pe, 1)
        for level in range(1, 6):
            dve.wait_ge(*take(pe_dve, "dve"))
            dve.tensor_copy(m_y[:, :, :], bank(0)).then_inc(dve_pe, 1)
            if level < 5:
                dve.tensor_tensor(m_qm[:, :, :], m_q[:, :, :], level_of(level + 1), ALU.mult)
            dve.wait_ge(*take(pe_dve, "dve"))
            if level < 5:
                dve.tensor_tensor(m_t[:, :, :], m_t[:, :, :], bank(2), ALU.add)
            dve.tensor_tensor(m_r[:, :, :], m_r[:, :, :], bank(3), ALU.add).then_inc(dve_pe, 1)
        for n in range(2):
            r = ROW[n]
            dve.wait_ge(*take(pe_dve, "dve"))
            dve.tensor_tensor(u_rw[r, :], u_rw[r, :], ps[r, 0, 0:2 * P], ALU.add).then_inc(dve_pe, 1)
            dve.wait_ge(*take(pe_dve, "dve"))
            added = m_y[:, 0:2, :]
            link(dve.tensor_tensor(added, ps[:, 1, 0:2 * P].rearrange("p (t c) -> p t c", c=P),
                                   heads1.unsqueeze(1).to_broadcast([P, 2, P]), ALU.mult))
            for t in range(2):
                ins = dve.scalar_tensor_tensor(state[:, t, :], state[:, t, :], e_in[:, t, HD * n + HD - 1:HD * n + HD],
                                               added[:, t, :], ALU.mult, ALU.add)
            ins.then_inc(dve_pe, 1)

    def merge_sp(l):
        w = layer_of("w_in_2", l)
        for m in range(4):
            load_rows(layer_of("w_branch_2", l, m), m % 2, 2, D)
            with loop(sp, "sp", 2) as i:
                for c in range(2):
                    load_cols(w, i * 512 + (IN_GATE + D * m + 256 * c), (m + 1 + c) % 2)

    def merge_pe():
        pe.wait_ge(*take(xlo_ready, "pe", 6))
        hm = moving(h_hi, h_lo)
        for m in range(4):
            pe_tiles(moving(br_hi[m], br_lo[m]), 2, D, m % 2, (4, 5, 6, 7) * 2, free=copied)
            with loop(pe, "pe", 2):
                for c in range(2):
                    pe_tiles(hm, DT, 256, (m + 1 + c) % 2, (2 * c, 2 * c + 1), free=gate_out)
        pe.wait_ge(*take(xlo_ready, "pe", DT))

    def merge_act():
        for m in range(4):
            split_hi((m + 1) % 2)
            for t in range(DT):
                act.wait_ge(*take(tile_done, "act"))
                act.wait_ge(*take(p2_used, "act"))
                act.activation(y_f[:, t, :], ps[:, 4 + t % 4, :], ACT.Copy).then_inc(copied, 1)
            with loop(act, "act", 2):
                for c in range(2):
                    split_hi((m + c) % 2)
                    for t in range(2 * c, 2 * c + 2):
                        act.wait_ge(*take(gate_out, "act"))
                        act.activation(tmp[:, t, :], tmp[:, t, :], ACT.Sigmoid).then_inc(act_ready, 1)
            skip(tile_done, "act", DT)
        act.wait_ge(*take(prod_ready, "act", DT))
        act.dma_start(mem_n[:, :, :], scratch["mem"]).then_inc(mem_landed, 16)
        for t in range(DT):
            act.activation(h_hi[:, t, :], merged[:, t, :], ACT.Copy).then_inc(xhi_ready, 1)

    def merge_dve():
        for m in range(4):
            skip(tile_done, "dve", DT)
            with loop(dve, "dve", 2) as i:
                for n in range(5):
                    if n < 4:
                        dve.wait_ge(*take(tile_done, "dve"))
                        dve.tensor_tensor(tmp[:, n, :], ps[:, n, :], rstd[:, :], ALU.mult).then_inc(gate_out, 1)
                    if n:
                        t = bass.ds(i * 4 + (n - 1), 1)
                        s = tmp[:, n - 1:n, :]
                        dve.wait_ge(*take(act_ready, "dve"))
                        dve.wait_ge(*take(copied, "dve"))
                        dst = merged[:, t, :] if m == 0 else s
                        dve.tensor_tensor(dst, s, y_f[:, t, :], ALU.mult).then_inc(p2_used, 1)
                        dve.wait_ge(*take(p2_used, "dve"))
                        if m:
                            ins = dve.tensor_tensor(merged[:, t, :], merged[:, t, :], s, ALU.add)
                            ins.then_inc((prod_ready if m == 3 else dve_step), 1)
                            if m < 3:
                                dve.wait_ge(*take(dve_step, "dve"))
        for t in range(DT):
            dve.wait_ge(*take(xhi_ready, "dve"))
            dve.tensor_tensor(h_lo[:, t, :], merged[:, t, :], h_hi[:, t, :].bitcast(F32), ALU.subtract)\
                .then_inc(xlo_ready, 1)

    def out_sp(name, l):
        with loop(sp, "sp", 2) as i:
            for c in range(2):
                load_cols(layer_of(name, l), i * 512 + 256 * c, c)

    def out_pe():
        hm = moving(h_hi, h_lo)
        with loop(pe, "pe", 2):
            for c in range(2):
                pe_tiles(hm, DT, 256, c, (2 * c, 2 * c + 1), free=y_ready)
        sums_pe(sq2)
        end_stage("pe")

    def out_act():
        with loop(act, "act", 2) as i:
            for c in range(2):
                split_hi(1 - c)
                squares_act(i, (2 * c, 2 * c + 1), sq2)
        skip(tile_done, "act", DT)
        factor_act()
        end_stage("act")

    def squares_act(i, tiles, dst):
        for t in tiles:
            act.wait_ge(*take(y_ready, "act"))
            act.activation(dst[:, bass.ds(i * 4 + t, 1), :], y_f[:, bass.ds(i * 4 + t, 1), :], ACT.Square).then_inc(sq_ready, 1)

    def out_dve(gain):
        with loop(dve, "dve", 2) as i:
            for t in range(4):
                dve.wait_ge(*take(tile_done, "dve"))
                dve.tensor_copy(y_f[:, bass.ds(i * 4 + t, 1), :], ps[:, t:t + 1, :]).then_inc(y_ready, 1)
        post_norm_dve(gain)
        end_stage("dve")

    def post_norm_dve(gain):
        factor_dve()
        for t in range(DT):
            link(dve.scalar_tensor_tensor(y_f[:, t, :], y_f[:, t, :], par_of(gain, t), rstd[:, :], ALU.mult, ALU.mult))
            link(dve.tensor_tensor(x[:, t, :], x[:, t, :], y_f[:, t, :], ALU.add))

    def memory_sp(l):
        w = layer_of("xa_wkv_2", l)
        with loop(sp, "sp", 4) as i:
            for c in range(2):
                load_cols(w, i * 512 + 256 * c, c)

    def memory_pe():
        pe.wait_ge(*take(xlo_ready, "pe", DT))
        mm = moving(mn_hi, mn_lo)
        with loop(pe, "pe", 2):
            for c in range(2):
                pe_tiles(mm, DT, 256, c, (2 * c, 2 * c + 1), n=MEM)
        with loop(pe, "pe", 2):
            for c in range(2):
                pe.wait_ge(*take(w_split, "pe"))
                for q in range(2):
                    pe.wait_ge(*take(v_out, "pe"))
                    value_product(ps[:, 4 + 2 * c + q, 0:256], parts_of(c, DT, 256), mm, slice(P * q, P * q + P), begin=q == 0)\
                        .then_inc(tile_done, 1)
        end_stage("pe")

    def memory_act():
        act.wait_ge(*take(mem_landed, "act", 16))
        for t in range(DT):
            act.activation(mn_hi[:, t, :], mem_n[:, t, :], ACT.Identity, scale=par_of(LN_MEM, t)).then_inc(xhi_ready, 1)
        with loop(act, "act", 2):
            for c in range(2):
                split_hi(1 - c)
        skip(tile_done, "act", DT)
        with loop(act, "act", 2) as i:
            for c in range(2):
                split_hi(1 - c)
                for q in range(2):
                    act.wait_ge(*take(tile_done, "act"))
                    act.activation(v_xa[:, q:q + 1, bass.ds(i * 512 + 256 * c, 256)], ps[:, 4 + 2 * c + q:5 + 2 * c + q, 0:256], ACT.Copy)\
                        .then_inc(v_out, 1)
        end_stage("act")

    def memory_dve():
        for t in range(DT):
            dve.wait_ge(*take(xhi_ready, "dve"))
            dve.scalar_tensor_tensor(mn_lo[:, t, :], mem_n[:, t, :], par_of(LN_MEM, t), mn_hi[:, t, :].bitcast(F32),
                                     ALU.mult, ALU.subtract).then_inc(xlo_ready, 1)
        with loop(dve, "dve", 2) as i:
            for t in range(4):
                dve.wait_ge(*take(tile_done, "dve"))
                dve.tensor_copy(k_xa[:, bass.ds(i * 4 + t, 1), :], ps[:, t:t + 1, 0:MEM]).then_inc(bank_free, 1)
        skip(tile_done, "dve", DT)
        end_stage("dve")

    def cross_pe():
        norm_pe()
        hm = moving(h_hi, h_lo)
        with loop(pe, "pe", 2):
            for c in range(2):
                pe_tiles(hm, DT, 256, c, (2 * c, 2 * c + 1))
        end_stage("pe")
        for half in range(2):
            units_pe(cross_units(half), smx, ptx)
            pe.drain().then_inc(pv_done, 1)
            pe.wait_ge(*take(o_taken, "pe"))

    def cross_units(half):
        units = []
        for h in (2 * half, 2 * half + 1):
            for q in range(TT):
                u = len(units)
                units.append(dict(q=[q_xa[:, 2 * h + a, P * q:P * q + P] for a in range(2)], k=[k_xa[:, 2 * h + a, :] for a in range(2)],
                                  n=MEM, bias=None, scale=1.0 / 16, gate=None, max=col[:, u:u + 1], sum=col[:, 32 + u:33 + u],
                                  inv=col[:, 64 + u % 2:65 + u % 2],
                                  v=[lambda j, at=256 * h + P * a: v_xa[:, j, at:at + P] for a in range(2)],
                                  o=[ps[:, 4 + 2 * (h % 2) + a, P * q:P * q + P] for a in range(2)], first=True, last=True))
        return units

    def cross_act():
        norm_act(XA_PRE)
        for c in range(4):
            split_hi(1 - c % 2)
        skip(tile_done, "act", DT)
        end_stage("act")
        for half in range(2):
            units_act(cross_units(half), smx, ptx)
            act.wait_ge(*take(pv_done, "act"))
            act.activation(h_hi[:, 4 * half:4 * half + 4, :], ps[:, 4:8, :], ACT.Copy).then_inc(xhi_ready, 1)

    def cross_dve():
        norm_dve(XA_PRE)
        with loop(dve, "dve", 2) as i:
            for t in range(4):
                dve.wait_ge(*take(tile_done, "dve"))
                dve.tensor_tensor(q_xa[:, bass.ds(i * 4 + t, 1), :], ps[:, t:t + 1, :], rstd[:, :].unsqueeze(1), ALU.mult)\
                    .then_inc(bank_free, 1)
        end_stage("dve")
        for half in range(2):
            units_dve(cross_units(half), smx, ptx)
            dve.wait_ge(*take(pv_done, "dve"))
            dve.wait_ge(*take(xhi_ready, "dve"))
            dve.tensor_tensor(h_lo[:, 4 * half:4 * half + 4, :], ps[:, 4:8, :], h_hi[:, 4 * half:4 * half + 4, :].bitcast(F32),
                              ALU.subtract).then_inc(o_taken, 1)

    def mlp_sp(l):
        w1, w2 = layer_of("mlp_w1_2", l), layer_of("mlp_w2_2", l)
        for half in range(2):
            with loop(sp, "sp", 4) as i:
                for c in range(2):
                    load_cols(w1, i * 512 + (2048 * half + 256 * c), c)
            with loop(sp, "sp", 4) as i:
                for c in range(2):
                    load_rows(w2[2048 * half:2048 * half + 2048, bass.ds(i * 256 + P * c, P)], c, 16, P)

    def mlp_pe():
        norm_pe()
        hm, dm = moving(h_hi, h_lo), moving(hid_hi, hid_lo)
        for half in range(2):
            with loop(pe, "pe", 4):
                for c in range(2):
                    pe_tiles(hm, DT, 256, c, (2 * c, 2 * c + 1), free=relu_out)
            pe.wait_ge(*take(hid_ready, "pe", 16))
            with loop(pe, "pe", 2):
                for c in range(4):
                    pe_tiles(dm, 16, P, c % 2, (c if half else 4 + c,), free=y_ready if half else bank_free)
        sums_pe(sq_h)
        end_stage("pe")

    def mlp_act():
        norm_act(MLP_PRE)
        for half in range(2):
            with loop(act, "act", 4) as i:
                for c in range(2):
                    split_hi(1 - c)
                    for t in range(2 * c, 2 * c + 2):
                        act.wait_ge(*take(prod_ready, "act"))
                        act.activation(hid_hi[:, bass.ds(i * 4 + t, 1), :], tmp[:, t:t + 1, :], ACT.Copy).then_inc(hid_hi_ready, 1)
            if half == 0:
                for c in range(DT):
                    split_hi(1 - c % 2)
            skip(tile_done, "act", 16)
            if half == 0:
                act.wait_ge(*take(tile_done, "act", DT))
        skip(tile_done, "act", DT)
        for c in range(DT):
            if c < DT - 1:
                split_hi(1 - c % 2)
            squares_act(0, (c,), sq_h)
        factor_act()
        end_stage("act")

    def mlp_dve():
        norm_dve(MLP_PRE)
        for half in range(2):
            with loop(dve, "dve", 4) as i:
                for t in range(4):
                    h = tmp[:, t, :]
                    dve.wait_ge(*take(tile_done, "dve"))
                    dve.scalar_tensor_tensor(h, ps[:, t, :], 0.0, rstd[:, :], ALU.max, ALU.mult).then_inc(relu_out, 1)
                    dve.wait_ge(*take(relu_out, "dve"))
                    dve.tensor_tensor(h, h, h, ALU.mult).then_inc(prod_ready, 1)
                    dve.wait_ge(*take(hid_hi_ready, "dve"))
                    hid = bass.ds(i * 4 + t, 1)
                    dve.tensor_tensor(hid_lo[:, hid, :], tmp[:, t:t + 1, :], hid_hi[:, hid, :].bitcast(F32), ALU.subtract)\
                        .then_inc(hid_ready, 1)
                    dve.wait_ge(*take(hid_ready, "dve"))
            with loop(dve, "dve", 2) as i:
                for c in range(4):
                    y = y_f[:, bass.ds(i * 4 + c, 1), :]
                    dve.wait_ge(*take(tile_done, "dve"))
                    if half == 0:
                        dve.tensor_copy(y, ps[:, 4 + c:5 + c, :]).then_inc(bank_free, 1)
                    else:
                        dve.tensor_tensor(y, y, ps[:, c:c + 1, :], ALU.add).then_inc(y_ready, 1)
        post_norm_dve(MLP_POST)
        end_stage("dve")

    def result_sp():
        sp.wait_ge(*take(out_ready, "sp", DT))
        sp.dma_start(out[0].rearrange("(t p) d -> p t d", p=P), out_rows[:, :, :]).then_inc(stored, 16)
        sp.wait_ge(*take(stored, "sp", 16))

    def result_pe():
        for t in range(DT):
            for q in range(TT):
                ins = pe.transpose(ps[:, t, P * q:P * q + P], x[:, t, P * q:P * q + P], ident)
            ins.then_inc(turned, 1)

    def result_dve():
        for t in range(DT):
            dve.wait_ge(*take(turned, "dve"))
            dve.tensor_copy(out_rows[:, :, P * t:P * t + P], ps[:, t, :].rearrange("p (q c) -> p q c", c=P))\
                .then_inc(out_ready, 1)


    with ExitStack() as ctx:
        block = ctx.enter_context(nc.Block())

        @block.sync
        def _(_eng):
            start_sp()
            pool_sp()
            ffn_sp(0)
            qkv_sp()
            pattern_sp()
            ffn_sp(1)
            setup_sp()
            with loop(sp, "sp", LAYERS) as l:
                params_sp(l)
                mixer_in_sp(l)
                merge_sp(l)
                out_sp("w_mix_out_2", l)
                memory_sp(l)
                out_sp("xa_wq_2", l)
                out_sp("xa_wo_2", l)
                mlp_sp(l)
            result_sp()

        @block.gpsimd
        def _(_eng):
            pool.memset(rows[:, :], 0.0).then_inc(rows_zero, 1)
            split_lo(0)
            split_lo(1)
            with loop(pool, "pool", (CHUNKS_1 + LAYERS * CHUNKS_2) // 2 - 1):
                split_lo(0)
                split_lo(1)

        @block.tensor
        def _(_eng):
            for s, n in ((bank_free, 4), (gate_scaled, 2), (up_scaled, 2), (s_taken, 2), (rot_taken, 4), (copied, 4),
                         (p2_used, 8), (gate_out, 4), (y_ready, 4), (relu_out, 4), (v_out, 4)):
                pe.sem_inc(s, n)
            start_pe()
            pool_pe()
            ffn_pe()
            qkv_pe()
            pattern_pe()
            ffn_pe()
            final_pe()
            setup_pe()
            with loop(pe, "pe", LAYERS):
                params_pe()
                mixer_in_pe()
                end_stage("pe")
                retention_pe()
                nsa_pe()
                rwkv_pe()
                merge_pe()
                out_pe()
                memory_pe()
                cross_pe()
                out_pe()
                mlp_pe()
            result_pe()

        @block.scalar
        def _(_eng):
            start_act()
            pool_act()
            ffn_act(B1["norm_ffn"], False)
            qkv_act()
            pattern_act()
            ffn_act(B1["norm_ffn"] + DT, True)
            final_act()
            setup_act()
            with loop(act, "act", LAYERS) as l:
                params_act(l)
                mixer_in_act()
                conv_act()
                retention_act(l)
                nsa_act()
                rwkv_act()
                merge_act()
                out_act()
                memory_act()
                cross_act()
                out_act()
                mlp_act()

        @block.vector
        def _(_eng):
            start_dve()
            pool_dve()
            ffn_dve(B1["norm_ffn"])
            qkv_dve()
            pattern_dve()
            ffn_dve(B1["norm_ffn"] + DT)
            final_dve()
            setup_dve()
            with loop(dve, "dve", LAYERS):
                params_dve()
                mixer_in_dve()
                conv_dve()
                retention_dve()
                nsa_dve()
                rwkv_dve()
                merge_dve()
                out_dve(MIX_POST)
                memory_dve()
                cross_dve()
                out_dve(XA_POST)
                mlp_dve()
            result_dve()


CHUNKS_1 = 4 + 2 + 4 + 2 * (22 + 16) + 12 + 4
CHUNKS_2 = 14 + 4 * (1 + 4) + 4 + 8 + 4 + 4 + 2 * (8 + 8)


def kernel(**inputs):
    import concourse.bacc as bacc
    from concourse.bass_utils import run_bass_kernel_spmd

    arrays = {name: np.ascontiguousarray(a) for name, a in inputs.items()}
    arrays.update(const=constant_table(), masks=pattern_masks(), onehot=bucket_of_distance())
    rises = {}
    for _ in range(2):
        nc = bacc.Bacc("TRN2", target_bir_lowering=False, num_devices=1, dynamic_dma_scratch_size=1024)
        A = {name: nc.dram_tensor(name, a.shape, F32, kind="ExternalInput").ap() for name, a in arrays.items()}
        out = nc.dram_tensor("out", (1, S, D), F32, kind="ExternalOutput").ap()
        scratch = {"vec": nc.dram_tensor("vec_store", (4, N_DIST), F32, kind="Internal").ap(),
                   "mem": nc.dram_tensor("mem_store", (P, DT, MEM), F32, kind="Internal").ap()}
        build(nc, A, out, scratch, rises)
    r = run_bass_kernel_spmd(nc, [arrays], core_ids=[0])
    return r.results[0]["out"]
```

```python
from contextlib import ExitStack, contextmanager

import numpy as np

import concourse.bass as bass
from concourse import mybir

F32 = mybir.dt.float32
F32R = mybir.dt.float32r
ALU = mybir.AluOpType
ACT = mybir.ActivationFunctionType
AX = mybir.AxisListType.X

P = 128
S = 512
D = 1024
DT = D // P
TT = S // P
HD = 64
EPS = 1e-6
NEG = -1e30
D_FF = 2816
FFN_HALVES = (12, 10)
POOL_WINDOWS = (2, 4, 8, 16)
PAD = 16
LAYERS = 2
MEM = 256
NSA_LEN, NSA_STRIDE, N_CMP = 32, 16, 31
IN_NSA, IN_RET = 0, 652
IN_GATE = 3340
DECAY = float(np.exp(-0.5))

CONST_COLS = {}


def _layout():
    at = 0
    for name, n in (("ident", P), ("ones", P), ("heads", P), ("flip", P), ("rot", P), ("cos", S), ("sin", S),
                    ("decay", 4 * S), ("level", 6 * P), ("strict", P), ("incl", P), ("chunk", HD), ("invcnt", 64), ("late", 1)):
        CONST_COLS[name] = (at, at + n)
        at += n
    return -(-at // 8) * 8


N_CONST = _layout()


def constant_table():
    t = np.zeros((P, N_CONST), np.float32)

    def put(name, a):
        lo, hi = CONST_COLS[name]
        t[:, lo:hi] = np.asarray(a, np.float32).reshape(P, hi - lo)

    p = np.arange(P)
    put("ident", np.eye(P))
    put("ones", np.ones((P, P)))
    put("heads", (p[:, None] // HD == p[None, :] // HD))
    put("flip", np.eye(P)[::-1])
    rot = np.zeros((P, P))
    for m in range(P):
        base, d = m // HD * HD, m % HD
        if d < HD // 2:
            rot[base + d + HD // 2, m] = -1.0
        else:
            rot[base + d - HD // 2, m] = 1.0
    put("rot", rot)
    inv = (np.float32(1.0) / (np.float32(10000.0) ** (np.arange(0, HD, 2, dtype=np.float32) / np.float32(HD)))).astype(np.float32)
    ang = (np.arange(S, dtype=np.float32)[None, :] * inv[p % (HD // 2)][:, None]).astype(np.float32)
    put("cos", np.cos(ang.astype(np.float64)))
    put("sin", np.sin(ang.astype(np.float64)))
    dist = np.arange(S)[None, :] - p[:, None]
    put("decay", np.concatenate([np.where(dist >= 0, (1.0 - 2.0 ** (-5.0 - h)) ** np.maximum(dist, 0), 0.0)
                                 for h in range(4)], 1))
    same = p[:, None] // HD == p[None, :] // HD
    strict = same & (p[:, None] < p[None, :])
    levels = []
    for b in (1, 2, 4, 8, 16, 32):
        levels.append((p[:, None] // (2 * b) == p[None, :] // (2 * b)) & (p[:, None] // b % 2 == 0) & (p[None, :] // b % 2 == 1))
    put("level", np.concatenate(levels, 1))
    put("strict", strict)
    put("incl", strict | np.eye(P, dtype=bool))
    put("chunk", np.tile((np.arange(HD) != 0)[None, :], (P, 1)))
    put("late", p >= 31)
    put("invcnt", np.tile(np.concatenate([1.0 / np.minimum(np.arange(16) + 1, w) for w in POOL_WINDOWS])[None], (P, 1)))
    return t


def pattern_masks():
    q = np.arange(P)[:, None]
    local = P + q - np.arange(2 * P)[None, :]
    far = q + 3 * P - np.arange(S)[None, :]
    allowed = [(local >= 0) & (local <= P), (far >= 0) & (far % 4 == 0), (far >= 0) & (far % 16 == 0)]
    return np.concatenate([np.where(a, 0.0, NEG) for a in allowed], 1).astype(np.float32)


N_DIST = 1152


def bucket_of_distance():
    d = 511 - np.arange(N_DIST)
    n = np.maximum(d, 0)
    nf = np.maximum(n, 1).astype(np.float32)
    large = 16 + (np.log(nf / np.float32(16)) / np.float32(np.log(128 / 16)) * np.float32(16)).astype(np.int32)
    bucket = np.where(n < 16, n, np.minimum(large, 31))
    t = np.zeros((33, N_DIST), np.float32)
    t[bucket[d >= 0], np.arange(N_DIST)[d >= 0]] = 1.0
    t[32, d < 0] = 1.0
    return t


BASE = 1152
SBUF_END = 229344


def build(nc, A, out, scratch, rises):
    order, credits, taken, terms = [], {}, {}, {}

    def signal(name, credit=0, credited=None):
        sem = nc.alloc_semaphore(name)
        order.append(sem)
        credits[name] = (credit, credited)
        names[id(sem)] = name
        return sem

    names = {}

    def start(sem, who, value=None):
        key = (names[id(sem)], who)
        if key not in taken:
            credit, credited = credits[key[0]]
            taken[key] = value if value is not None else 0 if who == credited else credit
            terms[key] = []
        return key

    def skip(sem, who, n):
        taken[start(sem, who)] += n

    def take(sem, who, n=1):
        key = start(sem, who)
        taken[key] += n
        value = taken[key]
        for register, per in terms[key]:
            if per:
                value = register * per + value
        return sem, value

    def ahead(sem, who, n):
        value = take(sem, who, n)
        skip(sem, who, -n)
        return value

    def settle(eng):
        eng.sem_inc(settled, 1)

    nloops = {}

    @contextmanager
    def loop(eng, who, n):
        which = (who, nloops.get(who, 0))
        nloops[who] = which[1] + 1
        per = rises.get(which, {})
        keys = [start(s, who) for s in order]
        before = [taken[key] for key in keys]
        settle(eng)
        with eng.Fori(0, n) as i:
            for a, key in enumerate(keys):
                terms[key].append((i, per.get(a, 0)))
            yield i
            settle(eng)
            for key in keys:
                terms[key].pop()
        took = {a: taken[key] - before[a] for a, key in enumerate(keys) if taken[key] != before[a]}
        rises[which] = took
        for a, key in enumerate(keys):
            taken[key] = before[a] + n * took.get(a, 0)

    free_from = [BASE]

    def sbuf_at(name, offset, shape, dtype=F32):
        assert offset + 4 * int(np.prod(shape)) <= SBUF_END, name
        return nc.alloc_sbuf_tensor_at(name, [P, *shape], dtype, offset=offset)

    def sbuf_next(name, shape, dtype=F32):
        offset = free_from[0]
        free_from[0] += 4 * int(np.prod(shape))
        return sbuf_at(name, offset, shape, dtype)

    x = sbuf_next("x", [DT, S])
    h_hi = sbuf_next("h_hi", [DT, S], F32R)
    h_lo = sbuf_next("h_lo", [DT, S], F32R)
    w_raw = sbuf_next("w_raw", [2, 2048])
    w_hi = sbuf_next("w_hi", [2, 2048], F32R)
    w_lo = sbuf_next("w_lo", [2, 2048], F32R)
    area = free_from[0]
    free_from[0] += 32 * 2048
    y_at = free_from[0]
    free_from[0] += 8 * 2048
    const = sbuf_next("const", [N_CONST])
    bias_at = free_from[0]
    bias_f = sbuf_next("bias", [4 * S])
    cbias_f = sbuf_next("cbias", [4 * TT * 32])
    bias = bias_f[:, :].rearrange("p (h s) -> p h s", s=S)
    cbias = cbias_f[:, :].rearrange("p (h q n) -> p h q n", q=TT, n=32)
    rows = sbuf_next("rows", [P])
    par = sbuf_next("par", [P])
    rstd = sbuf_next("rstd", [S])
    col = sbuf_next("col", [256])
    tmp = sbuf_next("tmp", [6, S])

    def cst(name, a=0, b=None):
        lo, hi = CONST_COLS[name]
        return const[:, lo + a:(hi if b is None else lo + b)]

    ident, ones, heads1, flip, rot = (cst(n) for n in ("ident", "ones", "heads", "flip", "rot"))

    def area_tiles(name, first, n, dtype=F32, base=area):
        return sbuf_at(name, base + first * 2048, [n, S], dtype)

    x_rows = sbuf_at("x_rows", area, [TT, D])
    sq = area_tiles("sq", 0, DT, F32, y_at)
    u_pool = sbuf_at("u_pool", area, [DT, PAD + S])
    s_pool = sbuf_at("s_pool", area + 4 * DT * (PAD + S), [2, 2, PAD + S])
    d_pool = sbuf_at("d_pool", y_at, [4, 2, S])
    z_hi = area_tiles("z_hi", 16, DT, F32R)
    z_lo = area_tiles("z_lo", 24, DT, F32R)
    hid_hi = area_tiles("hid_hi", 0, 16, F32R)
    hid_lo = area_tiles("hid_lo", 16, 16, F32R)
    ffn_tmp = area_tiles("ffn_tmp", 0, 8, F32, y_at)
    qk = area_tiles("qk", 0, 16)
    o_t = area_tiles("o_t", 16, DT)
    v_tok = sbuf_at("v_tok", y_at, [TT, D])
    masks = sbuf_at("masks", bias_at, [2 * P + 2 * S])
    alpha_dg = sbuf_at("alpha_dg", area + 27 * 2048, [3, TT, P])
    sm = area_tiles("sm", 27, 3)
    ptb = area_tiles("ptb", 30, 2)

    RET, RWK, CONV, NSA = 0, 8, 15, 21
    z = area_tiles("z", 0, 32)
    y_f = area_tiles("y_f", 0, DT, F32, y_at)
    PARTS = (0, 17, 4, 27)
    br_hi = [area_tiles(f"br_hi{a}", t, 2, F32R) for a, t in enumerate(PARTS)]
    br_lo = [area_tiles(f"br_lo{a}", t + 2, 2, F32R) for a, t in enumerate(PARTS)]
    merged = area_tiles("merged", 8, DT)
    tmp_at = free_from[0] - 6 * 2048
    mem_rows = sbuf_at("mem_rows", area, [2, D])
    mem_t = sbuf_at("mem_t", area + 4 * 2048, [DT, MEM])
    mem_sq = sbuf_at("mem_sq", area + 8 * 2048, [DT, MEM])
    onehot = sbuf_at("onehot", area + 12 * 2048, [N_DIST])
    vec = sbuf_at("vec", area + 16 * 2048, [N_DIST])
    rel = sbuf_at("rel", area + 20 * 2048, [4])
    hankel = sbuf_at("hankel", area + 21 * 2048, [4, 2 * S])
    cmp_w = sbuf_at("cmp_w", y_at, [NSA_LEN, HD])
    cmp_in_t = sbuf_at("cmp_in_t", y_at + 4 * 2048, [NSA_LEN, N_CMP])
    k_dup = area_tiles("k_dup", 6, 2, F32, y_at)
    acc = sbuf_at("acc", tmp_at + 5 * 2048, [S])
    o_hi, o_lo = area_tiles("o_hi", 0, DT, F32R), area_tiles("o_lo", 8, DT, F32R)
    sm2, pt2 = area_tiles("sm2", 0, 3, F32, y_at), area_tiles("pt2", 3, 2, F32, y_at)
    smx, ptx = area_tiles("smx", 0, 3, F32, tmp_at), area_tiles("ptx", 3, 2, F32, tmp_at)
    v_nsa = sbuf_at("v_nsa", area + 4 * 2048, [2, TT, HD])
    kc_dup = sbuf_at("kc_dup", area + 5 * 2048, [32])
    kc_raw = sbuf_at("kc_raw", area + 5 * 2048 + 128, [32])
    vc_tok = sbuf_at("vc_tok", area + 5 * 2048 + 256, [P])
    gate_tok = sbuf_at("gate_tok", area + 5 * 2048 + 768, [TT * 12])
    v_ret = sbuf_at("v_ret", y_at + 6 * 2048, [TT, 2 * P])
    u_conv = sbuf_at("u_conv", tmp_at, [2, S + 2])
    y_conv = sbuf_at("y_conv", tmp_at + 3 * 2048, [2, S])
    lora = sbuf_at("lora", area + 16 * 2048, [2 * P])
    h_at = BASE + 4 * DT * S
    sw, cw, aa, kk, bb = (area_tiles(n, t, 2, F32, h_at)[:, :, :]
                          for n, t in (("sw", 0), ("cw", 2), ("aa", 4), ("kk", 6), ("bb", 8)))
    y_rw = area_tiles("y_rw", 4, 2, F32, h_at)[:, :, :]
    g_rw = area_tiles("g_rw", 14, 2)[:, :, :]
    m_q, m_qm, m_r, m_t, m_y, m_ak = (sbuf_at(f"m{a}", h_at + (10 + a) * 2048, [4, P]) for a in range(6))
    m_rk, m_rb = sbuf_at("m_rk", area + 31 * 2048, [4, P]), sbuf_at("m_rb", area + 16 * 2048, [4, P])
    tok = sbuf_at("tok", area + 6 * 2048, [4, 2 * P])
    pb = sbuf_at("pb", tmp_at, [7, 2, P])
    e_in, e_any, w_t = (sbuf_at(n, tmp_at + t * 1024, [2, P]) for n, t in (("e_in", 7), ("e_any", 8), ("w_t", 9)))
    g1, u_rw = sbuf_at("g1", tmp_at + 10 * 1024, [2 * P]), sbuf_at("u_rw", tmp_at + 11 * 1024, [2 * P])
    state = (sbuf_next("state", [2, P]), sbuf_at("state1", area + 5 * 2048 + 1024, [2, P]))
    mem_n = sbuf_at("mem_n", area, [DT, MEM])
    mn_hi = sbuf_at("mn_hi", area + 4 * 2048, [DT, MEM], F32R)
    mn_lo = sbuf_at("mn_lo", area + 28 * 2048, [DT, MEM], F32R)
    k_xa = sbuf_at("k_xa", area + 12 * 2048, [DT, MEM])
    v_xa = sbuf_at("v_xa", area + 16 * 2048, [2, D])
    q_xa = area_tiles("q_xa", 20, DT)
    sq2 = area_tiles("sq2", 12, DT)
    sq_h = sbuf_at("sq_h", BASE + 2 * 4 * DT * S, [DT, S])
    out_rows = sbuf_at("out_rows", area, [TT, D])

    ps = nc.alloc_psum_tensor("ps", [P, 8, S], F32)

    const_in = signal("const_in")
    rows_in = signal("rows_in")
    rows_zero = signal("rows_zero")
    raw_landed = [signal(f"raw_landed{i}") for i in range(2)]
    hi_done = signal("hi_done")
    w_split = signal("w_split")
    chunk_begun = signal("chunk_begun")
    tile_done = signal("tile_done")
    bank_free = signal("bank_free", 4, "pe")
    sq_ready = signal("sq_ready")
    ss_ready = signal("ss_ready")
    xhi_ready = signal("xhi_ready")
    xlo_ready = signal("xlo_ready")
    mv_ready = signal("mv_ready")
    rstd_ready = signal("rstd_ready")
    gate_scaled = signal("gate_scaled", 2, "pe")
    up_scaled = signal("up_scaled", 2, "pe")
    act_ready = signal("act_ready")
    prod_ready = signal("prod_ready")
    hid_hi_ready = signal("hid_hi_ready")
    hid_ready = signal("hid_ready")
    turned = signal("turned")
    x_ready = signal("x_ready", 4, "pe")
    acc_ready = signal("acc_ready")
    rot_ready = signal("rot_ready")
    rot_taken = signal("rot_taken", 4, "pe")
    staged = signal("staged")
    v_taken = signal("v_taken")
    alpha_ready = signal("alpha_ready")
    alpha_sum = signal("alpha_sum")
    par_done = signal("par_done")
    cmp_landed, lora_landed = signal("cmp_landed"), signal("lora_landed")
    mem_landed, mem_stored = signal("mem_landed"), signal("mem_stored")
    vec_ready, vec_stored, hankel_in = signal("vec_ready"), signal("vec_stored"), signal("hankel_in")
    pe_dve, pe_act = signal("pe_dve"), signal("pe_act")
    dve_pe, act_pe = signal("dve_pe"), signal("act_pe")
    copied = signal("copied", 4, "pe")
    p2_used = signal("p2_used", 8, "act")
    gate_out = signal("gate_out", 4, "pe")
    y_ready = signal("y_ready", 4, "pe")
    mn_ready = signal("mn_ready")
    v_out = signal("v_out", 4, "pe")
    settled = signal("settled")
    relu_out = signal("relu_out", 4, "pe")
    v_turned = signal("v_turned")
    out_ready = signal("out_ready")
    rel_marked = signal("rel_marked")
    a_to_d, d_to_a = signal("a_to_d"), signal("d_to_a")
    act_step = signal("act_step")
    dve_step = signal("dve_step")
    s_ready = signal("s_ready")
    s_taken = signal("s_taken", 2, "pe")
    e_ready = signal("e_ready")
    p_ready = signal("p_ready")
    pt_ready = signal("pt_ready")
    pt_copied = signal("pt_copied")
    pv_done = signal("pv_done")
    o_taken = signal("o_taken")
    stage_pe, stage_act, stage_dve = (signal(n) for n in ("stage_pe", "stage_act", "stage_dve"))
    stored = signal("stored")
    ends = {"pe": stage_pe, "act": stage_act, "dve": stage_dve}
    for who, value in (("sp", -2), ("act", -1), ("pool", -1)):
        start(chunk_begun, who, value)

    pe, act, dve, sp, pool = nc.tensor, nc.scalar, nc.vector, nc.sync, nc.gpsimd

    def wait(eng, sem_value):
        sem, value = sem_value
        if not isinstance(value, int) or value > 0:
            eng.wait_ge(sem, value)

    def end_stage(who):
        settle({"pe": pe, "act": act, "dve": dve}[who])
        {"pe": pe, "act": act, "dve": dve}[who].drain().then_inc(ends[who], 1)
        for other in ends:
            if other != who:
                {"pe": pe, "act": act, "dve": dve}[who].wait_ge(*take(ends[other], who))

    def link(ins):
        ins.then_inc(dve_step, 1)
        dve.wait_ge(*take(dve_step, "dve"))

    def alink(ins):
        ins.then_inc(act_step, 1)
        act.wait_ge(*take(act_step, "act"))

    def load(slot, *parts):
        wait(sp, take(chunk_begun, "sp"))
        settle(sp)
        for dst, src in parts:
            sp.dma_start(dst, src).then_inc(raw_landed[slot], 16)

    def raw(slot, kt, c, at=0):
        return w_raw[:, slot, at:at + kt * c].rearrange("p (k c) -> p k c", c=c)

    def split_hi(slot, size=2048):
        act.wait_ge(*take(raw_landed[slot], "act", 32))
        wait(act, take(chunk_begun, "act"))
        act.activation(w_hi[:, slot, 0:size], w_raw[:, slot, 0:size], ACT.Copy).then_inc(hi_done, 1)

    def split_lo(slot):
        pool.wait_ge(*take(hi_done, "pool"))
        wait(pool, take(chunk_begun, "pool"))
        pool.tensor_tensor(w_lo[:, slot], w_raw[:, slot], w_hi[:, slot].bitcast(F32), ALU.subtract)\
            .then_inc(w_split, 1)

    def parts_of(slot, kt, c, at=0):
        return [w[:, slot, at:at + kt * c].rearrange("p (k c) -> p k c", c=c) for w in (w_hi, w_lo)]

    def product(o, w, cols, rhs, kts, begin=False, first=True, last=True):
        (whi, wlo), (rhi, rlo) = w, rhs
        n = len(kts)
        for a, (kw, kr) in enumerate(kts):
            ins = pe.matmul(o, whi[:, kw, cols], rhi(kr), start=first and a == 0, stop=False)
            if begin and a == 0:
                ins.then_inc(chunk_begun, 1)
            pe.matmul(o, whi[:, kw, cols], rlo(kr), start=False, stop=False)
            ins = pe.matmul(o, wlo[:, kw, cols], rhi(kr), start=False, stop=last and a == n - 1)
        return ins

    def moving(hi, lo):
        return (lambda t: hi[:, t, :]), (lambda t: lo[:, t, :])

    def pe_tiles(rhs, kt, c, slot, banks, free=bank_free, n=S):
        pe.wait_ge(*take(w_split, "pe"))
        w = parts_of(slot, kt, c)
        for t in range(-(-c // P)):
            pe.wait_ge(*take(free, "pe"))
            width = min(P, c - P * t)
            product(ps[0:width, banks[t], 0:n], w, slice(P * t, P * t + width), rhs, [(a, a) for a in range(kt)], begin=t == 0)\
                .then_inc(tile_done, 1)

    def norm_act(gain):
        for t in range(DT):
            norm_tile_act(gain, t)
        factor_act()

    def norm_tile_act(gain, t):
        act.wait_ge(*take(x_ready, "act"))
        act.activation(sq[:, t, :], x[:, t, :], ACT.Square).then_inc(sq_ready, 1)
        act.activation(h_hi[:, t, :], x[:, t, :], ACT.Identity, scale=par[:, gain + t:gain + t + 1]).then_inc(xhi_ready, 1)

    def factor_act(n=S):
        act.wait_ge(*take(mv_ready, "act"))
        act.activation(rstd[:, 0:n], rstd[:, 0:n], ACT.Sqrt).then_inc(rstd_ready, 1)

    def add_square_dve(src, t):
        dve.wait_ge(*take(sq_ready, "dve"))
        link(dve.tensor_tensor(acc[:, :].unsqueeze(1), acc[:, :].unsqueeze(1), src[:, t, :], ALU.add))

    def clear_sum_dve():
        link(dve.memset(acc[:, :], 0.0))

    def add_squares_dve():
        clear_sum_dve()
        for t in range(DT):
            add_square_dve(sq, slice(t, t + 1))
        dve.sem_inc(acc_ready, 1)

    def norm_dve(gain):
        for t in range(DT):
            dve.wait_ge(*take(xhi_ready, "dve"))
            dve.wait_ge(*take(x_ready, "dve"))
            dve.scalar_tensor_tensor(h_lo[:, t, :], x[:, t, :], par[:, gain + t:gain + t + 1],
                                     h_hi[:, t, :].bitcast(F32), ALU.mult, ALU.subtract).then_inc(xlo_ready, 1)
        factor_dve()

    def factor_dve(n=S):
        dve.wait_ge(*take(ss_ready, "dve"))
        link(dve.tensor_scalar(rstd[:, 0:n], ps[:, 7, 0:n], 1.0 / D, EPS, ALU.mult, ALU.add))
        dve.reciprocal(rstd[:, 0:n], rstd[:, 0:n]).then_inc(mv_ready, 1)
        dve.wait_ge(*take(rstd_ready, "dve"))

    def sums_pe():
        pe.wait_ge(*take(acc_ready, "pe"))
        pe.matmul(ps[:, 7, :], ones, acc[:, :], start=True, stop=True).then_inc(ss_ready, 1)

    def norm_pe():
        sums_pe()
        pe.wait_ge(*take(xlo_ready, "pe", DT))

    def to_parts_act(src, n):
        for t in range(n):
            act.wait_ge(*take(prod_ready, "act"))
            act.activation(h_hi[:, t, :], src[:, t, :], ACT.Copy).then_inc(xhi_ready, 1)

    B1 = dict(norm_mix=0, norm_ffn=16, norm_final=32, pool_scale=40)

    def start_sp():
        sp.dma_start(const[:, :], A["const"]).then_inc(const_in, 16)
        sp.dma_start(masks[:, :], A["masks"]).then_inc(const_in, 16)
        sp.dma_start(x_rows[:, :, :], A["x"][0].rearrange("(t p) d -> p t d", p=P)).then_inc(const_in, 16)
        sp.wait_ge(*take(rows_zero, "sp"))
        for at, src, n in ((0, A["norm_mix"].rearrange("l (t c) -> (l t) c", c=P), 16),
                           (16, A["norm_ffn"].rearrange("l (t c) -> (l t) c", c=P), 16),
                           (32, A["norm_final"].rearrange("(t c) -> t c", c=P), 8),
                           (40, A["pool_scale"].rearrange("l (t c) -> (l t) c", c=P), 8)):
            sp.dma_start(rows[at:at + n, :], src).then_inc(rows_in, 16)

    def start_pe():
        pe.wait_ge(*take(const_in, "pe", 48))
        for t in range(DT):
            for q in range(TT):
                ins = pe.transpose(ps[:, t, P * q:P * q + P], x_rows[:, q, P * t:P * t + P], ident)
            ins.then_inc(turned, 1)
        pe.wait_ge(*take(rows_in, "pe", 64))
        pe.wait_ge(*ahead(x_ready, "pe", 4 + 1))
        skip(x_ready, "pe", DT)
        pe.transpose(ps[:, 0, 0:P], rows[:, :], ident).then_inc(turned, 1)
        end_stage("pe")

    def start_act():
        split_hi(0)
        end_stage("act")

    def start_dve():
        for t in range(DT):
            dve.wait_ge(*take(turned, "dve"))
            dve.tensor_copy(x[:, t, :], ps[:, t, :]).then_inc(x_ready, 1)
        dve.wait_ge(*take(turned, "dve"))
        dve.tensor_copy(par[:, :], ps[:, 0, 0:P]).then_inc(par_done, 1)
        end_stage("dve")

    pool_in = A["pool_w_in"][0]
    pool_out = A["pool_w_out"][0]

    def load_cols(w, c0, slot, c=256):
        load_rows(w[:, bass.ds(c0, c)], slot, DT, c)

    def load_rows(w, slot, kt, c):
        src, dst, half = w.rearrange("(k p) c -> p k c", p=P), raw(slot, kt, c), kt // 2
        load(slot, (dst[:, 0:half, :], src[:, 0:half, :]), (dst[:, half:, :], src[:, half:, :]))

    def pool_sp():
        for c in range(4):
            load_cols(pool_in, 256 * c, c % 2)
        for c in range(2):
            load_rows(A["pool_w_group"][0].rearrange("g d c -> (g d) c")[512 * c:512 * c + 512, :], c, 4, 256)
        for c in range(4):
            load_cols(pool_out, 256 * c, c % 2)

    def pool_pe():
        norm_pe()
        hm = moving(h_hi, h_lo)
        for c in range(4):
            pe_tiles(hm, DT, 256, c % 2, (2 * c % 4, 2 * c % 4 + 1))
        end_stage("pe")
        pe.wait_ge(*take(xlo_ready, "pe", DT))
        for g in range(4):
            if g % 2 == 0:
                pe.wait_ge(*take(w_split, "pe"))
            for t in range(2):
                pe.wait_ge(*take(bank_free, "pe"))
                product(ps[:, (2 * g + t) % 4, :], parts_of(g // 2, 4, 256), slice(P * t, P * t + P), hm,
                        [(2 * (g % 2) + a, 2 * g + a) for a in range(2)], begin=g % 2 == 0 and t == 0)\
                    .then_inc(tile_done, 1)
        zm = moving(z_hi, z_lo)
        pe.wait_ge(*ahead(bank_free, "pe", 4))
        for c in range(4):
            pe_tiles(zm, DT, 256, c % 2, (2 * c % 4, 2 * c % 4 + 1), free=x_ready)

    def pool_act():
        norm_act(B1["norm_mix"])
        for c in range(4):
            split_hi((c + 1) % 2)
        skip(tile_done, "act", DT)
        end_stage("act")
        for g in range(4):
            act.wait_ge(*take(prod_ready, "act"))
            act.activation(h_hi[:, 2 * g:2 * g + 2, :], d_pool[:, g], ACT.Copy).then_inc(xhi_ready, 1)
        split_hi(1)
        for t in range(DT):
            if t == 4:
                split_hi(0)
            act.wait_ge(*take(tile_done, "act"))
            act.activation(z_hi[:, t, :], ps[:, t % 4, :], ACT.Identity,
                           scale=par[:, B1["pool_scale"] + t:B1["pool_scale"] + t + 1]).then_inc(hid_hi_ready, 1)
        add_to_x_act(B1["norm_ffn"])

    def add_to_x_act(gain):
        for c in range(4):
            split_hi(1 - c % 2)
            if c:
                norm_tile_act(gain, 2 * c - 2)
                norm_tile_act(gain, 2 * c - 1)
        norm_tile_act(gain, 6)
        norm_tile_act(gain, 7)
        skip(tile_done, "act", DT)
        factor_act()

    def pool_dve():
        add_squares_dve()
        norm_dve(B1["norm_mix"])
        for t in range(DT):
            dve.wait_ge(*take(tile_done, "dve"))
            dve.tensor_tensor(u_pool[:, t, PAD:], ps[:, t % 4, :], rstd[:, :], ALU.mult).then_inc(bank_free, 1)
        end_stage("dve")
        for t in (u_pool, s_pool[:, 0], s_pool[:, 1]):
            link(dve.memset(t[:, :, 0:PAD], 0.0))
        for g, w in enumerate(POOL_WINDOWS):
            u = u_pool[:, 2 * g:2 * g + 2, :]
            cur = u
            for s in range(g + 1):
                nxt = s_pool[:, s % 2]
                link(dve.tensor_tensor(nxt[:, :, PAD:], cur[:, :, PAD:], cur[:, :, PAD - 2 ** s:PAD + S - 2 ** s], ALU.add))
                cur = nxt
            d = d_pool[:, g]
            link(dve.scalar_tensor_tensor(d, cur[:, :, PAD:], 1.0 / w, u[:, :, PAD:], ALU.mult, ALU.subtract))
            inv = cst("invcnt", 16 * g, 16 * g + 16).unsqueeze(1).to_broadcast([P, 2, 16])
            link(dve.tensor_tensor(d[:, :, 0:16], cur[:, :, PAD:PAD + 16], inv, ALU.mult))
            dve.tensor_tensor(d[:, :, 0:16], d[:, :, 0:16], u[:, :, PAD:PAD + 16], ALU.subtract).then_inc(prod_ready, 1)
            dve.wait_ge(*take(xhi_ready, "dve"))
            dve.tensor_tensor(h_lo[:, 2 * g:2 * g + 2, :], d, h_hi[:, 2 * g:2 * g + 2, :].bitcast(F32), ALU.subtract)\
                .then_inc(xlo_ready, 2)
        for t in range(DT):
            dve.wait_ge(*take(hid_hi_ready, "dve"))
            dve.scalar_tensor_tensor(z_lo[:, t, :], ps[:, t % 4, :],
                                     par[:, B1["pool_scale"] + t:B1["pool_scale"] + t + 1],
                                     z_hi[:, t, :].bitcast(F32), ALU.mult, ALU.subtract).then_inc(bank_free, 1)
        skip(tile_done, "dve", DT)
        add_to_x_dve(0)

    def add_to_x_dve(bank):
        clear_sum_dve()
        for t in range(DT):
            dve.wait_ge(*take(tile_done, "dve"))
            dve.tensor_tensor(x[:, t, :], x[:, t, :], ps[:, bank + t % 4, :], ALU.add).then_inc(x_ready, 1)
            add_square_dve(sq, slice(t, t + 1))
        dve.sem_inc(acc_ready, 1)

    def ffn_sp(l):
        f0 = 0
        wg, wu, wd = A["ffn_w_gate"][l], A["ffn_w_up"][l], A["ffn_w_down"][l]
        for n in FFN_HALVES:
            with loop(sp, "sp", n // 2) as i:
                for c in range(2):
                    cols = bass.ds(i * 256 + (f0 + c) * P, P)
                    load(c, (raw(c, DT, P), wg[:, cols].rearrange("(k p) c -> p k c", p=P)),
                         (raw(c, DT, P, 1024), wu[:, cols].rearrange("(k p) c -> p k c", p=P)))
            with loop(sp, "sp", 4) as i:
                for c in range(2):
                    load_rows(wd[f0 * P:(f0 + n) * P, bass.ds(i * 256 + c * P, P)], c, n, P)
            f0 += n

    def ffn_pe():
        norm_pe()
        hm, dm = moving(h_hi, h_lo), moving(hid_hi, hid_lo)
        whole, kts = slice(0, P), [(a, a) for a in range(DT)]
        for half, n in enumerate(FFN_HALVES):
            with loop(pe, "pe", n // 2):
                for c in range(2):
                    pe.wait_ge(*take(w_split, "pe"))
                    pe.wait_ge(*take(gate_scaled, "pe"))
                    product(ps[:, 2 * c, :], parts_of(c, DT, P), whole, hm, kts, begin=True).then_inc(tile_done, 1)
                    pe.wait_ge(*take(up_scaled, "pe"))
                    product(ps[:, 2 * c + 1, :], parts_of(c, DT, P, 1024), whole, hm, kts).then_inc(tile_done, 1)
            pe.wait_ge(*take(hid_ready, "pe", n))
            with loop(pe, "pe", 2):
                for c in range(4):
                    pe.wait_ge(*take(w_split, "pe"))
                    pe.wait_ge(*take(x_ready if half else bank_free, "pe"))
                    product(ps[:, 4 + c, :], parts_of(c % 2, n, P), whole, dm, [(a, a) for a in range(n)], begin=True)\
                        .then_inc(tile_done, 1)

    def ffn_act(next_gain, last=False):
        tg, sg, _, tt = (ffn_tmp[:, 2 * a:2 * a + 2, :] for a in range(4))

        def after(t):
            if last:
                square_act(t)
            else:
                norm_tile_act(next_gain, t)

        for half, n in enumerate(FFN_HALVES):
            with loop(act, "act", n // 2) as i:
                for c in range(2):
                    split_hi(1 - c)
                    act.wait_ge(*take(gate_scaled, "act"))
                    act.activation(sg[:, c, :], tg[:, c, :], ACT.Silu).then_inc(act_ready, 1)
                    act.wait_ge(*take(prod_ready, "act"))
                    act.activation(hid_hi[:, bass.ds(i * 2 + c, 1), :], tt[:, c:c + 1, :], ACT.Copy)\
                        .then_inc(hid_hi_ready, 1)
            skip(tile_done, "act", 2 * n + DT * half)
            for c in range(DT):
                if not (last and half and c == DT - 1):
                    split_hi(1 - c % 2)
                if half and c:
                    after(c - 1)
            if half == 0:
                act.wait_ge(*take(tile_done, "act", DT))
        after(DT - 1)
        factor_act()

    def ffn_dve(gain):
        tg, sg, tu, tt = (ffn_tmp[:, 2 * a:2 * a + 2, :] for a in range(4))
        norm_dve(gain)
        for half, n in enumerate(FFN_HALVES):
            with loop(dve, "dve", n // 2) as i:
                for c in range(2):
                    dve.wait_ge(*take(tile_done, "dve"))
                    dve.tensor_tensor(tg[:, c, :], ps[:, 2 * c, :], rstd[:, :], ALU.mult).then_inc(gate_scaled, 1)
                    dve.wait_ge(*take(tile_done, "dve"))
                    dve.tensor_tensor(tu[:, c, :], ps[:, 2 * c + 1, :], rstd[:, :], ALU.mult).then_inc(up_scaled, 1)
                    dve.wait_ge(*take(up_scaled, "dve"))
                    dve.wait_ge(*take(act_ready, "dve"))
                    dve.tensor_tensor(tt[:, c, :], sg[:, c, :], tu[:, c, :], ALU.mult).then_inc(prod_ready, 1)
                    dve.wait_ge(*take(hid_hi_ready, "dve"))
                    dve.tensor_tensor(hid_lo[:, bass.ds(i * 2 + c, 1), :], tt[:, c:c + 1, :],
                                      hid_hi[:, bass.ds(i * 2 + c, 1), :].bitcast(F32), ALU.subtract)\
                        .then_inc(hid_ready, 1)
                    dve.wait_ge(*take(hid_ready, "dve"))
            if half:
                clear_sum_dve()
            with loop(dve, "dve", 2) as i:
                for c in range(4):
                    t = bass.ds(i * 4 + c, 1)
                    dve.wait_ge(*take(tile_done, "dve"))
                    dve.tensor_tensor(x[:, t, :], x[:, t, :], ps[:, 4 + c:5 + c, :], ALU.add)\
                        .then_inc(x_ready if half else bank_free, 1)
                    if half:
                        add_square_dve(sq, t)
        settle(dve)
        dve.sem_inc(acc_ready, 1)

    w_qkv = A["attn_w_qkv"][0]

    def qkv_sp():
        with loop(sp, "sp", 6) as i:
            for c in range(2):
                load_cols(w_qkv, i * 512 + 256 * c, c)

    def value_product(o, w, rhs, tok, begin):
        (whi, wlo), (rhi, rlo) = w, rhs
        for a in range(DT):
            ins = pe.matmul(o, rhi(a)[:, tok], whi[:, a, :], start=a == 0, stop=False)
            if begin and a == 0:
                ins.then_inc(chunk_begun, 1)
            pe.matmul(o, rhi(a)[:, tok], wlo[:, a, :], start=False, stop=False)
            ins = pe.matmul(o, rlo(a)[:, tok], whi[:, a, :], start=False, stop=a == DT - 1)
        return ins

    def qkv_pe():
        norm_pe()
        hm = moving(h_hi, h_lo)
        with loop(pe, "pe", 4):
            for c in range(2):
                pe_tiles(hm, DT, 256, c, (2 * c, 2 * c + 1))
        pe.wait_ge(*ahead(bank_free, "pe", 4))
        for q in range(TT):
            ins = pe.matmul(ps[:, 6, q:q + 1], rstd[:, P * q:P * q + P], ident[:, 0:1], start=True, stop=True)
        ins.then_inc(turned, 1)
        for c in range(4):
            pe.wait_ge(*take(w_split, "pe"))
            for q in range(TT):
                pe.wait_ge(*take(bank_free, "pe"))
                value_product(ps[:, q, 0:256], parts_of(c % 2, DT, 256), hm, slice(P * q, P * q + P), begin=q == 0)\
                    .then_inc(tile_done, 1)
        pe.wait_ge(*ahead(bank_free, "pe", 4))
        with loop(pe, "pe", 4) as i:
            for c in range(4):
                pe.wait_ge(*take(rot_taken, "pe"))
                pe.matmul(ps[:, c:c + 1, :], rot, qk[:, bass.ds(i * 4 + c, 1), :], start=True, stop=True)\
                    .then_inc(rot_ready, 1)
        end_stage("pe")

    def qkv_act():
        for c in range(8):
            split_hi(1 - c % 2)
        skip(tile_done, "act", 16)
        act.wait_ge(*take(v_taken, "act"))
        for c in range(4):
            split_hi(1 - c % 2)
            for q in range(TT):
                act.wait_ge(*take(tile_done, "act"))
                act.activation(v_tok[:, q, 256 * c:256 * c + 256], ps[:, q, 0:256], ACT.Identity, scale=col[:, q:q + 1])\
                    .then_inc(bank_free, 1)
        end_stage("act")

    def qkv_dve():
        norm_dve(B1["norm_mix"] + DT)
        with loop(dve, "dve", 4) as i:
            for c in range(4):
                dve.wait_ge(*take(tile_done, "dve"))
                dve.tensor_tensor(qk[:, bass.ds(i * 4 + c, 1), :], ps[:, c:c + 1, :], rstd[:, :].unsqueeze(1), ALU.mult)\
                    .then_inc(bank_free, 1)
        dve.wait_ge(*take(turned, "dve"))
        dve.tensor_copy(col[:, 0:TT], ps[:, 6, 0:TT]).then_inc(v_taken, 1)
        skip(tile_done, "dve", 16)
        with loop(dve, "dve", 4) as i:
            for c in range(4):
                t = qk[:, bass.ds(i * 4 + c, 1), :]
                dve.wait_ge(*take(rot_ready, "dve"))
                dve.tensor_tensor(tmp[:, c:c + 1, :], ps[:, c:c + 1, :], cst("sin").unsqueeze(1), ALU.mult)\
                    .then_inc(rot_taken, 1)
                link(dve.tensor_tensor(t, t, cst("cos").unsqueeze(1), ALU.mult))
                dve.wait_ge(*take(rot_taken, "dve"))
                link(dve.tensor_tensor(t, t, tmp[:, c:c + 1, :], ALU.add))
        end_stage("dve")

    TWO_BANKS, ONE_BANK = ((0, 1), (2, 3)), ((4, 4), (5, 5))

    def units_pe(units, sm, ptb):
        for step in range(len(units) + 3):
            unit_pe(units, step, sm, ptb, TWO_BANKS)

    def unit_pe(units, step, sm, ptb, banks):
        n, single = len(units), banks is ONE_BANK

        def scores(u):
            if single:
                pe.wait_ge(*ahead(s_taken, "pe", 2))
                skip(s_taken, "pe", 1)
            else:
                pe.wait_ge(*take(s_taken, "pe"))
            for a, (q, key) in enumerate(zip(u["q"], u["k"])):
                ins = pe.matmul(ps[:, banks[0][step % 2], 0:u["n"]], q, key, start=a == 0, stop=a == len(u["q"]) - 1)
            ins.then_inc(s_ready, 1)

        def transposes(u):
            pe.wait_ge(*take(p_ready, "pe"))
            for j in range(0, u["n"], P):
                w = min(P, u["n"] - j)
                ins = pe.transpose(ps[0:w, banks[1][step % 2], j:j + P], sm[:, (step - 2) % 3, j:j + w], ident)
            ins.then_inc(pt_ready, 1)

        def outputs(u):
            if u["begin"]:
                pe.wait_ge(*take(o_taken, "pe"))
            pe.wait_ge(*take(pt_copied, "pe"))
            js = range(0, u["n"], P)
            for v, o in zip(u["v"], u["o"]):
                for j in js:
                    w = min(P, u["n"] - j)
                    ins = pe.matmul(o, v(j // P), ptb[0:w, (step - 3) % 2, j:j + P], start=u["first"] and j == 0,
                                    stop=u["last"] and j == js[-1])
            if u["end"] is not None:
                ins.then_inc(pv_done, 1)

        if step < n:
            scores(units[step])
        if single and 0 <= step - 3 < n:
            outputs(units[step - 3])
        if 0 <= step - 2 < n:
            transposes(units[step - 2])
        if not single and 0 <= step - 3 < n:
            outputs(units[step - 3])

    def units_act(units, sm, ptb, leave):
        for step in range(len(units) + 4):
            unit_act(units, step, sm, ptb, TWO_BANKS, leave)

    def unit_act(units, step, sm, ptb, banks, leave):
        n = len(units)
        if step < n:
            u, b = units[step], step % 3
            act.wait_ge(*take(s_taken, "act"))
            act.activation(sm[:, b, 0:u["n"]], sm[:, b, 0:u["n"]], ACT.Exp, bias=u["max"], accum_out=u["sum"])\
                .then_inc(e_ready, 1)
        if 0 <= step - 2 < n:
            u, b = units[step - 2], step % 2
            w, n2 = min(P, u["n"]), -(-u["n"] // P) * P
            act.wait_ge(*take(pt_ready, "act"))
            act.activation(ptb[0:w, b, 0:n2], ps[0:w, banks[1][b], 0:n2], ACT.Copy).then_inc(pt_copied, 1)
        if 0 <= step - 4 < n and units[step - 4]["end"] is not None:
            act.wait_ge(*take(pv_done, "act"))
            leave(units[step - 4]["end"])

    def units_dve(units, sm, leave=None):
        for step in range(len(units) + 4):
            unit_dve(units, step, sm, TWO_BANKS, leave)

    def unit_dve(units, step, sm, banks, leave):
        n = len(units)
        if step < n:
            u, b = units[step], step % 3
            dve.wait_ge(*take(s_ready, "dve"))
            s_sb, s_ps = sm[:, b, 0:u["n"]], ps[:, banks[0][step % 2], 0:u["n"]]
            if u["bias"] is None:
                link(dve.tensor_scalar(s_sb, s_ps, u["scale"], None, ALU.mult))
            else:
                link(dve.scalar_tensor_tensor(s_sb, s_ps, u["scale"], u["bias"], ALU.mult, ALU.add))
            dve.tensor_reduce(u["max"], s_sb, AX, ALU.max, negate=True).then_inc(s_taken, 1)
        if 0 <= step - 1 < n:
            u, b = units[step - 1], (step - 1) % 3
            dve.wait_ge(*take(e_ready, "dve"))
            link(dve.reciprocal(u["inv"], u["sum"]))
            if u["gate"] is not None:
                link(dve.tensor_tensor(u["inv"], u["inv"], u["gate"], ALU.mult))
            dve.tensor_scalar(sm[:, b, 0:u["n"]], sm[:, b, 0:u["n"]], u["inv"], None, ALU.mult).then_inc(p_ready, 1)
        if 0 <= step - 4 < n and units[step - 4]["end"] is not None and leave:
            leave(units[step - 4]["end"])

    GROUP_OF = [0] * 6 + [1] * 5 + [2] * 5
    maxes, sums, invs = col[:, 0:64], col[:, 64:128], col[:, 128:130]

    def mask_of(g, a, n):
        return masks[:, (0, 2 * P, 2 * P + S)[g] + a:(0, 2 * P, 2 * P + S)[g] + a + n]

    def pattern_units():
        units = []
        for h in range(16):
            t, e, g = h // 2, h % 2, GROUP_OF[h]
            f = slice(HD * e, HD * e + HD)
            for q in range(TT):
                k0 = max(q - 1, 0) if g == 0 else 0
                n = (q + 1 - k0) * P
                c = h * TT + q
                units.append(dict(
                    q=[qk[f, t, P * q:P * q + P]], k=[qk[f, DT + t, P * k0:P * k0 + n]], gate=None,
                    n=n, bias=mask_of(0, 2 * P - n, n) if g == 0 else mask_of(g, S - n, n), scale=HD ** -0.5,
                    max=maxes[:, c:c + 1], sum=sums[:, c:c + 1], inv=invs[:, q % 2:q % 2 + 1],
                    v=[lambda j, k0=k0, h=h: v_tok[:, k0 + j, HD * h:HD * h + HD]],
                    o=[ps[f, 4 + t % 4, P * q:P * q + P]], first=True, last=True,
                    begin=t >= 4 and e == 0 and q == 0, end=t if e == 1 and q == TT - 1 else None))
        return units

    def pattern_pe():
        units_pe(pattern_units(), sm, ptb)
        pe.wait_ge(*take(o_taken, "pe", 4))
        for g in range(3):
            for q in range(TT):
                pe.wait_ge(*take(alpha_ready, "pe"))
                ins = pe.matmul(ps[:, g, P * q:P * q + P], ones, alpha_dg[:, g, q, :], start=True, stop=True)
        ins.then_inc(alpha_sum, 1)
        pe.wait_ge(*take(xlo_ready, "pe", DT))
        om = moving(o_hi, o_lo)
        for c in range(4):
            pe_tiles(om, DT, 256, c % 2, (4 + 2 * c % 4, 5 + 2 * c % 4), free=x_ready)

    lse, top, total, best, scale3 = (col[:, a:b] for a, b in ((130, 194), (194, 206), (206, 218), (218, 222), (222, 226)))
    HEADS = ((0, 6), (6, 11), (11, 16))

    def by_group(a, g):
        lo, hi = HEADS[g]
        return a[:, lo * TT:hi * TT].rearrange("p (h q) -> p q h", q=TT)

    def pattern_act():
        def leave(t):
            act.activation(o_t[:, t, :], ps[:, 4 + t % 4, :], ACT.Copy).then_inc(o_taken, 1)

        units_act(pattern_units(), sm, ptb, leave)
        act.activation(lse, sums, ACT.Ln).then_inc(a_to_d, 1)
        act.wait_ge(*take(d_to_a, "act"))
        act.activation(lse, lse, ACT.Exp).then_inc(a_to_d, 1)
        act.wait_ge(*take(d_to_a, "act"))
        for g, (lo, hi) in enumerate(HEADS):
            t = total[:, TT * g:TT * g + TT]
            act.activation(t, t, ACT.Ln, scale=1.0 / (hi - lo)).then_inc(a_to_d, 1)
        act.wait_ge(*take(d_to_a, "act"))
        act.activation(total, total, ACT.Exp).then_inc(a_to_d, 1)
        for t in range(DT):
            act.wait_ge(*take(prod_ready, "act"))
            act.activation(o_hi[:, t, :], o_t[:, t, :], ACT.Copy).then_inc(xhi_ready, 1)
        add_to_x_act(B1["norm_ffn"] + DT)

    def pattern_dve():
        units_dve(pattern_units(), sm)
        dve.wait_ge(*take(a_to_d, "dve"))
        link(dve.tensor_tensor(lse, lse, maxes, ALU.subtract))
        for g, (lo, hi) in enumerate(HEADS):
            t = top[:, TT * g:TT * g + TT]
            link(dve.tensor_reduce(t, by_group(lse, g), AX, ALU.max))
            ins = dve.tensor_tensor(by_group(lse, g), by_group(lse, g),
                                    t.unsqueeze(2).to_broadcast([P, TT, hi - lo]), ALU.subtract)
            if g < 2:
                link(ins)
        ins.then_inc(d_to_a, 1)
        dve.wait_ge(*take(a_to_d, "dve"))
        for g in range(3):
            ins = dve.tensor_reduce(total[:, TT * g:TT * g + TT], by_group(lse, g), AX, ALU.add)
        ins.then_inc(d_to_a, 1)
        dve.wait_ge(*take(a_to_d, "dve", 3))
        link(dve.tensor_tensor(total, total, top, ALU.add))
        over = total.rearrange("p (g q) -> p q g", q=TT)
        link(dve.tensor_reduce(best, over, AX, ALU.max))
        dve.tensor_tensor(over, over, best.unsqueeze(2).to_broadcast([P, TT, 3]), ALU.subtract).then_inc(d_to_a, 1)
        dve.wait_ge(*take(a_to_d, "dve"))
        link(dve.tensor_reduce(best, over, AX, ALU.add))
        link(dve.reciprocal(scale3, best))
        link(dve.tensor_scalar(scale3, scale3, 3.0, None, ALU.mult))
        link(dve.tensor_tensor(over, over, scale3.unsqueeze(2).to_broadcast([P, TT, 3]), ALU.mult))
        for g in range(3):
            for q in range(TT):
                dve.tensor_scalar(alpha_dg[:, g, q, :], ident, total[:, TT * g + q:TT * g + q + 1], None, ALU.mult)\
                    .then_inc(alpha_ready, 1)
        dve.wait_ge(*take(alpha_sum, "dve"))
        for t in range(DT):
            for f, g in (((slice(0, P), 0),) if t < 3 else ((slice(0, P), 1),) if t < 5 else
                         ((slice(0, HD), 1), (slice(HD, P), 2)) if t == 5 else ((slice(0, P), 2),)):
                ins = dve.tensor_tensor(o_t[f, t, :], o_t[f, t, :], ps[f, g, :], ALU.mult)
            ins.then_inc(prod_ready, 1)
            dve.wait_ge(*take(xhi_ready, "dve"))
            dve.tensor_tensor(o_lo[:, t, :], o_t[:, t, :], o_hi[:, t, :].bitcast(F32), ALU.subtract).then_inc(xlo_ready, 1)
        add_to_x_dve(4)

    def pattern_sp():
        for c in range(4):
            load_cols(A["attn_w_out"][0], 256 * c, c % 2)

    def square_act(t):
        act.wait_ge(*take(x_ready, "act"))
        act.activation(sq[:, t, :], x[:, t, :], ACT.Square).then_inc(sq_ready, 1)

    def final_pe():
        sums_pe()
        end_stage("pe")

    def final_dve():
        skip(x_ready, "dve", DT)
        factor_dve()
        for t in range(DT):
            g = B1["norm_final"] + t
            dve.scalar_tensor_tensor(x[:, t, :], x[:, t, :], par[:, g:g + 1], rstd[:, :], ALU.mult, ALU.mult).then_inc(x_ready, 1)
        end_stage("dve")

    MIX_PRE, MIX_POST, XA_PRE, LN_MEM, XA_POST, MLP_PRE, MLP_POST = range(0, 56, 8)
    RET_G, MU, W0, A0, K_K, K_A, R_K, LN_G, LN_B, CONV_W, CMP_PE = 56, 58, 65, 67, 69, 71, 73, 75, 77, 79, 96

    def par_of(col0, t=0):
        return par[:, col0 + t:col0 + t + 1]

    def layer_of(name, l, *at):
        return A[name][(bass.ds(l, 1), *at)].rearrange("o r c -> (o r) c")

    def setup_sp():
        sp.wait_ge(*take(rel_marked, "sp"))
        sp.dma_start(mem_rows[:, :, :], A["mem_2"][0].rearrange("(t p) d -> p t d", p=P)).then_inc(mem_landed, 16)
        sp.dma_start(onehot[0:33, :], A["onehot"]).then_inc(mem_landed, 16)
        sp.dma_start(rel[0:32, :], A["rel_bias_2"]).then_inc(mem_landed, 16)
        sp.wait_ge(*take(vec_ready, "sp"))
        sp.dma_start(scratch["vec"], vec[0:4, :]).then_inc(vec_stored, 16)
        sp.wait_ge(*take(vec_stored, "sp", 16))
        shifted = bass.AP(scratch["vec"].tensor, 0, [[1, P], [N_DIST, 4], [1, 2 * S]])
        sp.dma_start(hankel[:, :, :], shifted).then_inc(hankel_in, 16)
        sp.wait_ge(*take(mn_ready, "sp"))
        sp.dma_start(scratch["mem"], mem_t[:, :, :]).then_inc(mem_stored, 16)

    def setup_pe():
        pe.wait_ge(*take(mem_landed, "pe", 48))
        for f in range(DT):
            for q in range(2):
                at = MEM * (f % 2) + P * q
                ins = pe.transpose(ps[:, f // 2, at:at + P], mem_rows[:, q, P * f:P * f + P], ident)
        ins.then_inc(turned, 1)
        for a in range(3):
            ins = pe.matmul(ps[0:4, 4 + a, 0:384], rel[0:33, :], onehot[0:33, 384 * a:384 * a + 384], start=True, stop=True)
        ins.then_inc(pe_dve, 1)
        pe.wait_ge(*take(act_pe, "pe"))
        for f in range(DT):
            ins = pe.matmul(ps[:, 7, 0:MEM], ones, mem_sq[:, f, :], start=f == 0, stop=f == DT - 1)
        ins.then_inc(ss_ready, 1)
        pe.wait_ge(*take(hankel_in, "pe", 16))
        pe.wait_ge(*take(mn_ready, "pe"))
        for h in range(4):
            for a in range(2):
                ins = pe.matmul(ps[:, 2 * h + a, :], flip, hankel[:, h, S * a:S * a + S], start=True, stop=True)
        ins.then_inc(pe_dve, 1)
        end_stage("pe")

    def setup_act():
        act.wait_ge(*take(d_to_a, "act"))
        act.activation(mem_sq[:, :, :], mem_t[:, :, :], ACT.Square).then_inc(act_pe, 1)
        factor_act(MEM)
        skip(mem_landed, "act", 48)
        skip(par_done, "act", 1)
        act.wait_ge(*take(mem_stored, "act", 16))
        end_stage("act")

    def setup_dve():
        dve.memset(rel[0:33, :], NEG).then_inc(rel_marked, 1)
        dve.wait_ge(*take(turned, "dve"))
        dve.tensor_copy(mem_t[:, :, :].rearrange("p (b f) m -> p b (f m)", f=2), ps[:, 0:4, :]).then_inc(d_to_a, 1)
        dve.wait_ge(*take(pe_dve, "dve"))
        dve.tensor_copy(vec[0:4, :].rearrange("p (a c) -> p a c", c=384), ps[0:4, 4:7, 0:384]).then_inc(vec_ready, 1)
        factor_dve(MEM)
        dve.tensor_tensor(mem_t[:, :, :], mem_t[:, :, :], rstd[:, 0:MEM].unsqueeze(1).to_broadcast([P, DT, MEM]), ALU.mult)\
            .then_inc(mn_ready, 1)
        dve.wait_ge(*take(pe_dve, "dve"))
        dve.tensor_copy(bias[:, :, :], ps[:, 0:8:2, :])
        for h in range(4):
            wide = ps[:, 2 * h:2 * h + 2, :].rearrange("p a s -> p (a s)")
            for q in range(TT):
                at = 3 * P + NSA_LEN - 1 - P * q
                dve.tensor_copy(cbias[:, h, q, 0:N_CMP], wide[:, at:at + NSA_STRIDE * (N_CMP - 1) + 1:NSA_STRIDE])
        end_stage("dve")

    def params_sp(l):
        wait(sp, take(par_done, "sp"))
        at = 0
        for name, n in (("ln_mix_pre_2", 8), ("ln_mix_post_2", 8), ("ln_xa_pre_2", 8), ("ln_mem_2", 8), ("ln_xa_post_2", 8),
                        ("ln_mlp_pre_2", 8), ("ln_mlp_post_2", 8), ("ret_norm_g_2", 2), ("rwkv_mu_2", 7), ("rwkv_w0_2", 2),
                        ("rwkv_a0_2", 2), ("rwkv_k_k_2", 2), ("rwkv_k_a_2", 2), ("rwkv_r_k_2", 2), ("rwkv_ln_g_2", 2),
                        ("rwkv_ln_b_2", 2)):
            sp.dma_start(rows[at:at + n, :], A[name][bass.ds(l, 1)].rearrange("o (t c) -> (o t) c", c=P))\
                .then_inc(rows_in, 16)
            at += n
        sp.dma_start(rows[CONV_W:CONV_W + 6, :], A["conv_w_2"][bass.ds(l, 1)].rearrange("o j (t c) -> (o j t) c", c=P))\
            .then_inc(rows_in, 16)
        for a in range(2):
            sp.dma_start(rows[CMP_PE:P, HD * a:HD * a + HD], layer_of("nsa_cmp_pe_2", l)).then_inc(rows_in, 16)

    def params_pe():
        pe.wait_ge(*take(rows_in, "pe", 19 * 16))
        pe.transpose(ps[:, 0, 0:P], rows[:, :], ident).then_inc(turned, 1)

    def params_dve():
        dve.wait_ge(*take(turned, "dve"))
        dve.tensor_copy(par[:, :], ps[:, 0, 0:P]).then_inc(par_done, 1)

    def mixer_in_sp(l):
        w = layer_of("w_in_2", l)
        with loop(sp, "sp", 5) as i:
            for c in range(2):
                load_cols(w, i * 512 + (IN_RET + 256 * c), c)
        load_cols(w, IN_RET + 2560, 0, P)
        load_cols(w, IN_NSA, 1)
        load_cols(w, IN_NSA + 256, 0)
        load_cols(w, IN_NSA + 512, 1, IN_RET - 512)

    def mixer_in_pe():
        norm_pe()
        hm = moving(h_hi, h_lo)
        with loop(pe, "pe", 5):
            for c in range(2):
                pe_tiles(hm, DT, 256, c, (2 * c, 2 * c + 1))
        pe_tiles(hm, DT, P, 0, (0,))
        pe_tiles(hm, DT, 256, 1, (1, 2))
        pe_tiles(hm, DT, 256, 0, (3, 0))
        pe_tiles(hm, DT, IN_RET - 512, 1, (1, 2))
        end_stage("pe")

    def mixer_in_act(l):
        split_hi(0)
        for t in range(DT):
            square_act(t)
        act.wait_ge(*take(par_done, "act"))
        for t in range(DT):
            act.activation(h_hi[:, t, :], x[:, t, :], ACT.Identity, scale=par_of(MIX_PRE, t)).then_inc(xhi_ready, 1)
        factor_act()
        for a in range(2):
            act.dma_start(cmp_w[HD * a:HD * a + HD, :, :], A["nsa_cmp_w_2"][bass.ds(l, 1), a].rearrange("o l d e -> d (o l) e"))\
                .then_inc(cmp_landed, 16)
        with loop(act, "act", 7):
            for c in range(2):
                split_hi(1 - c)
        skip(tile_done, "act", 27)
        end_stage("act")

    def mixer_in_dve():
        add_squares_dve()
        norm_dve(MIX_PRE)
        with loop(dve, "dve", 5) as i:
            for c in range(4):
                dve.wait_ge(*take(tile_done, "dve"))
                dve.tensor_tensor(z[:, bass.ds(i * 4 + c, 1), :], ps[:, c:c + 1, :], rstd[:, :].unsqueeze(1), ALU.mult)\
                    .then_inc(bank_free, 1)
        for t in range(20, 27):
            r = slice(0, P if t < 26 else 12)
            dve.wait_ge(*take(tile_done, "dve"))
            dve.tensor_tensor(z[r, t, :], ps[r, t % 4, :], rstd[r, :], ALU.mult).then_inc(bank_free, 1)
        end_stage("dve")

    def branch_act(m, src):
        for t in range(2):
            act.wait_ge(*take(prod_ready, "act"))
            act.activation(br_hi[m][:, t, :], src[:, t, :], ACT.Copy).then_inc(xhi_ready, 1)

    def branch_dve(m, src):
        for t in range(2):
            dve.wait_ge(*take(xhi_ready, "dve"))
            dve.tensor_tensor(br_lo[m][:, t, :], src[:, t, :], br_hi[m][:, t, :].bitcast(F32), ALU.subtract)\
                .then_inc(xlo_ready, 1)

    def conv_act():
        branch_act(3, y_conv)
        end_stage("act")

    def conv_dve():
        link(dve.memset(u_conv[:, :, 0:2], 0.0))
        link(dve.tensor_tensor(u_conv[:, :, 2:], z[:, CONV + 2:CONV + 4, :], z[:, CONV + 4:CONV + 6, :], ALU.mult))
        for t in range(2):
            y = y_conv[:, t, :]
            link(dve.tensor_scalar(y, u_conv[:, t, 0:S], par_of(CONV_W, t), None, ALU.mult))
            for j in (1, 2):
                link(dve.scalar_tensor_tensor(y, u_conv[:, t, j:j + S], par_of(CONV_W + 2 * j, t), y, ALU.mult, ALU.add))
            dve.tensor_tensor(y, y, z[:, CONV + t, :], ALU.mult).then_inc(prod_ready, 1)
        branch_dve(3, y_conv)
        end_stage("dve")

    def head_norm_pe(o, v):
        for src, bank in ((o, 0), (v, 2)):
            pe.wait_ge(*take(act_pe, "pe"))
            for t in range(2):
                ins = pe.matmul(ps[:, bank + t, :], heads1, src[:, t, :], start=True, stop=True)
            ins.then_inc(pe_dve, 1)

    def head_norm_act(c, v):
        act.wait_ge(*take(d_to_a, "act"))
        act.activation(v, c, ACT.Square).then_inc(act_pe, 1)
        act.wait_ge(*take(d_to_a, "act"))
        act.activation(v, v, ACT.Sqrt).then_inc(a_to_d, 1)

    def head_norm_dve(o, c, v, eps):
        dve.wait_ge(*take(pe_dve, "dve"))
        dve.scalar_tensor_tensor(c, ps[:, 0:2, :], -1.0 / HD, o, ALU.mult, ALU.add).then_inc(d_to_a, 1)
        dve.wait_ge(*take(pe_dve, "dve"))
        link(dve.tensor_scalar(v, ps[:, 2:4, :], 1.0 / HD, eps, ALU.mult, ALU.add))
        dve.reciprocal(v, v).then_inc(d_to_a, 1)
        dve.wait_ge(*take(a_to_d, "dve"))
        link(dve.tensor_tensor(c, c, v, ALU.mult))

    rq, rk, rv, rg = (z[:, RET + 2 * a:RET + 2 * a + 2, :] for a in range(4))
    RET_UNITS = [(h, j) for h in range(4) for j in range(TT)]

    def retention_pe():
        for t in range(4):
            pe.matmul(ps[:, t, :], rot, z[:, RET + t, :], start=True, stop=True).then_inc(rot_ready, 1)
        for t in range(2):
            for q in range(TT):
                ins = pe.transpose(ps[:, 4 + t, P * q:P * q + P], rv[:, t, P * q:P * q + P], ident)
            ins.then_inc(v_turned, 1)
        pe.wait_ge(*take(staged, "pe"))
        pe.wait_ge(*take(act_pe, "pe", 2))

        def outputs(u, more):
            h, j = RET_UNITS[u]
            f = slice(HD * (h % 2), HD * (h % 2) + HD)
            pe.wait_ge(*ahead(s_taken, "pe", more))
            return pe.matmul(ps[f, 6 + h // 2, P * j:S], v_ret[:, j, HD * h:HD * h + HD], tmp[:, u % 2, 0:S - P * j],
                             start=j == 0, stop=j == TT - 1)

        for u, (h, j) in enumerate(RET_UNITS):
            f = slice(HD * (h % 2), HD * (h % 2) + HD)
            pe.wait_ge(*take(s_taken, "pe"))
            pe.matmul(ps[:, u % 2, 0:S - P * j], rk[f, h // 2, P * j:P * j + P], rq[f, h // 2, P * j:S], start=True, stop=True)\
                .then_inc(s_ready, 1)
            if u:
                outputs(u - 1, 1)
        outputs(len(RET_UNITS) - 1, 2).then_inc(pe_act, 1)
        head_norm_pe(rq, rv)
        end_stage("pe")

    def retention_act(l):
        for at, name in ((0, "rwkv_w2_2"), (32, "rwkv_a2_2"), (64, "rwkv_g2_2")):
            n = 32 if at < 64 else 64
            act.dma_start(lora[at:at + n, :], layer_of(name, l)).then_inc(lora_landed, 16)
        act.activation(rg, rg, ACT.Silu)
        skip(s_taken, "act", len(RET_UNITS))
        for t in range(2):
            act.wait_ge(*take(v_turned, "act"))
            act.activation(v_ret[:, :, P * t:P * t + P], ps[:, 4 + t, :].rearrange("p (q c) -> p q c", c=P), ACT.Copy)\
                .then_inc(act_pe, 1)
        act.wait_ge(*take(pe_act, "act"))
        act.activation(rq, ps[:, 6:8, :], ACT.Copy).then_inc(act_pe, 1)
        head_norm_act(rk, rv)
        branch_act(1, rk)
        end_stage("act")

    def retention_dve():
        dve.wait_ge(*take(rot_ready, "dve", 4))
        qk4, t4 = z[:, RET:RET + 4, :], tmp[:, 0:4, :]
        link(dve.tensor_tensor(t4, ps[:, 0:4, :], cst("sin").unsqueeze(1).to_broadcast([P, 4, S]), ALU.mult))
        link(dve.tensor_tensor(qk4, qk4, cst("cos").unsqueeze(1).to_broadcast([P, 4, S]), ALU.mult))
        link(dve.tensor_tensor(qk4, qk4, t4, ALU.add))
        dve.sem_inc(staged, 1)
        for u, (h, j) in enumerate(RET_UNITS):
            n = S - P * j
            dve.wait_ge(*take(s_ready, "dve"))
            dve.scalar_tensor_tensor(tmp[:, u % 2, 0:n], ps[:, u % 2, 0:n], HD ** -0.5, cst("decay", S * h, S * h + n),
                                     ALU.mult, ALU.mult).then_inc(s_taken, 1)
        head_norm_dve(rq, rk, rv, 1e-5)
        for t in range(2):
            dve.scalar_tensor_tensor(rk[:, t, :], rk[:, t, :], par_of(RET_G, t), rg[:, t, :], ALU.mult, ALU.mult)\
                .then_inc(prod_ready, 1)
        branch_dve(1, rk)
        end_stage("dve")

    def nsa_units():
        units = []
        for h in range(4):
            t, e = h // 2, h % 2
            f = slice(HD * e, HD * e + HD)
            for q in range(TT):
                for b in range(3):
                    n = N_CMP if b == 0 else P * (q + 1)
                    if b == 0:
                        key, bias_ = kc_dup[f, 0:n], cbias[:, h, q, 0:n]
                        v = lambda j: vc_tok[0:N_CMP, HD:P]
                    else:
                        key, bias_ = k_dup[f, b - 1, 0:n], bias[:, h, S - n:S]
                        v = lambda j, b=b: v_nsa[:, b - 1, j, :]
                    u, at = len(units), 12 * q + 3 * h + b
                    units.append(dict(q=[z[f, NSA + t, P * q:P * q + P]], k=[key], n=n, bias=bias_, scale=HD ** -0.5,
                                      max=col[:, u:u + 1], sum=col[:, 48 + u:49 + u], inv=col[:, 96 + u % 2:97 + u % 2],
                                      gate=gate_tok[:, at:at + 1], v=[v], o=[ps[f, 6 + t, P * q:P * q + P]],
                                      first=b == 0, last=b == 2, begin=False,
                                      end=t if (e, q, b) == (1, TT - 1, 2) else None))
        return units

    def nsa_pe():
        pe.wait_ge(*take(act_pe, "pe"))
        for b in range(2):
            for q in range(TT):
                pe.transpose(ps[:, 2 + b, P * q:P * q + P], z[:, NSA + 3 + b, P * q:P * q + P], ident)
        for q in range(TT):
            ins = pe.transpose(ps[:, 1, 12 * q:12 * q + 12], z[0:12, NSA + 5, P * q:P * q + P], ident[0:12, 0:12])
        ins.then_inc(pe_dve, 1)
        pe.wait_ge(*take(cmp_landed, "pe", 32))
        pe.wait_ge(*take(dve_pe, "pe"))
        settle(pe)
        for a in range(2):
            f = slice(HD * a, HD * a + HD)
            for j in range(NSA_LEN):
                ins = pe.matmul(ps[f, 0, 0:N_CMP], cmp_w[f, j, :], cmp_in_t[f, j, :], start=j == 0, stop=j == NSA_LEN - 1)
        ins.then_inc(pe_dve, 1)
        pe.wait_ge(*take(dve_pe, "pe"))
        pe.transpose(ps[0:N_CMP, 4, 0:P], kc_raw[:, 0:N_CMP], ident).then_inc(pe_dve, 1)
        pe.wait_ge(*take(staged, "pe"))

    def nsa_step_pe(step):
        unit_pe(nsa_units(), step, sm2, pt2, ONE_BANK)

    def nsa_step_act(step):
        def leave(t):
            act.activation(br_hi[0][:, t, :], ps[:, 6 + t, :], ACT.Copy).then_inc(xhi_ready, 1)

        unit_act(nsa_units(), step, sm2, pt2, ONE_BANK, leave)

    def nsa_step_dve(step):
        def leave(t):
            dve.wait_ge(*take(xhi_ready, "dve"))
            dve.tensor_tensor(br_lo[0][:, t, :], ps[:, 6 + t, :], br_hi[0][:, t, :].bitcast(F32), ALU.subtract)\
                .then_inc(o_taken, 1)

        unit_dve(nsa_units(), step, sm2, ONE_BANK, leave)

    NSA_UNITS, PER_PAIR = 4 * TT * 3, 12

    def nsa_act():
        g = z[0:12, NSA + 5, :]
        act.activation(g, g, ACT.Sigmoid).then_inc(act_pe, 1)

    def nsa_dve():
        strided = z[:, NSA + 2, :].rearrange("p (n b) -> p b n", b=NSA_STRIDE)
        for a in range(2):
            pe_cols = par[:, CMP_PE + NSA_STRIDE * a:CMP_PE + NSA_STRIDE * a + NSA_STRIDE]
            ins = dve.tensor_tensor(cmp_in_t[:, NSA_STRIDE * a:NSA_STRIDE * a + NSA_STRIDE, :], strided[:, :, a:a + N_CMP],
                                    pe_cols.unsqueeze(2).to_broadcast([P, NSA_STRIDE, N_CMP]), ALU.add)
        ins.then_inc(dve_pe, 1)
        for b in range(2):
            for e in range(2):
                dve.tensor_copy(k_dup[HD * e:HD * e + HD, b, :], z[0:HD, NSA + 3 + b, :])
        dve.wait_ge(*take(pe_dve, "dve"))
        link(dve.tensor_copy(gate_tok[:, :], ps[:, 1, 0:12 * TT]))
        link(dve.tensor_scalar(gate_tok[:, 0:12:3], gate_tok[:, 0:12:3], cst("late"), None, ALU.mult))
        dve.tensor_copy(v_nsa[:, :, :, :], ps[:, 2:4, :].rearrange("p b (q c) -> p b q c", c=P)[:, :, :, HD:P])
        dve.wait_ge(*take(pe_dve, "dve"))
        for e in range(2):
            dve.tensor_copy(kc_dup[HD * e:HD * e + HD, 0:N_CMP], ps[0:HD, 0, 0:N_CMP])
        dve.tensor_copy(kc_raw[:, 0:N_CMP], ps[:, 0, 0:N_CMP]).then_inc(dve_pe, 1)
        dve.wait_ge(*take(pe_dve, "dve"))
        dve.tensor_copy(vc_tok[0:N_CMP, :], ps[0:N_CMP, 4, 0:P]).then_inc(staged, 1)

    wr, wk, wv = (z[:, RWK + 2 * a:RWK + 2 * a + 2, :] for a in range(3))
    misc = z[:, RWK + 6, :]
    RT, AT, KH, BH, KBAR, BBAR, VV = range(7)
    ROW = [slice(HD * e, HD * e + HD) for e in range(2)]

    def wide(a):
        return a.unsqueeze(1).to_broadcast([P, 4, P])

    def rwkv_pe():
        pe.wait_ge(*take(act_pe, "pe", 2))
        pe.wait_ge(*take(lora_landed, "pe", 48))
        for r, bank in ((slice(0, 32), 0), (slice(32, 64), 2), (slice(64, P), 4)):
            for t in range(2):
                pe.matmul(ps[:, bank + t, :], lora[r, P * t:P * t + P], misc[r, :], start=True, stop=True)
        for t in range(2):
            ins = pe.matmul(ps[:, 6 + t, :], heads1, bb[:, t, :], start=True, stop=True)
        ins.then_inc(pe_act, 1)
        for j in range(TT):
            pair_pe(lambda n: nsa_step_pe(PER_PAIR * j + n))
        for step in range(NSA_UNITS, NSA_UNITS + 3):
            nsa_step_pe(step)
        pe.wait_ge(*take(o_taken, "pe", 2))
        pe.wait_ge(*take(dve_pe, "pe"))
        for t in range(2):
            ins = pe.matmul(ps[:, 4 + t, :], heads1, wr[:, t, :], start=True, stop=True)
        ins.then_inc(pe_dve, 1)
        head_norm_pe(y_rw, cw)
        end_stage("pe")

    HEADS_RW = [(2 * t + e, t, ROW[e], 2 * e + t, slice(HD * (2 * t + e), HD * (2 * t + e) + HD)) for e in range(2) for t in range(2)]

    def pair_pe(fill):
        def inner(bank, a, b):
            for h, t, f, c, _ in HEADS_RW:
                ins = pe.matmul(ps[:, bank + c // 2, P * t:P * t + P], pb[f, a, t, :], pb[f, b, t, :], start=True, stop=True)
            return ins

        def place(bank, c):
            return ps[:, bank, P * c:P * c + P]

        pe.wait_ge(*take(dve_pe, "pe"))
        inner(0, BH, AT).then_inc(pe_dve, 1)
        pe.wait_ge(*take(dve_pe, "pe"))
        inner(2, KH, AT).then_inc(pe_dve, 1)
        fill(0)
        pe.wait_ge(*take(dve_pe, "pe"))
        inner(0, BH, RT).then_inc(pe_dve, 1)
        pe.wait_ge(*take(dve_pe, "pe"))
        inner(2, KH, RT).then_inc(pe_dve, 1)
        fill(1)
        pe.wait_ge(*take(dve_pe, "pe"))
        pe.wait_ge(*take(act_pe, "pe"))
        for o, src in enumerate((AT, KBAR, BBAR, VV)):
            for t in range(2):
                at = 2 * P * (o % 2) + P * t
                ins = pe.transpose(ps[:, o // 2, at:at + P], pb[:, src, t, :], ident)
        ins.then_inc(pe_act, 1)
        pe.wait_ge(*take(dve_pe, "pe"))
        for h, t, f, c, d in HEADS_RW:
            ins = pe.matmul(place(2, c), m_qm[:, c, :], ident, start=True, stop=True)
        ins.then_inc(pe_dve, 1)
        fill(2)
        pe.wait_ge(*take(act_pe, "pe"))
        for h, t, f, c, d in HEADS_RW:
            ins = pe.matmul(ps[:, 3, d], m_ak[:, c, :], tok[:, 3, d], start=True, stop=True)
        ins.then_inc(pe_act, 1)
        for level in range(1, 6):
            pe.wait_ge(*take(dve_pe, "pe"))
            for h, t, f, c, d in HEADS_RW:
                ins = pe.matmul(place(2, c), m_qm[:, c, :], m_t[:, c, :], start=True, stop=True)
            ins.then_inc(pe_dve, 1)
            if level < 4:
                fill(1 + 2 * level)
            pe.wait_ge(*take(dve_pe, "pe"))
            if level < 5:
                for h, t, f, c, d in HEADS_RW:
                    pe.matmul(place(0, c), m_r[:, c, :], m_y[:, c, :], start=True, stop=True)
            for h, t, f, c, d in HEADS_RW:
                ins = pe.matmul(place(1, c), m_y[:, c, :], m_r[:, c, :], start=True, stop=True)
            ins.then_inc(pe_dve, 1)
            if level < 4:
                fill(2 + 2 * level)
            elif level == 4:
                fill(9)
        pe.wait_ge(*take(dve_pe, "pe"))
        for h, t, f, c, d in HEADS_RW:
            pe.matmul(ps[f, 1, P * t:P * t + P], tok[:, 0, d], m_r[:, c, :], start=True, stop=True)
        pe.wait_ge(*take(act_pe, "pe"))
        for h, t, f, c, d in HEADS_RW:
            ins = pe.matmul(ps[:, 3, d], m_r[:, c, :], g1[:, d], start=True, stop=True)
        ins.then_inc(pe_act, 1)
        pe.wait_ge(*take(act_pe, "pe"))
        y_bank = (1, 3)
        for n in range(2):
            r = ROW[n]
            for t in range(2):
                ins = pe.matmul(ps[:, 2, P * t:P * t + P], w_t[:, t, :], state[n][:, t, :], start=True, stop=True)
            ins.then_inc(pe_dve, 1)
            fill(10 + n)
            if n == 0:
                for h, t, f, c, d in HEADS_RW:
                    pe.matmul(ps[f, y_bank[t], 0:P], tok[:, 3, d], m_rk[:, c, :], start=True, stop=False)
            for t in range(2):
                pe.matmul(ps[:, y_bank[t], r], state[n][:, t, :], pb[:, RT, t, r], start=False, stop=False)
            pe.wait_ge(*take(dve_pe, "pe"))
            for t in range(2):
                o, both = ps[:, 0, P * t:P * t + P], slice(P * t, P * t + P)
                pe.matmul(o, tok[r, 1, both], tok[r, 3, both], start=True, stop=False)
                ins = pe.matmul(o, tok[r, 2, both], u_rw[r, both], start=False, stop=True)
            ins.then_inc(pe_dve, 1)
            if n == 1:
                for h, t, f, c, d in HEADS_RW:
                    ins = pe.matmul(ps[f, y_bank[t], 0:P], u_rw[:, d], m_rb[:, c, :], start=False, stop=True)
                ins.then_inc(pe_act, 1)
            pe.wait_ge(*take(dve_pe, "pe"))
        pe.wait_ge(*take(act_pe, "pe"))

    def rwkv_act():
        act.wait_ge(*take(d_to_a, "act"))
        act.activation(misc[0:32, :], misc[0:32, :], ACT.Tanh)
        act.activation(misc[HD:P, :], misc[HD:P, :], ACT.Sigmoid).then_inc(act_pe, 1)
        act.wait_ge(*take(d_to_a, "act"))
        act.activation(bb, kk, ACT.Square).then_inc(act_pe, 1)
        act.wait_ge(*take(pe_act, "act"))
        act.activation(bb, ps[:, 6:8, :], ACT.Sqrt).then_inc(a_to_d, 1)
        for t in range(2):
            act.activation(sw[:, t, :], ps[:, t, :], ACT.Sigmoid, bias=par_of(W0, t))
            act.activation(aa[:, t, :], ps[:, 2 + t, :], ACT.Sigmoid, bias=par_of(A0, t))
        act.activation(g_rw[:, :, :], ps[:, 4:6, :], ACT.Copy).then_inc(a_to_d, 1)
        for j in range(TT):
            pair_act(slice(P * j, P * j + P), lambda n: nsa_step_act(PER_PAIR * j + n))
        for step in range(NSA_UNITS, NSA_UNITS + 4):
            nsa_step_act(step)
        act.drain().then_inc(act_pe, 1)
        head_norm_act(sw[:, :, :], cw[:, :, :])
        branch_act(2, sw)
        end_stage("act")

    def pair_act(J, fill):
        act.wait_ge(*take(d_to_a, "act"))
        act.activation(e_any[:, :, :], e_any[:, :, :], ACT.Exp, scale=-DECAY)
        act.activation(pb[:, BBAR], cw[:, :, J], ACT.Exp, scale=DECAY).then_inc(a_to_d, 1)
        act.activation(e_in[:, :, :], cw[:, :, J], ACT.Exp, scale=-DECAY).then_inc(a_to_d, 1)
        act.activation(pb[:, VV], wv[:, :, J], ACT.Copy).then_inc(act_pe, 1)
        fill(0)
        fill(1)
        act.wait_ge(*take(pe_act, "act"))
        act.activation(tok[:, :, :].rearrange("p (b o) c -> p b (o c)", o=2), ps[:, 0:2, :], ACT.Copy).then_inc(act_pe, 1)
        fill(2)
        act.wait_ge(*take(pe_act, "act"))
        act.activation(g1[:, :], ps[:, 3, 0:2 * P], ACT.Copy).then_inc(act_pe, 1)
        for n in range(3, 10):
            fill(n)
        act.wait_ge(*take(pe_act, "act"))
        act.activation(w_t[:, :, :].rearrange("p t c -> p (t c)"), ps[:, 1, 0:2 * P], ACT.Copy)
        act.activation(u_rw[:, :], ps[:, 3, 0:2 * P], ACT.Copy).then_inc(act_pe, 1)
        fill(10)
        fill(11)
        act.wait_ge(*take(pe_act, "act"))
        act.activation(y_rw[:, :, J], ps[:, 1:4:2, 0:P], ACT.Copy).then_inc(act_pe, 1)

    def rwkv_dve():
        for at, n in ((0, 4), (4, 3)):
            zt, d = z[:, RWK + at:RWK + at + n, :], tmp[:, 0:n, :]
            dve.tensor_tensor(d[:, :, 1:], zt[:, :, 0:S - 1], zt[:, :, 1:], ALU.subtract)
            link(dve.tensor_scalar(d[:, :, 0:1], zt[:, :, 0:1], -1.0, None, ALU.mult))
            for t in range(n):
                ins = dve.scalar_tensor_tensor(zt[:, t, :], d[:, t, :], par_of(MU, at + t), zt[:, t, :], ALU.mult, ALU.add)
            if at == 0:
                link(ins)
        ins.then_inc(d_to_a, 1)
        for t in range(2):
            ins = dve.tensor_scalar(kk[:, t, :], wk[:, t, :], par_of(K_K, t), None, ALU.mult)
        ins.then_inc(d_to_a, 1)
        dve.memset(state[0][:, :, :], 0.0)
        dve.wait_ge(*take(a_to_d, "dve"))
        link(dve.tensor_scalar(bb, bb, 1e-12, None, ALU.max))
        link(dve.reciprocal(bb, bb))
        link(dve.tensor_tensor(kk, kk, bb, ALU.mult))
        dve.wait_ge(*take(a_to_d, "dve"))
        link(dve.tensor_copy(tmp[:, 2, :].rearrange("p (n s) -> p n s", s=HD),
                             cst("chunk").unsqueeze(1).to_broadcast([P, S // HD, HD])))
        for t in range(2):
            link(dve.tensor_tensor_scan(cw[:, t, :], tmp[:, 2, :], sw[:, t, :], 0.0, ALU.mult, ALU.add))
        link(dve.tensor_tensor(bb, kk, aa, ALU.mult))
        for t in range(2):
            link(dve.tensor_scalar(tmp[:, t, :], aa[:, t, :], -1.0, par_of(K_A, t), ALU.add, ALU.mult))
            link(dve.scalar_tensor_tensor(wk[:, t, :], tmp[:, t, :], 1.0, wk[:, t, :], ALU.add, ALU.mult))
        for j in range(TT):
            pair_dve(slice(P * j, P * j + P), lambda n: nsa_step_dve(PER_PAIR * j + n))
        for step in range(NSA_UNITS, NSA_UNITS + 4):
            nsa_step_dve(step)
        for t in range(2):
            ins = dve.scalar_tensor_tensor(wr[:, t, :], wr[:, t, :], par_of(R_K, t), wk[:, t, :], ALU.mult, ALU.mult)
        ins.then_inc(dve_pe, 1)
        dve.wait_ge(*take(pe_dve, "dve"))
        link(dve.tensor_tensor(wv, wv, ps[:, 4:6, :], ALU.mult))
        head_norm_dve(y_rw, sw[:, :, :], cw[:, :, :], 64e-5)
        for t in range(2):
            s = sw[:, t, :]
            link(dve.tensor_scalar(s, s, par_of(LN_G, t), par_of(LN_B, t), ALU.mult, ALU.add))
            link(dve.tensor_tensor(s, s, wv[:, t, :], ALU.add))
            dve.tensor_tensor(s, s, g_rw[:, t, :], ALU.mult).then_inc(prod_ready, 1)
        branch_dve(2, sw)
        end_stage("dve")

    def pair_dve(J, fill):
        dve.tensor_tensor(e_any[:, :, :], cw[:, :, J], sw[:, :, J], ALU.subtract).then_inc(d_to_a, 1)
        dve.wait_ge(*take(a_to_d, "dve"))
        dve.scalar_tensor_tensor(pb[:, AT], kk[:, :, J], -1.0, e_any[:, :, :], ALU.mult, ALU.mult)
        dve.tensor_tensor(pb[:, BH], bb[:, :, J], pb[:, BBAR], ALU.mult).then_inc(dve_pe, 1)
        link(dve.tensor_tensor(pb[:, KH], wk[:, :, J], pb[:, BBAR], ALU.mult))
        dve.wait_ge(*take(a_to_d, "dve"))
        end = e_in[:, :, HD - 1::HD].unsqueeze(3).to_broadcast([P, 2, 2, HD])
        for dst, src in ((KBAR, KH), (BBAR, BH)):
            dve.tensor_tensor(pb[:, dst].rearrange("p t (c s) -> p t c s", s=HD), pb[:, src].rearrange("p t (c s) -> p t c s", s=HD),
                              end, ALU.mult)
        dve.tensor_tensor(pb[:, RT], wr[:, :, J], e_in[:, :, :], ALU.mult).then_inc(dve_pe, 1)

        def bank(b):
            return ps[:, b, :].rearrange("p (h c) -> p h c", c=P)

        def masked(dst, b, mask):
            return dve.tensor_tensor(dst[:, :, :].rearrange("p (e t) c -> p e t c", e=2),
                                     ps[:, b:b + 2, 0:2 * P].rearrange("p e (t c) -> p e t c", c=P),
                                     cst(mask).unsqueeze(1).unsqueeze(1).to_broadcast([P, 2, 2, P]), ALU.mult)

        def level_of(n):
            return wide(cst("level", P * n, P * n + P))

        dve.wait_ge(*take(pe_dve, "dve"))
        link(masked(m_q, 0, "strict"))
        link(dve.tensor_tensor(m_qm[:, :, :], m_q[:, :, :], level_of(0), ALU.mult))
        dve.tensor_tensor(m_r[:, :, :], m_qm[:, :, :], wide(ident), ALU.add).then_inc(dve_pe, 1)
        dve.wait_ge(*take(pe_dve, "dve"))
        masked(m_ak, 2, "strict").then_inc(dve_pe, 1)
        fill(0)
        dve.wait_ge(*take(pe_dve, "dve"))
        masked(m_rb, 0, "incl").then_inc(dve_pe, 1)
        dve.wait_ge(*take(pe_dve, "dve"))
        masked(m_rk, 2, "incl").then_inc(dve_pe, 1)
        fill(1)
        dve.wait_ge(*take(pe_dve, "dve"))
        dve.tensor_tensor(m_t[:, :, :], bank(2), wide(ident), ALU.add)
        dve.tensor_tensor(m_qm[:, :, :], m_q[:, :, :], level_of(1), ALU.mult).then_inc(dve_pe, 1)
        fill(2)
        for level in range(1, 6):
            dve.wait_ge(*take(pe_dve, "dve"))
            dve.tensor_copy(m_y[:, :, :], bank(2)).then_inc(dve_pe, 1)
            if level < 5:
                dve.tensor_tensor(m_qm[:, :, :], m_q[:, :, :], level_of(level + 1), ALU.mult)
            if level < 4:
                fill(1 + 2 * level)
            dve.wait_ge(*take(pe_dve, "dve"))
            if level < 5:
                dve.tensor_tensor(m_t[:, :, :], m_t[:, :, :], bank(0), ALU.add)
            dve.tensor_tensor(m_r[:, :, :], m_r[:, :, :], bank(1), ALU.add).then_inc(dve_pe, 1)
            if level < 4:
                fill(2 + 2 * level)
            elif level == 4:
                fill(9)
        for n in range(2):
            r = ROW[n]
            dve.wait_ge(*take(pe_dve, "dve"))
            dve.tensor_tensor(u_rw[r, :], u_rw[r, :], ps[r, 2, 0:2 * P], ALU.add).then_inc(dve_pe, 1)
            fill(10 + n)
            dve.wait_ge(*take(pe_dve, "dve"))
            added = m_y[:, 0:2, :]
            link(dve.tensor_tensor(added, ps[:, 0, 0:2 * P].rearrange("p (t c) -> p t c", c=P),
                                   heads1.unsqueeze(1).to_broadcast([P, 2, P]), ALU.mult))
            for t in range(2):
                ins = dve.scalar_tensor_tensor(state[1 - n][:, t, :], state[n][:, t, :], e_in[:, t, HD * n + HD - 1:HD * n + HD],
                                               added[:, t, :], ALU.mult, ALU.add)
            ins.then_inc(dve_pe, 1)

    def merge_sp(l):
        w = layer_of("w_in_2", l)
        for m in range(4):
            load_rows(layer_of("w_branch_2", l, m), m % 2, 2, D)
            with loop(sp, "sp", 2) as i:
                for c in range(2):
                    load_cols(w, i * 512 + (IN_GATE + D * m + 256 * c), (m + 1 + c) % 2)

    def merge_pe():
        pe.wait_ge(*take(xlo_ready, "pe", 6))
        hm = moving(h_hi, h_lo)
        for m in range(4):
            pe_tiles(moving(br_hi[m], br_lo[m]), 2, D, m % 2, (4, 5, 6, 7) * 2, free=copied)
            if m == 0:
                pe.wait_ge(*take(xlo_ready, "pe", DT))
            with loop(pe, "pe", 2):
                for c in range(2):
                    pe_tiles(hm, DT, 256, (m + 1 + c) % 2, (2 * c, 2 * c + 1), free=gate_out)
        pe.wait_ge(*take(xlo_ready, "pe", DT))

    def merge_act():
        for m in range(4):
            split_hi((m + 1) % 2)
            if m == 0:
                for t in range(DT):
                    act.activation(h_hi[:, t, :], x[:, t, :], ACT.Identity, scale=par_of(MIX_PRE, t)).then_inc(xhi_ready, 1)
            if m == 1:
                act.dma_start(mem_n[:, :, :], scratch["mem"]).then_inc(mem_landed, 16)
            for t in range(DT):
                act.wait_ge(*take(tile_done, "act"))
                act.wait_ge(*take(p2_used, "act"))
                act.activation(y_f[:, t, :], ps[:, 4 + t % 4, :], ACT.Copy).then_inc(copied, 1)
            with loop(act, "act", 2):
                for c in range(2):
                    split_hi((m + c) % 2)
                    for t in range(2 * c, 2 * c + 2):
                        act.wait_ge(*take(gate_out, "act"))
                        act.activation(tmp[:, t, :], tmp[:, t, :], ACT.Sigmoid).then_inc(act_ready, 1)
            skip(tile_done, "act", DT)
        act.wait_ge(*take(prod_ready, "act", DT))
        for t in range(DT):
            act.activation(h_hi[:, t, :], merged[:, t, :], ACT.Copy).then_inc(xhi_ready, 1)
        act.wait_ge(*take(mem_landed, "act", 16))
        for t in range(DT):
            act.activation(mn_hi[:, t, :], mem_n[:, t, :], ACT.Identity, scale=par_of(LN_MEM, t)).then_inc(xhi_ready, 1)

    def merge_dve():
        for t in range(DT):
            dve.wait_ge(*take(xhi_ready, "dve"))
            dve.scalar_tensor_tensor(h_lo[:, t, :], x[:, t, :], par_of(MIX_PRE, t), h_hi[:, t, :].bitcast(F32),
                                     ALU.mult, ALU.subtract).then_inc(xlo_ready, 1)
        for m in range(4):
            skip(tile_done, "dve", DT)
            with loop(dve, "dve", 2) as i:
                for n in range(5):
                    if n < 4:
                        dve.wait_ge(*take(tile_done, "dve"))
                        dve.tensor_tensor(tmp[:, n, :], ps[:, n, :], rstd[:, :], ALU.mult).then_inc(gate_out, 1)
                    if n:
                        t = bass.ds(i * 4 + (n - 1), 1)
                        s = tmp[:, n - 1:n, :]
                        dve.wait_ge(*take(act_ready, "dve"))
                        dve.wait_ge(*take(copied, "dve"))
                        dst = merged[:, t, :] if m == 0 else s
                        dve.tensor_tensor(dst, s, y_f[:, t, :], ALU.mult).then_inc(p2_used, 1)
                        dve.wait_ge(*take(p2_used, "dve"))
                        if m:
                            ins = dve.tensor_tensor(merged[:, t, :], merged[:, t, :], s, ALU.add)
                            ins.then_inc((prod_ready if m == 3 else dve_step), 1)
                            if m < 3:
                                dve.wait_ge(*take(dve_step, "dve"))
        for t in range(DT):
            dve.wait_ge(*take(xhi_ready, "dve"))
            dve.tensor_tensor(h_lo[:, t, :], merged[:, t, :], h_hi[:, t, :].bitcast(F32), ALU.subtract)\
                .then_inc(xlo_ready, 1)
        for t in range(DT):
            dve.wait_ge(*take(xhi_ready, "dve"))
            dve.scalar_tensor_tensor(mn_lo[:, t, :], mem_n[:, t, :], par_of(LN_MEM, t), mn_hi[:, t, :].bitcast(F32),
                                     ALU.mult, ALU.subtract).then_inc(xlo_ready, 1)

    def out_sp(name, l):
        with loop(sp, "sp", 2) as i:
            for c in range(2):
                load_cols(layer_of(name, l), i * 512 + 256 * c, c)

    def out_pe():
        hm = moving(h_hi, h_lo)
        with loop(pe, "pe", 2):
            for c in range(2):
                pe_tiles(hm, DT, 256, c, (2 * c, 2 * c + 1), free=y_ready)
        sums_pe()
        skip(x_ready, "pe", DT)

    def out_act():
        with loop(act, "act", 2) as i:
            for c in range(2):
                split_hi(1 - c)
                squares_act(i, (2 * c, 2 * c + 1), sq2)
        skip(tile_done, "act", DT)
        factor_act()

    def squares_act(i, tiles, dst):
        for t in tiles:
            act.wait_ge(*take(y_ready, "act"))
            act.activation(dst[:, bass.ds(i * 4 + t, 1), :], y_f[:, bass.ds(i * 4 + t, 1), :], ACT.Square).then_inc(sq_ready, 1)

    def out_dve():
        clear_sum_dve()
        with loop(dve, "dve", 2) as i:
            for c in range(4):
                t = bass.ds(i * 4 + c, 1)
                dve.wait_ge(*take(tile_done, "dve"))
                dve.tensor_copy(y_f[:, t, :], ps[:, c:c + 1, :]).then_inc(y_ready, 1)
                add_square_dve(sq2, t)
        settle(dve)
        dve.sem_inc(acc_ready, 1)

    def post_norm_dve(gain, chained=True, between=None):
        factor_dve()
        clear_sum_dve()
        for t in range(DT + 1):
            if t < DT:
                link(dve.scalar_tensor_tensor(y_f[:, t, :], y_f[:, t, :], par_of(gain, t), rstd[:, :], ALU.mult, ALU.mult))
                dve.tensor_tensor(x[:, t, :], x[:, t, :], y_f[:, t, :], ALU.add).then_inc(x_ready, 1)
                if between:
                    between(t)
            if t and chained:
                add_square_dve(sq, slice(t - 1, t))
        if chained:
            dve.sem_inc(acc_ready, 1)

    def memory_sp(l):
        w = layer_of("xa_wkv_2", l)
        with loop(sp, "sp", 4) as i:
            for c in range(2):
                load_cols(w, i * 512 + 256 * c, c)

    def memory_pe():
        pe.wait_ge(*take(xlo_ready, "pe", DT))
        mm = moving(mn_hi, mn_lo)
        with loop(pe, "pe", 2):
            for c in range(2):
                pe_tiles(mm, DT, 256, c, (2 * c, 2 * c + 1), n=MEM)
        with loop(pe, "pe", 2):
            for c in range(2):
                pe.wait_ge(*take(w_split, "pe"))
                for q in range(2):
                    pe.wait_ge(*take(v_out, "pe"))
                    value_product(ps[:, 4 + 2 * c + q, 0:256], parts_of(c, DT, 256), mm, slice(P * q, P * q + P), begin=q == 0)\
                        .then_inc(tile_done, 1)
        pe.wait_ge(*ahead(v_out, "pe", 4))

    def memory_act():
        for c in range(4):
            split_hi(1 - c % 2)
            norm_tile_act(XA_PRE, 2 * c)
            norm_tile_act(XA_PRE, 2 * c + 1)
        skip(tile_done, "act", DT)
        with loop(act, "act", 2) as i:
            for c in range(2):
                split_hi(1 - c)
                for q in range(2):
                    act.wait_ge(*take(tile_done, "act"))
                    act.activation(v_xa[:, q:q + 1, bass.ds(i * 512 + 256 * c, 256)], ps[:, 4 + 2 * c + q:5 + 2 * c + q, 0:256], ACT.Copy)\
                        .then_inc(v_out, 1)

    def memory_dve():
        def key_tile(t):
            dve.wait_ge(*take(tile_done, "dve"))
            dve.tensor_copy(k_xa[:, t, :], ps[:, t % 4, 0:MEM]).then_inc(bank_free, 1)

        post_norm_dve(MIX_POST, between=key_tile)
        skip(tile_done, "dve", DT)

    def cross_pe():
        norm_pe()
        hm = moving(h_hi, h_lo)
        with loop(pe, "pe", 2):
            for c in range(2):
                pe_tiles(hm, DT, 256, c, (2 * c, 2 * c + 1))
        end_stage("pe")
        units_pe(cross_units(), smx, ptx)
        pe.wait_ge(*take(o_taken, "pe", 2))

    def cross_units():
        units = []
        for h in range(4):
            for q in range(TT):
                u = len(units)
                units.append(dict(q=[q_xa[:, 2 * h + a, P * q:P * q + P] for a in range(2)], k=[k_xa[:, 2 * h + a, :] for a in range(2)],
                                  n=MEM, bias=None, scale=1.0 / 16, gate=None, max=col[:, u:u + 1], sum=col[:, 32 + u:33 + u],
                                  inv=col[:, 64 + u % 2:65 + u % 2],
                                  v=[lambda j, at=256 * h + P * a: v_xa[:, j, at:at + P] for a in range(2)],
                                  o=[ps[:, 4 + 2 * (h % 2) + a, P * q:P * q + P] for a in range(2)], first=True, last=True,
                                  begin=h >= 2 and q == 0, end=h if q == TT - 1 else None))
        return units

    def cross_act():
        factor_act()
        for c in range(4):
            split_hi(1 - c % 2)
        skip(tile_done, "act", DT)
        end_stage("act")

        def leave(h):
            b = 4 + 2 * (h % 2)
            act.activation(h_hi[:, 2 * h:2 * h + 2, :], ps[:, b:b + 2, :], ACT.Copy).then_inc(xhi_ready, 1)

        units_act(cross_units(), smx, ptx, leave)

    def cross_dve():
        norm_dve(XA_PRE)
        with loop(dve, "dve", 2) as i:
            for t in range(4):
                dve.wait_ge(*take(tile_done, "dve"))
                dve.tensor_tensor(q_xa[:, bass.ds(i * 4 + t, 1), :], ps[:, t:t + 1, :], rstd[:, :].unsqueeze(1), ALU.mult)\
                    .then_inc(bank_free, 1)
        end_stage("dve")

        def leave(h):
            b = 4 + 2 * (h % 2)
            dve.wait_ge(*take(xhi_ready, "dve"))
            dve.tensor_tensor(h_lo[:, 2 * h:2 * h + 2, :], ps[:, b:b + 2, :], h_hi[:, 2 * h:2 * h + 2, :].bitcast(F32),
                              ALU.subtract).then_inc(o_taken, 1)

        units_dve(cross_units(), smx, leave)

    def mlp_sp(l):
        w1, w2 = layer_of("mlp_w1_2", l), layer_of("mlp_w2_2", l)
        for half in range(2):
            with loop(sp, "sp", 4) as i:
                for c in range(2):
                    load_cols(w1, i * 512 + (2048 * half + 256 * c), c)
            with loop(sp, "sp", 4) as i:
                for c in range(2):
                    load_rows(w2[2048 * half:2048 * half + 2048, bass.ds(i * 256 + P * c, P)], c, 16, P)

    def mlp_pe():
        norm_pe()
        hm, dm = moving(h_hi, h_lo), moving(hid_hi, hid_lo)
        for half in range(2):
            with loop(pe, "pe", 4):
                for c in range(2):
                    pe_tiles(hm, DT, 256, c, (2 * c, 2 * c + 1), free=relu_out)
            pe.wait_ge(*take(hid_ready, "pe", 16))
            with loop(pe, "pe", 2):
                for c in range(4):
                    pe_tiles(dm, 16, P, c % 2, (c if half else 4 + c,), free=y_ready if half else bank_free)
        sums_pe()
        skip(x_ready, "pe", DT)

    def mlp_act():
        norm_act(MLP_PRE)
        for half in range(2):
            with loop(act, "act", 4) as i:
                for c in range(2):
                    split_hi(1 - c)
                    for t in range(2 * c, 2 * c + 2):
                        act.wait_ge(*take(prod_ready, "act"))
                        act.activation(hid_hi[:, bass.ds(i * 4 + t, 1), :], tmp[:, t:t + 1, :], ACT.Copy).then_inc(hid_hi_ready, 1)
            if half == 0:
                for c in range(DT):
                    split_hi(1 - c % 2)
            skip(tile_done, "act", 16)
            if half == 0:
                act.wait_ge(*take(tile_done, "act", DT))
        skip(tile_done, "act", DT)
        for c in range(DT):
            if c < DT - 1:
                split_hi(1 - c % 2)
            squares_act(0, (c,), sq_h)
        factor_act()

    def mlp_dve():
        norm_dve(MLP_PRE)
        for half in range(2):
            with loop(dve, "dve", 4) as i:
                for t in range(4):
                    h = tmp[:, t, :]
                    dve.wait_ge(*take(tile_done, "dve"))
                    dve.scalar_tensor_tensor(h, ps[:, t, :], 0.0, rstd[:, :], ALU.max, ALU.mult).then_inc(relu_out, 1)
                    dve.wait_ge(*take(relu_out, "dve"))
                    dve.tensor_tensor(h, h, h, ALU.mult).then_inc(prod_ready, 1)
                    dve.wait_ge(*take(hid_hi_ready, "dve"))
                    hid = bass.ds(i * 4 + t, 1)
                    dve.tensor_tensor(hid_lo[:, hid, :], tmp[:, t:t + 1, :], hid_hi[:, hid, :].bitcast(F32), ALU.subtract)\
                        .then_inc(hid_ready, 1)
                    dve.wait_ge(*take(hid_ready, "dve"))
            if half:
                clear_sum_dve()
            with loop(dve, "dve", 2) as i:
                for c in range(4):
                    t = bass.ds(i * 4 + c, 1)
                    y = y_f[:, t, :]
                    dve.wait_ge(*take(tile_done, "dve"))
                    if half == 0:
                        dve.tensor_copy(y, ps[:, 4 + c:5 + c, :]).then_inc(bank_free, 1)
                    else:
                        dve.tensor_tensor(y, y, ps[:, c:c + 1, :], ALU.add).then_inc(y_ready, 1)
                        add_square_dve(sq_h, t)
        settle(dve)
        dve.sem_inc(acc_ready, 1)
        post_norm_dve(MLP_POST, chained=False)

    def result_sp():
        sp.wait_ge(*take(out_ready, "sp", DT))
        sp.dma_start(out[0].rearrange("(t p) d -> p t d", p=P), out_rows[:, :, :]).then_inc(stored, 16)
        sp.wait_ge(*take(stored, "sp", 16))

    def result_pe():
        pe.wait_ge(*ahead(x_ready, "pe", 4))
        for t in range(DT):
            for q in range(TT):
                ins = pe.transpose(ps[:, t, P * q:P * q + P], x[:, t, P * q:P * q + P], ident)
            ins.then_inc(turned, 1)

    def result_dve():
        for t in range(DT):
            dve.wait_ge(*take(turned, "dve"))
            dve.tensor_copy(out_rows[:, :, P * t:P * t + P], ps[:, t, :].rearrange("p (q c) -> p q c", c=P))\
                .then_inc(out_ready, 1)


    with ExitStack() as ctx:
        block = ctx.enter_context(nc.Block())

        @block.sync
        def _(_eng):
            start_sp()
            pool_sp()
            ffn_sp(0)
            qkv_sp()
            pattern_sp()
            ffn_sp(1)
            setup_sp()
            with loop(sp, "sp", LAYERS) as l:
                params_sp(l)
                mixer_in_sp(l)
                merge_sp(l)
                out_sp("w_mix_out_2", l)
                memory_sp(l)
                out_sp("xa_wq_2", l)
                out_sp("xa_wo_2", l)
                mlp_sp(l)
            result_sp()

        @block.gpsimd
        def _(_eng):
            pool.memset(rows[:, :], 0.0).then_inc(rows_zero, 1)
            split_lo(0)
            split_lo(1)
            with loop(pool, "pool", (CHUNKS_1 + LAYERS * CHUNKS_2) // 2 - 1):
                split_lo(0)
                split_lo(1)

        @block.tensor
        def _(_eng):
            for s, n in ((bank_free, 4), (x_ready, 4), (gate_scaled, 2), (up_scaled, 2), (s_taken, 2), (rot_taken, 4), (copied, 4),
                         (p2_used, 8), (gate_out, 4), (y_ready, 4), (relu_out, 4), (v_out, 4)):
                pe.sem_inc(s, n)
            start_pe()
            pool_pe()
            ffn_pe()
            qkv_pe()
            pattern_pe()
            ffn_pe()
            final_pe()
            skip(x_ready, "pe", DT)
            setup_pe()
            with loop(pe, "pe", LAYERS):
                params_pe()
                mixer_in_pe()
                end_stage("pe")
                retention_pe()
                nsa_pe()
                rwkv_pe()
                merge_pe()
                out_pe()
                memory_pe()
                cross_pe()
                out_pe()
                mlp_pe()
            result_pe()

        @block.scalar
        def _(_eng):
            start_act()
            pool_act()
            ffn_act(B1["norm_mix"] + DT)
            qkv_act()
            pattern_act()
            ffn_act(None, last=True)
            end_stage("act")
            setup_act()
            with loop(act, "act", LAYERS) as l:
                mixer_in_act(l)
                conv_act()
                retention_act(l)
                nsa_act()
                rwkv_act()
                merge_act()
                out_act()
                memory_act()
                cross_act()
                out_act()
                mlp_act()

        @block.vector
        def _(_eng):
            start_dve()
            pool_dve()
            ffn_dve(B1["norm_ffn"])
            qkv_dve()
            pattern_dve()
            ffn_dve(B1["norm_ffn"] + DT)
            final_dve()
            setup_dve()
            with loop(dve, "dve", LAYERS):
                params_dve()
                mixer_in_dve()
                conv_dve()
                retention_dve()
                nsa_dve()
                rwkv_dve()
                merge_dve()
                out_dve()
                memory_dve()
                cross_dve()
                out_dve()
                post_norm_dve(XA_POST)
                mlp_dve()
            result_dve()


CHUNKS_1 = 4 + 2 + 4 + 2 * (22 + 16) + 12 + 4
CHUNKS_2 = 14 + 4 * (1 + 4) + 4 + 8 + 4 + 4 + 2 * (8 + 8)


def kernel(**inputs):
    import concourse.bacc as bacc
    from concourse.bass_utils import run_bass_kernel_spmd

    arrays = {name: np.ascontiguousarray(a) for name, a in inputs.items()}
    arrays.update(const=constant_table(), masks=pattern_masks(), onehot=bucket_of_distance())
    rises = {}
    for _ in range(2):
        nc = bacc.Bacc("TRN2", target_bir_lowering=False, num_devices=1, dynamic_dma_scratch_size=1024)
        A = {name: nc.dram_tensor(name, a.shape, F32, kind="ExternalInput").ap() for name, a in arrays.items()}
        out = nc.dram_tensor("out", (1, S, D), F32, kind="ExternalOutput").ap()
        scratch = {"vec": nc.dram_tensor("vec_store", (4, N_DIST), F32, kind="Internal").ap(),
                   "mem": nc.dram_tensor("mem_store", (P, DT, MEM), F32, kind="Internal").ap()}
        build(nc, A, out, scratch, rises)
    r = run_bass_kernel_spmd(nc, [arrays], core_ids=[0])
    return r.results[0]["out"]
```
